# Optimizing a Trainium2 kernel written in Bass

```python
import jax, jax.numpy as jnp
from jax import lax
import numpy as np

D_MODEL = 1024
BATCH = 1
SEQ = 256
DEPTH = 2

CTX_LEN = 256
GRID_W = 64
EPS = 1e-6
GLA_HEADS = 4
GLA_DK = 128
GLA_DV = 256
GLA_LR = 16
GLA_TAU = 16.0
GLA_CHUNK = 64
ROPE_BASE = 10000.0
NA_HEADS = 8
NA_HD = 64
WIN_R = 8
WIN_C = 16
N_EXPERTS = 16
N_GROUPS = 4
EXPERTS_PER_GROUP = N_EXPERTS // N_GROUPS
TOP_K = 2
D_FF_EXPERT = 1024
MOE_BLOCK = 128

GLA_QK = GLA_HEADS * GLA_DK
GLA_V = GLA_HEADS * GLA_DV
NA_W = NA_HEADS * NA_HD
IN_SIZES = (GLA_QK, GLA_QK, GLA_V, GLA_V, 2 * GLA_LR, NA_W, NA_W, NA_W, D_MODEL, D_MODEL)
IN_COLS = sum(IN_SIZES)

kernel_name = 'hybrid_gla_natten_moe_prefix_dit'

def rmsnorm(x, w):
    xf = x.astype(jnp.float32)
    y = xf * lax.rsqrt(jnp.mean(xf * xf, axis=-1, keepdims=True) + EPS)
    return (y * w.astype(jnp.float32)).astype(x.dtype)

def heads(t, n, d):
    B, L, _ = t.shape
    return t.reshape(B, L, n, d).transpose(0, 2, 1, 3)

def axial_rope(t, rows, cols):
    half = t.shape[-1] // 2
    inv = ROPE_BASE ** (-jnp.arange(0, half, 2, dtype=jnp.float32) / half)

    def rot(u, pos):
        ang = pos.astype(jnp.float32)[:, None] * inv[None, :]
        cos, sin = jnp.cos(ang), jnp.sin(ang)
        u1, u2 = jnp.split(u, 2, axis=-1)
        return jnp.concatenate([u1 * cos - u2 * sin, u1 * sin + u2 * cos], axis=-1)

    return jnp.concatenate([rot(t[..., :half], rows), rot(t[..., half:], cols)], axis=-1)

def gla_chunk_scan(q, k, v, logg, s0, need_out):
    B, H, L, _ = q.shape
    dv = v.shape[-1]
    n = L // GLA_CHUNK

    def chunks(t):
        return jnp.moveaxis(t.reshape(B, H, n, GLA_CHUNK, t.shape[-1]), 2, 0)

    lower = jnp.tril(jnp.ones((GLA_CHUNK, GLA_CHUNK), dtype=bool))

    def step(S, inp):
        qc, kc, vc, gc = inp
        b = jnp.cumsum(gc, axis=2)
        b_end = b[:, :, -1:, :]
        k_dec = kc * jnp.exp(b_end - b)
        S_new = S * jnp.exp(b_end[:, :, 0, :, None]) + jnp.einsum('bhsd,bhse->bhde', k_dec, vc)
        if not need_out:
            return S_new, None
        inter = jnp.einsum('bhtd,bhde->bhte', qc * jnp.exp(b), S)
        att = jnp.einsum('bhtd,bhsd->bhts', qc * jnp.exp(b - b_end), k_dec)
        att = jnp.where(lower, att, 0.0)
        o = inter + jnp.einsum('bhts,bhse->bhte', att, vc)
        return S_new, o

    S, o = lax.scan(step, s0, (chunks(q), chunks(k), chunks(v), chunks(logg)))
    if need_out:
        o = jnp.moveaxis(o, 0, 2).reshape(B, H, L, dv)
    return S, o

def gla_branch(xp, cp, w_gk_up, b_gk, norm_w, ctx_out):
    f32 = jnp.float32

    def prep(parts, grid):
        q, k, v, _, lr = parts
        q = heads(q, GLA_HEADS, GLA_DK).astype(f32)
        k = heads(k, GLA_HEADS, GLA_DK).astype(f32)
        if grid:
            t = jnp.arange(q.shape[2])
            q = axial_rope(q, t // GRID_W, t % GRID_W)
            k = axial_rope(k, t // GRID_W, t % GRID_W)
        q = q * (GLA_DK ** -0.5)
        v = heads(v, GLA_HEADS, GLA_DV).astype(f32)
        gates = []
        for d in range(2):
            z = lr[..., d * GLA_LR:(d + 1) * GLA_LR].astype(f32) @ w_gk_up[d].astype(f32) + b_gk[d].astype(f32)
            gates.append(heads(jax.nn.log_sigmoid(z) / GLA_TAU, GLA_HEADS, GLA_DK))
        return q, k, v, gates

    qx, kx, vx, (gxf, gxb) = prep(xp, True)
    qc, kc, vc, (gcf, gcb) = prep(cp, False)
    B = qx.shape[0]
    s0 = jnp.zeros((B, GLA_HEADS, GLA_DK, GLA_DV), f32)

    def flip(t):
        return jnp.flip(t, axis=2)

    s_cf, oc_f = gla_chunk_scan(qc, kc, vc, gcf, s0, ctx_out)
    s_cb, oc_b = gla_chunk_scan(flip(qc), flip(kc), flip(vc), flip(gcb), s0, ctx_out)
    _, ox_f = gla_chunk_scan(qx, kx, vx, gxf, s_cf, True)
    _, ox_b = gla_chunk_scan(flip(qx), flip(kx), flip(vx), flip(gxb), s_cb, True)

    def finish(o, g):
        o = o * lax.rsqrt(jnp.mean(o * o, axis=-1, keepdims=True) + EPS) * norm_w.astype(f32)
        Bo, H, L, dv = o.shape
        o = o.transpose(0, 2, 1, 3).reshape(Bo, L, H * dv)
        return (o * jax.nn.silu(g.astype(f32))).astype(g.dtype)

    yx = finish(ox_f + flip(ox_b), xp[3])
    yc = finish(oc_f + flip(oc_b), cp[3]) if ctx_out else None
    return yx, yc

def na_branch(xp, cp, rpb, ctx_out):
    f32 = jnp.float32
    q, k, v = xp
    B, L, _ = q.shape
    rows = L // GRID_W
    kr = min(WIN_R, rows)
    scale = NA_HD ** -0.5
    qg = (q * scale).reshape(B, rows, GRID_W, NA_HEADS, NA_HD)
    kg = k.reshape(B, rows, GRID_W, NA_HEADS, NA_HD)
    vg = v.reshape(B, rows, GRID_W, NA_HEADS, NA_HD)
    qc, kc, vc = [t.reshape(B, -1, NA_HEADS, NA_HD) for t in cp]

    col = jnp.arange(GRID_W)
    c0 = jnp.clip(col - WIN_C // 2, 0, GRID_W - WIN_C)
    col_mask = (col[None, :] >= c0[:, None]) & (col[None, :] < c0[:, None] + WIN_C)
    col_idx = jnp.clip(col[None, :] - col[:, None], -(WIN_C - 1), WIN_C - 1) + (WIN_C - 1)
    rpb32 = rpb.astype(f32)
    n_loc = kr * GRID_W

    def row_block(r):
        r0 = jnp.clip(r - kr // 2, 0, rows - kr)
        q_r = lax.dynamic_index_in_dim(qg, r, axis=1, keepdims=False)
        k_b = lax.dynamic_slice_in_dim(kg, r0, kr, axis=1)
        v_b = lax.dynamic_slice_in_dim(vg, r0, kr, axis=1)
        row_idx = r0 + jnp.arange(kr) - r + (WIN_R - 1)
        bias = rpb32[:, row_idx][:, :, col_idx].transpose(0, 2, 1, 3)
        s_loc = jnp.einsum('bqhd,bikhd->bhqik', q_r, k_b).astype(f32) + bias[None]
        s_loc = jnp.where(col_mask[:, None, :], s_loc, -jnp.inf).reshape(B, NA_HEADS, GRID_W, n_loc)
        s_ctx = jnp.einsum('bqhd,bchd->bhqc', q_r, kc).astype(f32)
        p = jax.nn.softmax(jnp.concatenate([s_loc, s_ctx], axis=-1), axis=-1).astype(v.dtype)
        o = jnp.einsum('bhqk,bkhd->bqhd', p[..., :n_loc], v_b.reshape(B, n_loc, NA_HEADS, NA_HD))
        o = o + jnp.einsum('bhqc,bchd->bqhd', p[..., n_loc:], vc)
        return o

    o = lax.map(row_block, jnp.arange(rows))
    yx = o.transpose(1, 0, 2, 3, 4).reshape(B, L, NA_W)
    yc = None
    if ctx_out:
        s = jnp.einsum('bqhd,bkhd->bhqk', qc * scale, kc).astype(f32)
        p = jax.nn.softmax(s, axis=-1).astype(vc.dtype)
        yc = jnp.einsum('bhqk,bkhd->bqhd', p, vc).reshape(B, -1, NA_W)
    return yx, yc

def hybrid_mixer(hx, hc, w_in, w_gk_up, b_gk, gla_norm_w, rpb, w_bo_gla, w_bo_na, w_out, ctx_out):
    idx = np.cumsum(IN_SIZES)[:-1].tolist()
    xp = jnp.split(hx @ w_in, idx, axis=-1)
    cp = jnp.split(hc @ w_in, idx, axis=-1)
    gla_x, gla_c = gla_branch(xp[:5], cp[:5], w_gk_up, b_gk, gla_norm_w, ctx_out)
    na_x, na_c = na_branch(xp[5:8], cp[5:8], rpb, ctx_out)

    def merge(gla_o, na_o, gates):
        m = jax.nn.sigmoid(gates[0]) * (gla_o @ w_bo_gla) + jax.nn.sigmoid(gates[1]) * (na_o @ w_bo_na)
        return m @ w_out

    yx = merge(gla_x, na_x, xp[8:])
    yc = merge(gla_c, na_c, cp[8:]) if ctx_out else None
    return yx, yc

def moe_ffn(h, w_router, b_router, w1, w3, w2):
    N, D = h.shape
    aff = jax.nn.sigmoid(h.astype(jnp.float32) @ w_router.astype(jnp.float32))
    sel = aff + b_router.astype(jnp.float32)
    gscore = lax.top_k(sel.reshape(N, N_GROUPS, EXPERTS_PER_GROUP), 2)[0].sum(-1)
    gbest = jnp.argmax(gscore, axis=-1)
    in_grp = (jnp.arange(N_EXPERTS) // EXPERTS_PER_GROUP)[None, :] == gbest[:, None]
    _, top_idx = lax.top_k(jnp.where(in_grp, sel, -jnp.inf), TOP_K)
    top_w = jnp.take_along_axis(aff, top_idx, axis=1)
    top_w = top_w / jnp.sum(top_w, axis=-1, keepdims=True)

    flat_e = top_idx.reshape(-1)
    flat_tok = jnp.repeat(jnp.arange(N, dtype=jnp.int32), TOP_K)
    flat_w = top_w.reshape(-1)
    order = jnp.argsort(flat_e)
    se, stok, sw = flat_e[order], flat_tok[order], flat_w[order]
    counts = jnp.bincount(flat_e, length=N_EXPERTS)
    starts = jnp.cumsum(counts) - counts
    padded = (counts + MOE_BLOCK - 1) // MOE_BLOCK * MOE_BLOCK
    pends = jnp.cumsum(padded)
    pstarts = pends - padded
    dest = pstarts[se] + (jnp.arange(N * TOP_K) - starts[se])
    n_blocks = (N * TOP_K + N_EXPERTS * (MOE_BLOCK - 1) + MOE_BLOCK - 1) // MOE_BLOCK
    P = n_blocks * MOE_BLOCK
    buf_tok = jnp.full((P,), N, dtype=jnp.int32).at[dest].set(stok)
    buf_w = jnp.zeros((P,), jnp.float32).at[dest].set(sw)
    blk_expert = jnp.minimum(jnp.searchsorted(pends, jnp.arange(n_blocks) * MOE_BLOCK, side='right'), N_EXPERTS - 1)
    h_pad = jnp.concatenate([h, jnp.zeros((1, D), h.dtype)], axis=0)

    def run_block(args):
        tok, e = args
        xb = h_pad[tok]
        return (jax.nn.silu(xb @ w1[e]) * (xb @ w3[e])) @ w2[e]

    y = lax.map(run_block, (buf_tok.reshape(n_blocks, MOE_BLOCK), blk_expert)).reshape(P, D)
    y = y * buf_w[:, None].astype(y.dtype)
    return jnp.zeros((N + 1, D), y.dtype).at[buf_tok].add(y)[:N]

def setup_inputs(seed: int = 0) -> dict:
    key = jax.random.key(seed)
    ks = jax.random.split(key, 24)
    D = D_MODEL

    def nrm(k, shape, s):
        return jax.random.normal(k, shape, jnp.float32) * s

    return {
        'x': nrm(ks[0], (BATCH, SEQ, D), 1.0),
        'c': nrm(ks[1], (BATCH, D), 1.0),
        'ctx': nrm(ks[2], (BATCH, CTX_LEN, D), 1.0),
        'c_ctx': nrm(ks[3], (D,), 1.0),
        'w_ada': nrm(ks[4], (DEPTH, D, 6 * D), 0.5 * D ** -0.5),
        'b_ada': nrm(ks[5], (DEPTH, 6 * D), 0.01),
        'norm1_w': 1.0 + nrm(ks[6], (DEPTH, D), 0.05),
        'norm2_w': 1.0 + nrm(ks[7], (DEPTH, D), 0.05),
        'w_in': nrm(ks[8], (DEPTH, D, IN_COLS), D ** -0.5),
        'w_gk_up': nrm(ks[9], (DEPTH, 2, GLA_LR, GLA_QK), GLA_LR ** -0.5),
        'b_gk': nrm(ks[10], (DEPTH, 2, GLA_QK), 0.1),
        'gla_norm_w': 1.0 + nrm(ks[11], (DEPTH, GLA_DV), 0.05),
        'rpb': nrm(ks[12], (DEPTH, NA_HEADS, 2 * WIN_R - 1, 2 * WIN_C - 1), 0.1),
        'w_bo_gla': nrm(ks[13], (DEPTH, GLA_V, D), GLA_V ** -0.5),
        'w_bo_na': nrm(ks[14], (DEPTH, NA_W, D), NA_W ** -0.5),
        'w_out': nrm(ks[15], (DEPTH, D, D), D ** -0.5),
        'w_router': nrm(ks[16], (D, N_EXPERTS), D ** -0.5),
        'b_router': nrm(ks[17], (N_EXPERTS,), 0.01),
        'w1': nrm(ks[18], (DEPTH, N_EXPERTS, D, D_FF_EXPERT), D ** -0.5),
        'w3': nrm(ks[19], (DEPTH, N_EXPERTS, D, D_FF_EXPERT), D ** -0.5),
        'w2': nrm(ks[20], (DEPTH, N_EXPERTS, D_FF_EXPERT, D), D_FF_EXPERT ** -0.5),
        'final_norm_w': 1.0 + nrm(ks[21], (D,), 0.05),
    }

def reference(x, c, ctx, c_ctx, w_ada, b_ada, norm1_w, norm2_w, w_in, w_gk_up, b_gk, gla_norm_w, rpb,
              w_bo_gla, w_bo_na, w_out, w_router, b_router, w1, w3, w2, final_norm_w):
    B, L, D = x.shape
    Lc = ctx.shape[1]
    for l in range(DEPTH):
        ctx_out = l < DEPTH - 1
        mx = (jax.nn.silu(c) @ w_ada[l] + b_ada[l]).reshape(B, 6, 1, D)
        mc = (jax.nn.silu(c_ctx) @ w_ada[l] + b_ada[l]).reshape(6, D)
        hx = rmsnorm(x, norm1_w[l]) * (1.0 + mx[:, 1]) + mx[:, 0]
        hc = rmsnorm(ctx, norm1_w[l]) * (1.0 + mc[1]) + mc[0]
        yx, yc = hybrid_mixer(hx, hc, w_in[l], w_gk_up[l], b_gk[l], gla_norm_w[l], rpb[l],
                              w_bo_gla[l], w_bo_na[l], w_out[l], ctx_out)
        x = x + mx[:, 2] * yx
        hx = rmsnorm(x, norm2_w[l]) * (1.0 + mx[:, 4]) + mx[:, 3]
        if ctx_out:
            ctx = ctx + mc[2] * yc
            hc = rmsnorm(ctx, norm2_w[l]) * (1.0 + mc[4]) + mc[3]
            tokens = jnp.concatenate([hx.reshape(-1, D), hc.reshape(-1, D)], axis=0)
            y = moe_ffn(tokens, w_router, b_router, w1[l], w3[l], w2[l])
            x = x + mx[:, 5] * y[:B * L].reshape(B, L, D)
            ctx = ctx + mc[5] * y[B * L:].reshape(B, Lc, D)
        else:
            y = moe_ffn(hx.reshape(-1, D), w_router, b_router, w1[l], w3[l], w2[l])
            x = x + mx[:, 5] * y.reshape(B, L, D)
    return rmsnorm(x, final_norm_w)


_drawn_inputs = setup_inputs


def setup_inputs(seed=0):
    import zlib

    import numpy as np

    out = dict(_drawn_inputs(seed))
    spreads = {}
    factors = {'b_gk': 3.409, 'rpb': 17.163, 'gla_norm_w': 3.23}
    for name, (base, spread) in spreads.items():
        noise = np.random.default_rng([zlib.crc32(name.encode()), seed]).standard_normal(out[name].shape)
        drawn = base * np.exp(spread * noise) if base else spread * noise
        out[name] = __import__('jax').numpy.asarray(drawn.astype(out[name].dtype))
    for name, factor in factors.items():
        out[name] = (out[name] * factor).astype(out[name].dtype)
    return out
```

```python
from contextlib import ExitStack

import concourse.bass as bass
import numpy as np
from concourse import mybir

P = 128
D = 1024
KT = D // P
SEQ, CTX = 256, 256
TOK = SEQ + CTX
DEPTH = 2
GRID_W = 64
GROWS = SEQ // GRID_W
EPS = 1e-6
GH, DK, DV, LR = 4, 128, 256, 16
TAU = 16.0
CH = 64
NCH = TOK // CH
NH, HD = 8, 64
WIN_R, WIN_C = 8, 16
NE, NG, EPG = 16, 4, 4
FF = 1024
BLK = 64
MAXB = TOK * 2 // BLK + NE
XROWS = (MAXB + 2) * BLK
RPAD = 128
F32 = mybir.dt.float32
I32 = mybir.dt.int32
ALU = mybir.AluOpType
ACT = mybir.ActivationFunctionType
AX = mybir.AxisListType.X
BIG = 1e30

C_Q, C_K, C_V, C_G, C_LR = 0, 512, 1024, 2048, 3072
C_NQ, C_NK, C_NV, C_GA, C_GB = 3104, 3616, 4128, 4640, 5664


def weight_chunks():
    out = []
    for l in range(DEPTH):
        out += [(l, "ada", n) for n in range(12)]
        out += [(l, n, 0) for n in ("nq", "nk", "nv", "lr", "q", "k")] + [(l, "v", 0), (l, "v", 1)]
        out += [(l, "g", 0), (l, "g", 1)]
        for j in range(2):
            out += [(l, n, j) for n in ("ga", "bo", "gb", "bn")]
        out += [(l, "wo", 0), (l, "wo", 1)]
    return out


KIND = {"nq": (True, "act"), "nk": (True, "dve"), "nv": (False, "act"), "q": (False, "dve"), "k": (False, "dve"),
        "v": (False, "act"), "g": (False, "act"), "ga": (True, "act"), "bo": (True, "dve"), "gb": (True, "act"),
        "bn": (True, "dve"), "wo": (True, "dve")}


def q_tiles(l):
    return 4 if l < DEPTH - 1 else 2


def gemm_tiles(l, name):
    if KIND[name][0]:
        return 4
    return q_tiles(l) if name in ("q", "g") else 4


def evacuation_table(chunks):
    count, table = {"act": 0, "dve": 0}, {}
    for c, (l, name, _) in enumerate(chunks):
        if name in KIND:
            for i in range(gemm_tiles(l, name)):
                e = KIND[name][1]
                count[e] += 1
                table[c, i] = (e, count[e])
    return table


def bank_history(chunks):
    last, before, number, n = {}, {}, {}, 0
    for c, (l, name, _) in enumerate(chunks):
        if name in KIND:
            for i in range(gemm_tiles(l, name)):
                before[c, i] = last.get(i)
                last[i] = (c, i)
                n += 1
                number[c, i] = n
    return before, number


def build(nc, x, c, ctx, c_ctx, w_ada, b_ada, norm1_w, norm2_w, w_in, w_gk_up, b_gk, gla_norm_w, rpb,
          w_bo_gla, w_bo_na, w_out, w_router, b_router, w1, w3, w2, final_norm_w, consts, out):
    CHUNKS = weight_chunks()
    EVAC = evacuation_table(CHUNKS)
    BEFORE, NUMBER = bank_history(CHUNKS)
    RING = 2

    with ExitStack() as cm:
        def sb(name, shape, dt=F32):
            return cm.enter_context(nc.sbuf_tensor(name, shape, dt))

        def sem(name):
            return cm.enter_context(nc.semaphore(name))

        U = sb("units", [P, 12, 4096])
        xT = U[:, 0, :].rearrange("p (k t) -> p k t", k=KT)
        hT = U[:, 1, :].rearrange("p (k t) -> p k t", k=KT)
        ring = [U[:, 2 + r, :].rearrange("p (k n) -> p k n", k=8) for r in range(RING)]
        nqT = U[:, 4, 0:2048].rearrange("p (j t) -> p j t", j=4)
        nkT = U[:, 4, 2048:4096].rearrange("p (j t) -> p j t", j=4)
        O = U[:, 4, :].rearrange("p (i n) -> p i n", i=4)
        qk = U[:, 5, :].rearrange("p (a i n) -> p a i n", a=2, i=4)
        qkT = U[:, 6, :].rearrange("p (a h t) -> p a h t", a=2, h=GH)
        V = U[:, 7, :].rearrange("p (i n) -> p i n", i=4)
        gates = U[:, 8, :].rearrange("p (d i n) -> p d i n", d=2, i=4)
        glaT = U[:, 8, :].rearrange("p (k t) -> p k t", k=8)
        Pb = U[:, 9, 0:1024].rearrange("p (b n) -> p b n", b=2)
        PT = U[:, 9, 1024:3072].rearrange("p (b j q) -> p b j q", b=2, j=4)
        rtmp = U[:, 9, 3072:4096].rearrange("p (f n) -> p f n", f=2)
        S = U[:, 9, :].rearrange("p (d s e) -> p d s e", d=2, s=8)
        sq = U[:, 9, :].rearrange("p (k t) -> p k t", k=8)
        mT = U[:, 9, :].rearrange("p (k t) -> p k t", k=8)
        nv = U[:, 10, 0:2048].rearrange("p (i n) -> p i n", i=4)
        naT = U[:, 10, 2048:4096].rearrange("p (j t) -> p j t", j=4)
        tmp10 = U[:, 10, 0:2048]
        rt = U[:, 10, 0:1024]
        attP = tmp10[:, 0:512].rearrange("p (d i t) -> p d i t", d=2, i=4)
        attS = tmp10[:, 512:1024].rearrange("p (i t) -> p i t", i=4)
        junk = tmp10[:, 1024:1280]
        sg = tmp10[:, 0:1024].rearrange("p (b n) -> p b n", b=2)
        SG = U[:, 11, :].rearrange("p (a i t) -> p a i t", a=2, i=4)
        zero = U[:, 8, 0:1024]
        bias = U[:, 11, :].rearrange("p (i h k) -> p i h k", i=2, h=NH)
        gt = U[:, 11, :].rearrange("p (d a t) -> p d a t", d=2, a=4)
        h2n = U[:, 11, :].rearrange("p (i n) -> p i n", i=4)
        xload = U[:, 5, :].rearrange("p (i n) -> p i n", i=4)
        adarow = U[:, 6, 0:1536]
        W1 = [U[:, 4:6, :].rearrange("p a (k n) -> p (a k) n", k=4), U[:, 8:10, :].rearrange("p a (k n) -> p (a k) n", k=4)]
        W3 = [U[:, 6:8, :].rearrange("p a (k n) -> p (a k) n", k=4), U[:, 10:12, :].rearrange("p a (k n) -> p (a k) n", k=4)]
        W2 = U[:, 2:4, :].rearrange("p a (k n) -> p (a k) n", k=4)
        xblk = U[:, 1, 0:512]
        xbT = U[:, 1, 512:1024].rearrange("p (c a s) -> p c a s", c=4, a=2)
        xbT_flat = U[:, 1, 512:1024]
        silu_g = U[:, 1, 1024:1536]
        hblk = U[:, 1, 1536:2048]
        hbT = U[:, 1, 2048:2560].rearrange("p (c a s) -> p c a s", c=4, a=2)
        yblk = U[:, 1, 2560:3072]
        yg = U[:, 4:6, :].rearrange("p a (b n) -> p (a b) n", b=4)
        z = U[:, 6, :].rearrange("p (i n) -> p i n", i=4)
        fin = U[:, 7, :].rearrange("p (i n) -> p i n", i=4)

        K = sb("constants", [P, 1361])
        ident = K[:, 0:128]
        ones = K[:, 128:256]
        cum = K[:, 256:768].rearrange("p (d a t) -> p d a t", d=2, a=2)
        amask = K[:, 768:896].rearrange("p (d t) -> p d t", d=2)
        strict = K[:, 896:1024]
        rope = K[:, 1024:1280].rearrange("p (f i a e) -> p f i a e", f=2, i=2, a=2)
        cmask = K[:, 1280:1344]
        ramp = K[:, 1344:1360]
        epst = K[:, 1360:1361]
        vrow = U[:, 11, 0:256].rearrange("p (a n) -> p a n", a=2)
        vcol = sb("vector_columns", [P, 128 + 24])
        csil = sb("silu_c", [P, KT, 32])
        mod = sb("modulations", [P, DEPTH, 2, 48])
        s1 = sb("norm_scales", [P, DEPTH, 2, 2, KT])
        lrn = U[:, 9, 3072:3200].rearrange("p (i e) -> p i e", i=4)
        lrT = U[0:33, 9, 2048:2560]
        up = sb("gate_up", [33, 2 * 512])
        gnw = sb("gla_norm_w", [P, DV])
        wr = sb("router_w", [P, KT, NE])
        br = sb("router_b", [P, NE])
        dec = sb("chunk_decays", [P, 2, NCH])
        ssq = sb("head_squares", [P, 4, GH])
        st = sb("softmax_stats", [P, 4, 4])
        wsel = sb("choice_weights", [P, 4, 2])
        waited = sb("waited", [1, DEPTH])
        slot = sb("choice_slots", [P, 4, 2], I32)
        blocks = sb("expert_blocks", [P, 2, NE], I32)

        ps = cm.enter_context(nc.psum_tensor("ps", [P, 8, 512], F32))

        rp = nc.dram_tensor("bias_padded", [DEPTH, NH, 15, RPAD], F32, kind="Internal").ap()
        RW = 2 * GROWS - 1
        rx = nc.dram_tensor("bias_copies", [DEPTH, GRID_W, NH, RW, RPAD], F32, kind="Internal").ap()
        xbuf = nc.dram_tensor("dispatched", [XROWS, D], F32, kind="Internal").ap()
        ybuf = nc.dram_tensor("expert_out", [MAXB * BLK, D], F32, kind="Internal").ap()


        met = sem("compute_engines_met")
        s_const = sem("constants_in")
        s_vec = sem("vectors_in")
        s_x = sem("tokens_in")
        s_rw = sem("router_weights_in")
        s_zero = sem("zeros_made")
        s_zfill = sem("scratch_zeroed")
        s_rp = sem("bias_table_in")
        s_bias = sem("bias_in")
        s_par = sem("layer_vectors_in")
        s_w = [sem(f"weights_in_{r}") for r in range(RING)]
        s_wused = sem("chunk_used")
        acc_ready = sem("acc_ready")
        acc_free = {"act": sem("acc_emptied_act"), "dve": sem("acc_emptied_dve")}
        chain = {e: sem("own_steps_" + e) for e in ("act", "dve", "pool")}
        lr_one = sem("lr_ones_row")
        t_x, v_t, v_c = sem("tokens_turned"), sem("vectors_turned"), sem("vectors_copied")
        s_rpz, s_rx = sem("bias_table_zeroed"), sem("bias_copies_made")
        a_row, a_sb, a_col = sem("ada_rows"), sem("ada_rows_copied"), sem("ada_columns")
        n_sq, n_sum, n_root, n_rstd, n_h = (sem("norm_" + n) for n in ("squares", "sums", "root", "rstd", "scaled"))
        lr_ps, lr_sb, lr_tp, lr_T, gz, gl, gd = (sem(n) for n in (
            "lr_products", "lr_copied", "lr_turned", "lrT_copied", "gate_products", "gate_logs", "gates_made"))
        b_m = sem("bias_masked")
        na_sc, na_mx, na_e, na_p, na_tp, na_tc, na_o, na_oc = (sem(n) for n in (
            "na_scores", "na_max", "na_exp", "na_probs", "na_turned", "na_turned_copied", "na_out", "na_out_copied"))
        g_cum, g_exp, g_fac, g_kt, g_ktc, g_att, g_attm, g_ds, g_st, g_o, g_oc = (sem("gla_" + n) for n in (
            "sums", "exps", "factors", "kdecT", "kdec_copied", "att", "att_masked", "delta", "state", "out", "out_copied"))
        g_root, g_gated, g_t, g_tc_act, g_tc_dve = (sem("gla_" + n) for n in (
            "root", "gated", "out_turned", "turned_copied_act", "turned_copied_dve"))
        r_lg, r_aff, r_nat, r_natc, r_sel, r_rank, r_slot = (sem("route_" + n) for n in (
            "logits", "affinities", "turned", "copied", "selection", "ranks", "slots"))
        moe = [{n: sem(f"{n}_{l}") for n in (
            "x_in", "xT_ps", "xT_sb", "g_ps", "u_ps", "silu", "h_sb", "hT_ps", "hT_sb", "y_ps", "y_sb", "y_out",
            "w1_in0", "w1_in1", "w3_in0", "w3_in1", "w2_in", "scattered")} for l in range(DEPTH)]
        AHEAD = {"h_sb": 1, "hT_ps": 1, "y_ps": 1, "y_sb": 1, "y_out": 32}
        s_gather, c_z, c_t = sem("gathered"), sem("combined"), sem("combined_turned")
        f_t, f_c, s_out = sem("final_turned"), sem("final_copied"), sem("stored")

        STAGES = ("ada", "norm1", "mix", "gla", "gate", "merge", "norm2", "route", "experts", "combine")

        def met_at(l, stage):
            return 3 * (2 + len(STAGES) * l + STAGES.index(stage))

        def meet(eng, value):
            eng.drain().then_inc(met, 1)
            eng.wait_ge(met, value)

        def chunk_source(l, name, n):
            k8 = "(k p) n -> p k n"
            cols = slice(n * 512, (n + 1) * 512)
            if name == "ada":
                return w_ada[l][:, cols].rearrange(k8, p=P)
            if name == "bo":
                return w_bo_gla[l][:, cols].rearrange(k8, p=P)
            if name == "bn":
                return w_bo_na[l][:, cols].rearrange(k8, p=P)
            if name == "wo":
                return w_out[l][:, cols].rearrange(k8, p=P)
            c0 = {"nq": C_NQ, "nk": C_NK, "nv": C_NV, "q": C_Q, "k": C_K, "lr": C_LR, "v": C_V, "g": C_G,
                  "ga": C_GA, "gb": C_GB}[name] + n * 512
            return w_in[l][:, c0:c0 + (32 if name == "lr" else 512)].rearrange(k8, p=P)

        def chunk_view(cix):
            name, r = CHUNKS[cix][1], ring[cix % RING]
            return r[:, 0:4, :] if name == "bn" else r[:, :, 0:32] if name == "lr" else r

        def chunk_index(l, name, n=0):
            return CHUNKS.index((l, name, n))

        def used(cix):
            l, name, _ = CHUNKS[cix]
            if name in KIND:
                return acc_ready, NUMBER[cix, gemm_tiles(l, name) - 1]
            return s_wused, sum(CHUNKS[k][1] not in KIND for k in range(cix + 1))

        def scan_order(d):
            return [4, 5, 6, 7, 0, 1, 2, 3] if d == 0 else [7, 6, 5, 4, 3, 2, 1, 0]

        def streams(l):
            return [(0, 0, SEQ), (1, SEQ, TOK)][:q_tiles(l) // 2]

        def na_units(l):
            return [(h, s, i) for h in range(NH) for s in range(q_tiles(l) // 2) for i in range(2)]

        NA0 = [0, len(na_units(0))]
        GT0 = [0, GH * q_tiles(0)]
        NH0 = [0, 16, 32, 48, 56]
        QT0 = [0, q_tiles(0)]

        def mix_events(l):
            tiles = [(chunk_index(l, n, j), i) for n, j in (("q", 0), ("k", 0), ("v", 0), ("v", 1))
                     for i in range(gemm_tiles(l, n))]
            steps, ev, t = len(na_units(l)) + 3, [], 0
            for n, tile in enumerate(tiles):
                ev.append(("tile",) + tile)
                while t < steps * (n + 1) // len(tiles):
                    ev.append(("na", t, 0))
                    t += 1
            return ev

        ZFILLS = 16 * ((XROWS + MAXB * BLK) // P)

        block = cm.enter_context(nc.Block())

        @block.sync
        def _(sp):
            sp.dma_start(K[:], consts).then_inc(s_const, 16)
            for l in range(DEPTH):
                for src, r0, r1 in ((b_ada, 0, 48), (norm1_w, 48, 56), (norm2_w, 56, 64)):
                    sp.dma_start(vrow[64 * l + r0:64 * l + r1, 0, :], src[l].rearrange("(m p) -> m p", p=P)).then_inc(s_vec, 16)
            for src, r0 in ((final_norm_w, 0), (c[0], 8), (c_ctx, 16)):
                sp.dma_start(vrow[r0:r0 + 8, 1, :], src.rearrange("(m p) -> m p", p=P)).then_inc(s_vec, 16)
            sp.dma_start(xload[:, 0:2, :], x[0].rearrange("(i p) n -> p i n", p=P)).then_inc(s_x, 16)
            sp.dma_start(xload[:, 2:4, :], ctx[0].rearrange("(i p) n -> p i n", p=P)).then_inc(s_x, 16)
            sp.dma_start(wr[:], w_router.rearrange("(k p) e -> p k e", p=P)).then_inc(s_rw, 16)
            sp.dma_start(br[:], b_router.rearrange("(a e) -> a e", a=1).to_broadcast([P, NE])).then_inc(s_rw, 16)

            def load_chunk(cix):
                if cix >= RING:
                    sp.wait_ge(*used(cix - RING))
                sp.dma_start(chunk_view(cix), chunk_source(*CHUNKS[cix])).then_inc(s_w[cix % RING], 16)

            def load_expert(l, e, which, buf, name):
                w = {"w1": w1, "w3": w3, "w2": w2}[which][l]
                src = w[bass.ds(e, 1)].rearrange("a (k p) n -> p (a k) n", p=P)
                sp.dma_start(buf, src).then_inc(moe[l][name], 16)

            for l in range(DEPTH):
                if l:
                    sp.wait_ge(met, met_at(l - 1, "combine"))
                first = chunk_index(l, "ada", 0)
                for cix in range(first, chunk_index(l, "wo", 1) + 1):
                    load_chunk(cix)
                    if CHUNKS[cix][1] == "gb":
                        sp.wait_ge(met, met_at(l, "gate"))
                        if CHUNKS[cix][2] == 0:
                            load_expert(l, 0, "w1", W1[0], "w1_in0")
                        else:
                            load_expert(l, 0, "w3", W3[0], "w3_in0")
                    if cix == first + 11:
                        if l == 0:
                            sp.wait_ge(met, 3)
                            sp.wait_ge(s_rx, 32)
                        for r in range(GROWS):
                            for kr in range(GROWS):
                                src = bass.AP(tensor=rx.tensor,
                                              offset=(l * GRID_W * NH * RW + GROWS - 1 - r + kr) * RPAD + GRID_W - 1,
                                              ap=[[NH * RW * RPAD - 1, GRID_W], [RW * RPAD, NH], [1, GRID_W]])
                                sp.dma_start(bias[r % 2 * 64:r % 2 * 64 + 64, r // 2, :, kr * GRID_W:(kr + 1) * GRID_W],
                                             src).then_inc(s_bias, 16)
                        if l:
                            sp.wait_ge(met, met_at(0, "gate"))
                        sp.wait_ge(s_zero, 1)
                        for d in range(2):
                            sp.dma_start(up[16 * d:16 * d + 16, 512 * d:512 * d + 512], w_gk_up[l, d]).then_inc(s_par, 16)
                        sp.dma_start(up[32:33, :], b_gk[l].rearrange("(a d) n -> a (d n)", a=1)).then_inc(s_par, 16)
                        sp.dma_start(gnw[:], gla_norm_w[l].rearrange("(a e) -> a e", a=1).to_broadcast([P, DV])).then_inc(s_par, 16)
                m = moe[l]
                sp.wait_ge(met, met_at(l, "merge"))
                load_expert(l, 0, "w2", W2, "w2_in")
                sp.wait_ge(met, met_at(l, "route"))
                sp.wait_ge(m["scattered"], 16 * 2 * q_tiles(l))
                load_expert(l, 1, "w1", W1[1], "w1_in1")
                load_expert(l, 1, "w3", W3[1], "w3_in1")
                with sp.Fori(0, NE // 2 - 1) as p:
                    b1 = sp.value_load(blocks[0:1, 1, bass.ds(2 * p + 1, 1)], min_val=0, max_val=MAXB)
                    sp.wait_ge(m["y_ps"], b1 + 1)
                    load_expert(l, 2 * p + 1, "w2", W2, "w2_in")
                    load_expert(l, 2 * p + 2, "w1", W1[0], "w1_in0")
                    load_expert(l, 2 * p + 2, "w3", W3[0], "w3_in0")
                    b2 = sp.value_load(blocks[0:1, 1, bass.ds(2 * p + 2, 1)], min_val=0, max_val=MAXB)
                    sp.wait_ge(m["y_ps"], b2 + 1)
                    load_expert(l, 2 * p + 2, "w2", W2, "w2_in")
                    load_expert(l, 2 * p + 3, "w1", W1[1], "w1_in1")
                    load_expert(l, 2 * p + 3, "w3", W3[1], "w3_in1")
                b1 = sp.value_load(blocks[0:1, 1, NE - 1:NE], min_val=0, max_val=MAXB)
                sp.wait_ge(m["y_ps"], b1 + 1)
                load_expert(l, NE - 1, "w2", W2, "w2_in")
            sp.wait_ge(f_c, 2)
            sp.dma_start(out[0].rearrange("(i p) n -> p i n", p=P), fin[:, 0:2, :]).then_inc(s_out, 16)
            sp.wait_ge(s_out, 16)

        @block.tensor
        def _(pe):
            def turn(dst, src, n=P):
                return nc.tensor.transpose(dst, src, ident[0:n, 0:n])

            def gemm_tile(cix, i):
                l, name, n = CHUNKS[cix]
                w, TQ = chunk_view(cix), q_tiles(l) * P
                if i == 0:
                    pe.wait_ge(s_w[cix % RING], 16 * (cix // RING + 1))
                if BEFORE[cix, i] is not None:
                    e, cnt = EVAC[BEFORE[cix, i]]
                    pe.wait_ge(acc_free[e], cnt)
                if KIND[name][0]:
                    src = {"bo": glaT, "bn": naT, "wo": mT}.get(name, hT)
                    N = TOK if name == "nk" else TQ
                    kk = 4 if name == "bn" else 8
                    for k in range(kk):
                        mm = nc.tensor.matmul(ps[:, i, 0:N], w[:, k, i * P:(i + 1) * P], src[:, k, 0:N],
                                              start=(k == 0), stop=(k == kk - 1))
                else:
                    for k in range(8):
                        mm = nc.tensor.matmul(ps[:, i, :], hT[:, k, i * P:(i + 1) * P], w[:, k, :],
                                              start=(k == 0), stop=(k == 7))
                mm.then_inc(acc_ready, 1)

            def na_step(l, t):
                u0, units = NA0[l], na_units(l)
                if t < len(units):
                    h, s, i = units[t]
                    hp, k0 = (h % 2) * HD, s * SEQ
                    if u0 + t >= 2:
                        pe.wait_ge(na_e, u0 + t - 1)
                    nc.tensor.matmul(ps[:, 4 + t % 2, k0:TOK], nqT[hp:hp + HD, h // 2, (2 * s + i) * P:(2 * s + i + 1) * P],
                                     nkT[hp:hp + HD, h // 2, k0:TOK], start=True, stop=True).then_inc(na_sc, 1)
                if 0 <= t - 2 < len(units):
                    h, s, i = units[t - 2]
                    pe.wait_ge(na_p, u0 + t - 1)
                    if u0 + t - 2:
                        pe.wait_ge(na_tc, u0 + t - 2)
                    for j in range(2 * s, 4):
                        mm = turn(ps[:, 6, j * P:(j + 1) * P], Pb[:, (t - 2) % 2, j * P:(j + 1) * P])
                    mm.then_inc(na_tp, 1)
                if t - 3 >= 0 and (t - 3) % 2:
                    h, s, i = units[t - 3]
                    hs, hp = (t - 3) // 2, (h % 2) * HD
                    pe.wait_ge(na_tc, u0 + t - 2)
                    if u0 // 2 + hs >= 2:
                        pe.wait_ge(na_oc, u0 // 2 + hs - 1)
                    for j in range(2 * s, 4):
                        mm = nc.tensor.matmul(ps[hp:hp + HD, 7, (hs % 2) * 256:(hs % 2) * 256 + 256],
                                              nv[:, j, h * HD:(h + 1) * HD], PT[:, hs % 2, j, :],
                                              start=(j == 2 * s), stop=(j == 3), skip_group_check=True)
                    mm.then_inc(na_o, 1)

            def gla_head(l, h):
                n, NQC = GH * l + h, 2 * q_tiles(l)
                for d in range(2):
                    if n:
                        pe.wait_ge(g_st, 14 * n)
                    for i in range(4):
                        mm = nc.tensor.matmul(ps[:, 2 * d + i // 2, (i % 2) * 256:(i % 2) * 256 + 256],
                                              gates[:, d, i, h * DK:(h + 1) * DK], cum[:, d].rearrange("p a t -> p (a t)"),
                                              start=True, stop=True)
                    mm.then_inc(g_cum, 1)
                for d in range(2):
                    pe.wait_ge(g_fac, 2 * n + d + 1)
                    if d == 0 and n:
                        pe.wait_ge(g_attm, n)
                        pe.wait_ge(g_oc, GT0[l] + h * q_tiles(l))
                    for i in range(4):
                        mm = turn(ps[:, 4 + d, i * P:(i + 1) * P], gt[:, d, 2, i * P:(i + 1) * P])
                    mm.then_inc(g_kt, 1)
                    for cc in range(NQC):
                        t0 = (cc % 2) * CH
                        mm = nc.tensor.matmul(ps[t0:t0 + CH, 6, d * 256 + (cc // 2) * CH:d * 256 + (cc // 2 + 1) * CH],
                                              gt[:, d, 2, cc * CH:(cc + 1) * CH], gt[:, d, 1, cc * CH:(cc + 1) * CH],
                                              start=True, stop=True, skip_group_check=True)
                mm.then_inc(g_att, 1)
                pe.wait_ge(g_ktc, 2 * n + 2)
                pe.wait_ge(g_exp, 2 * n + 2)
                for i in range(7):
                    for d in range(2):
                        cc = scan_order(d)[i]
                        t0 = (cc % 2) * CH
                        if i >= 2:
                            pe.wait_ge(g_st, 14 * n + 2 * (i - 2) + d + 1)
                        b = ps[:, 2 * d + i % 2, 0:DV]
                        nc.tensor.matmul(b, gt[t0:t0 + CH, d, 3, (cc // 2) * P:(cc // 2 + 1) * P],
                                         V[t0:t0 + CH, cc // 2, h * DV:(h + 1) * DV],
                                         start=True, stop=True, skip_group_check=True).then_inc(g_ds, 1)
                pe.wait_ge(g_attm, n + 1)
                pe.wait_ge(g_st, 14 * n + 14)
                for i in range(q_tiles(l)):
                    o = GT0[l] + h * q_tiles(l) + i
                    if o >= 2:
                        pe.wait_ge(g_oc, o - 1)
                    dst = ps[:, (7, 5)[i % 2], 0:DV]
                    nc.tensor.matmul(dst, attS[:, i, :], V[:, i, h * DV:(h + 1) * DV], start=True, stop=False,
                                     skip_group_check=True)
                    for cc in (2 * i, 2 * i + 1):
                        t0 = (cc % 2) * CH
                        ds_ = [d for d in range(2) if scan_order(d).index(cc)]
                        for d in ds_:
                            mm = nc.tensor.matmul(dst[t0:t0 + CH, :], gt[:, d, 0, cc * CH:(cc + 1) * CH],
                                                  S[:, d, scan_order(d).index(cc), :], start=False, stop=(d == ds_[-1]),
                                                  skip_group_check=True)
                    mm.then_inc(g_o, 1)

            def norm_sum(n, T):
                pe.wait_ge(n_sq, n + 1)
                for k in range(KT):
                    mm = nc.tensor.matmul(ps[:, 7, 0:T], ones, sq[:, k, 0:T], start=(k == 0), stop=(k == KT - 1))
                mm.then_inc(n_sum, 1)

            pe.wait_ge(s_const, 16)
            pe.wait_ge(s_x, 32)
            for k in range(KT):
                for i in range(4):
                    mm = turn(ps[:, k, i * P:(i + 1) * P], xload[:, i, k * P:(k + 1) * P])
                mm.then_inc(t_x, 1)
            pe.wait_ge(s_vec, 16 * 9)
            pe.wait_ge(v_c, 1)
            turn(ps[:, 0, 0:128], vrow[:, 0, :])
            turn(ps[:, 0, 128:152], vrow[0:24, 1, :], 24).then_inc(v_t, 1)
            meet(pe, 3)

            for l in range(DEPTH):
                m, TQ, NQ = moe[l], q_tiles(l) * P, q_tiles(l)
                for n in range(12):
                    cix = chunk_index(l, "ada", n)
                    pe.wait_ge(s_w[cix % RING], 16 * (cix // RING + 1))
                    for k in range(KT):
                        for j in range(4):
                            mm = nc.tensor.matmul(ps[32 * j:32 * j + 32, n // 4, (n % 4) * P:(n % 4 + 1) * P], csil[:, k, :],
                                                  ring[cix % RING][:, k, j * P:(j + 1) * P], start=(k == 0), stop=(k == KT - 1),
                                                  skip_group_check=True)
                    mm.then_inc(s_wused, 1)
                pe.wait_ge(a_sb, l + 1)
                for n in range(12):
                    mm = turn(ps[:, 3 + n // 4, (n % 4) * P:(n % 4 + 1) * P], adarow[:, n * P:(n + 1) * P])
                mm.then_inc(a_col, 1)
                meet(pe, met_at(l, "ada"))
                norm_sum(2 * l, TOK)
                meet(pe, met_at(l, "norm1"))

                for name in ("nq", "nk", "nv"):
                    cix = chunk_index(l, name)
                    for i in range(gemm_tiles(l, name)):
                        gemm_tile(cix, i)
                cix = chunk_index(l, "lr")
                pe.wait_ge(s_w[cix % RING], 16 * (cix // RING + 1))
                for i in range(4):
                    for k in range(KT):
                        mm = nc.tensor.matmul(ps[:, 7, i * 32:(i + 1) * 32], hT[:, k, i * P:(i + 1) * P], chunk_view(cix)[:, k, :],
                                              start=(k == 0), stop=(k == KT - 1), skip_group_check=True)
                mm.then_inc(s_wused, 1)
                pe.wait_ge(lr_sb, l + 1)
                for i in range(4):
                    mm = turn(ps[0:32, 6, i * P:(i + 1) * P], lrn[:, i, :])
                mm.then_inc(lr_tp, 1)
                pe.wait_ge(lr_T, l + 1)
                pe.wait_ge(lr_one, l + 1)
                pe.wait_ge(s_par, 64 * (l + 1))
                for u in range(8):
                    d, i = u % 2, u // 2
                    if 8 * l + u >= 2:
                        pe.wait_ge(gd, 8 * l + u - 1)
                    nc.tensor.matmul(ps[:, 4 + u % 2, :], lrT[:, i * P:(i + 1) * P], up[:, 512 * d:512 * d + 512],
                                     start=True, stop=True).then_inc(gz, 1)
                pe.wait_ge(gd, 8 * l + 8)
                for ev, a, b in mix_events(l):
                    if ev == "tile":
                        gemm_tile(a, b)
                    else:
                        if a == 0:
                            pe.wait_ge(acc_free["act"], EVAC[chunk_index(l, "nv"), 3][1])
                            pe.wait_ge(acc_free["dve"], EVAC[chunk_index(l, "nk"), 3][1])
                        na_step(l, a)
                for a in range(2):
                    T = TQ if a == 0 else TOK
                    pe.wait_ge(acc_free["dve"], EVAC[chunk_index(l, "k"), 3][1])
                    for h in range(GH):
                        b = 4 * a + h
                        if a == 0:
                            if h == 0:
                                pe.wait_ge(acc_free["act"], EVAC[chunk_index(l, "v", 1), 3][1])
                                pe.wait_ge(na_oc, (NA0[l] + len(na_units(l))) // 2)
                        for i in range(T // P):
                            mm = turn(ps[:, b, i * P:(i + 1) * P], qk[:, a, i, h * DK:(h + 1) * DK])
                        mm.then_inc(g_t, 1)
                meet(pe, met_at(l, "mix"))
                for h in range(GH):
                    gla_head(l, h)
                meet(pe, met_at(l, "gla"))
                for n in range(2):
                    for i in range(NQ):
                        gemm_tile(chunk_index(l, "g", n), i)
                pe.wait_ge(g_gated, 2 * QT0[l] + 2 * NQ)
                for k in range(8):
                    if k >= 4:
                        pe.wait_ge((g_tc_act, g_tc_dve)[k % 2], 4 * l + (k - 4) // 2 + 1)
                    for i in range(NQ):
                        mm = turn(ps[:, 4 + k % 4, i * P:(i + 1) * P], O[:, i, k * P:(k + 1) * P])
                    mm.then_inc(g_t, 1)
                meet(pe, met_at(l, "gate"))
                for j in range(2):
                    for name in ("ga", "bo", "gb", "bn"):
                        for i in range(4):
                            gemm_tile(chunk_index(l, name, j), i)
                pe.wait_ge(acc_free["dve"], EVAC[chunk_index(l, "bn", 1), 3][1])
                for n in range(2):
                    for i in range(4):
                        gemm_tile(chunk_index(l, "wo", n), i)
                meet(pe, met_at(l, "merge"))
                norm_sum(2 * l + 1, TQ)
                meet(pe, met_at(l, "norm2"))

                pe.wait_ge(s_rw, 32)
                for i in range(NQ):
                    for k in range(KT):
                        mm = nc.tensor.matmul(ps[:, 0, i * NE:(i + 1) * NE], hT[:, k, i * P:(i + 1) * P], wr[:, k, :],
                                              start=(k == 0), stop=(k == KT - 1), skip_group_check=True)
                mm.then_inc(r_lg, 1)
                for i in range(NQ):
                    b = 1 + 2 * (i % 3)
                    if i >= 3:
                        pe.wait_ge(r_natc, QT0[l] + i - 2)
                    for k in range(KT):
                        mm = turn(ps[:, b + k // 4, (k % 4) * P:(k % 4 + 1) * P], hT[:, k, i * P:(i + 1) * P])
                    mm.then_inc(r_nat, 1)
                pe.wait_ge(r_sel, l + 1)
                M = rt[:, 0:NQ * NE]
                for i in range(NQ):
                    for j in range(i + 1):
                        mm = nc.tensor.matmul(ps[:, 7, i * NE:(i + 1) * NE], ones if j < i else strict, M[:, j * NE:(j + 1) * NE],
                                              start=(j == 0), stop=(j == i), skip_group_check=True)
                for j in range(NQ):
                    mm = nc.tensor.matmul(ps[:, 7, 64:64 + NE], ones, M[:, j * NE:(j + 1) * NE],
                                          start=(j == 0), stop=(j == NQ - 1), skip_group_check=True)
                mm.then_inc(r_rank, 1)
                meet(pe, met_at(l, "route"))

                def turn_block(b):
                    pe.wait_ge(m["x_in"], 32 * b + 32)
                    for cc in range(4):
                        mm = turn(ps[:, 0, cc * P:(cc + 1) * P], xblk[:, cc * P:(cc + 1) * P])
                    mm.then_inc(m["xT_ps"], 1)

                def expert_block(b, p, par):
                    pe.wait_ge(m["xT_sb"], b + 1)
                    for bank, w, arrived, done in ((1, W1[par], "w1_in", "g_ps"), (2, W3[par], "w3_in", "u_ps")):
                        pe.wait_ge(m[f"{arrived}{par}"], 16 * p + 16)
                        for k in range(KT):
                            for a in range(2):
                                mm = nc.tensor.matmul(ps[64 * a:64 * a + 64, bank, :], xbT[:, k % 4, k // 4, :],
                                                      w[:, k, a * 512:(a + 1) * 512], start=(k == 0), stop=(k == KT - 1),
                                                      skip_group_check=True)
                        mm.then_inc(m[done], 1)
                    turn_block(b + 1)
                    pe.wait_ge(m["h_sb"], b + 2)
                    for cc in range(4):
                        mm = turn(ps[:, 3, cc * P:(cc + 1) * P], hblk[:, cc * P:(cc + 1) * P])
                    mm.then_inc(m["hT_ps"], 1)
                    pe.wait_ge(m["hT_sb"], b + 1)
                    pe.wait_ge(m["y_sb"], b + 1)

                def expert_out(par):
                    for k in range(KT):
                        for a in range(2):
                            mm = nc.tensor.matmul(ps[64 * a:64 * a + 64, 4, :], hbT[:, k % 4, k // 4, :],
                                                  W2[:, k, a * 512:(a + 1) * 512], start=(k == 0), stop=(k == KT - 1),
                                                  skip_group_check=True)
                    mm.then_inc(m["y_ps"], 1)

                for name in AHEAD:
                    pe.sem_inc(m[name], AHEAD[name])
                turn_block(0)
                with pe.Fori(0, NE // 2) as p:
                    for par in range(2):
                        b1 = pe.value_load(blocks[0:1, 0, bass.ds(2 * p + par, 1)], min_val=1, max_val=MAXB)
                        b0 = pe.value_load(blocks[0:1, 1, bass.ds(2 * p + par, 1)], min_val=0, max_val=MAXB)
                        with pe.Fori(b0, b1) as b:
                            expert_block(b, p, par)
                            pe.wait_ge(m["w2_in"], 32 * p + 16 * par + 16)
                            expert_out(par)
                meet(pe, met_at(l, "experts"))
                for k in range(KT):
                    if k == 0:
                        pe.wait_ge(c_z, QT0[l] + NQ)
                    for i in range(NQ):
                        mm = turn(ps[:, k, i * P:(i + 1) * P], z[:, i, k * P:(k + 1) * P])
                    mm.then_inc(c_t, 1)
                meet(pe, met_at(l, "combine"))

            norm_sum(2 * DEPTH, SEQ)
            pe.wait_ge(n_h, NH0[2 * DEPTH] + KT)
            for i in range(2):
                for k in range(KT):
                    mm = turn(ps[:, 2 * i + k // 4, (k % 4) * P:(k % 4 + 1) * P], hT[:, k, i * P:(i + 1) * P])
                mm.then_inc(f_t, 1)

        @block.scalar
        def _(act):
            own = [0]

            def link(ins):
                own[0] += 1
                ins.then_inc(chain["act"], 1)
                act.wait_ge(chain["act"], own[0])

            def evacuate(cix, i):
                l, name, n = CHUNKS[cix]
                TQ = q_tiles(l) * P
                act.wait_ge(acc_ready, NUMBER[cix, i])
                if name == "nq":
                    ins = nc.scalar.activation(nqT[:, i, 0:TQ], ps[:, i, 0:TQ], ACT.Copy, scale=HD ** -0.5)
                elif name == "nv":
                    ins = nc.scalar.activation(nv[:, i, :], ps[:, i, :], ACT.Copy)
                elif name == "v":
                    ins = nc.scalar.activation(V[:, i, n * 512:(n + 1) * 512], ps[:, i, :], ACT.Copy)
                elif name == "g":
                    t = 2 * QT0[l] + n * q_tiles(l) + i
                    if n * q_tiles(l) + i >= 2:
                        act.wait_ge(g_gated, t - 1)
                    ins = nc.scalar.activation(sg[:, t % 2, :], ps[:, i, :], ACT.Silu)
                else:
                    a = 0 if name == "ga" else 1
                    if n:
                        act.wait_ge(acc_free["dve"], EVAC[chunk_index(l, ("bo", "bn")[a], 0), i][1])
                    ins = nc.scalar.activation(SG[:, a, i, 0:TQ], ps[:, i, 0:TQ], ACT.Sigmoid)
                ins.then_inc(acc_free["act"], 1)

            def na_step(l, t):
                u0, units = NA0[l], na_units(l)
                if t < len(units):
                    h, s, i = units[t]
                    act.wait_ge(na_mx, u0 + t + 1)
                    if u0 + t >= 2:
                        act.wait_ge(na_tp, u0 + t - 1)
                    nc.scalar.activation(Pb[:, t % 2, s * SEQ:TOK], ps[:, 4 + t % 2, s * SEQ:TOK], ACT.Exp,
                                         bias=st[:, t % 4, 0:1], accum_out=st[:, t % 4, 1:2]).then_inc(na_e, 1)
                if 0 <= t - 2 < len(units):
                    h, s, i = units[t - 2]
                    hs = (t - 2) // 2
                    act.wait_ge(na_tp, u0 + t - 1)
                    if u0 // 2 + hs >= 2:
                        act.wait_ge(na_o, u0 // 2 + hs - 1)
                    nc.scalar.activation(PT[:, hs % 2, 2 * s:4, i * P:(i + 1) * P],
                                         ps[:, 6, 2 * s * P:4 * P].rearrange("p (j q) -> p j q", q=P),
                                         ACT.Copy).then_inc(na_tc, 1)
                if t - 3 >= 0 and (t - 3) % 2:
                    h, s, i = units[t - 3]
                    hs, hp = (t - 3) // 2, (h % 2) * HD
                    act.wait_ge(na_o, u0 // 2 + hs + 1)
                    nc.scalar.activation(naT[hp:hp + HD, h // 2, s * SEQ:s * SEQ + SEQ],
                                         ps[hp:hp + HD, 7, (hs % 2) * 256:(hs % 2) * 256 + 256], ACT.Copy).then_inc(na_oc, 1)

            def norm(n, T, shift):
                nc.scalar.activation(sq[:, :, 0:T], xT[:, :, 0:T], ACT.Square).then_inc(n_sq, 1)
                act.wait_ge(n_sum, n + 1)
                nc.scalar.activation(tmp10[:, 0:T], ps[:, 7, 0:T], ACT.Sqrt, scale=1.0 / D, bias=epst).then_inc(n_root, 1)
                if shift is None:
                    return
                l, row = shift
                for k in range(KT):
                    for s, a, b in ((0, 0, SEQ), (1, SEQ, TOK)):
                        if a < T:
                            act.wait_ge(n_h, NH0[n] + k * (T // SEQ) + s + 1)
                            nc.scalar.activation(hT[:, k, a:b], hT[:, k, a:b], ACT.Identity,
                                                 bias=mod[:, l, s, row * 8 + k:row * 8 + k + 1])

            act.wait_ge(t_x, 8)
            nc.scalar.activation(xT[:, 4:8, :], ps[:, 4:8, :], ACT.Copy)
            act.wait_ge(v_c, 2)
            nc.scalar.activation(csil[:, :, 0:2].rearrange("p k s -> p s k"),
                                 vcol[:, 136:152].rearrange("p (s k) -> p s k", s=2), ACT.Silu)
            meet(act, 3)
            for l in range(DEPTH):
                m, TQ, NQ = moe[l], q_tiles(l) * P, q_tiles(l)
                act.wait_ge(s_wused, 13 * l + 12)
                nc.scalar.activation(adarow, ps[:, 0:3, :].rearrange("p b n -> p (b n)"), ACT.Copy).then_inc(a_sb, 1)
                meet(act, met_at(l, "ada"))
                norm(2 * l, TOK, (l, 0))
                meet(act, met_at(l, "norm1"))

                for name in ("nq", "nv"):
                    for i in range(gemm_tiles(l, name)):
                        evacuate(chunk_index(l, name), i)
                act.wait_ge(s_wused, 13 * l + 13)
                nc.scalar.activation(lrn, ps[:, 7, 0:128].rearrange("p (i e) -> p i e", i=4), ACT.Copy).then_inc(lr_sb, 1)
                act.wait_ge(lr_tp, l + 1)
                nc.scalar.activation(lrT[0:32, :], ps[0:32, 6, :], ACT.Copy).then_inc(lr_T, 1)
                act.wait_ge(s_zfill, ZFILLS)
                for u in range(8):
                    d, i = u % 2, u // 2
                    act.wait_ge(gz, 8 * l + u + 1)
                    g = gates[:, d, i, :]
                    link(nc.scalar.activation(g, ps[:, 4 + u % 2, :], ACT.Abs))
                    link(nc.scalar.activation(g, g, ACT.Exp, scale=-1.0))
                    nc.scalar.activation(g, g, ACT.Ln, bias=1.0).then_inc(gl, 1)
                for ev, a, b in mix_events(l):
                    if ev == "na":
                        na_step(l, a)
                    elif KIND[CHUNKS[a][1]][1] == "act":
                        evacuate(a, b)
                for h in range(GH):
                    act.wait_ge(g_t, 16 * l + h + 1)
                    nc.scalar.activation(qkT[:, 0, h, 0:TQ], ps[:, h, 0:TQ], ACT.Copy, scale=DK ** -0.5)
                meet(act, met_at(l, "mix"))

                for h in range(GH):
                    n = GH * l + h
                    for d in range(2):
                        act.wait_ge(g_cum, 2 * n + d + 1)
                        if h:
                            act.wait_ge(g_o, GT0[l] + h * NQ)
                        v = ps[:, 2 * d:2 * d + 2, :].rearrange("p b (i a t) -> p (b i) a t", i=2, a=2)
                        for slot_, a, scale in ((0, 0, 1 / TAU), (1, 1, -1 / TAU), (2, 1, 1 / TAU)):
                            ins = nc.scalar.activation(gt[:, d, slot_, :].rearrange("p (i t) -> p i t", i=4), v[:, :, a, :],
                                                       ACT.Exp, scale=scale)
                        ins.then_inc(g_exp, 1)
                    for d in range(2):
                        act.wait_ge(g_kt, 2 * n + d + 1)
                        nc.scalar.activation(gt[:, d, 3, :], ps[:, 4 + d, :], ACT.Copy).then_inc(g_ktc, 1)
                    for i in range(NQ):
                        o = GT0[l] + h * NQ + i
                        act.wait_ge(g_o, o + 1)
                        src = ps[:, (7, 5)[i % 2], 0:DV]
                        nc.scalar.activation(O[:, i, h * DV:(h + 1) * DV], src, ACT.Copy)
                        if h or i:
                            act.wait_ge(g_oc, o)
                        nc.scalar.activation(junk, src, ACT.Square, accum_out=ssq[:, i, h:h + 1]).then_inc(g_oc, 1)
                meet(act, met_at(l, "gla"))
                nc.scalar.activation(ssq[:, 0:NQ, :], ssq[:, 0:NQ, :], ACT.Sqrt, scale=1.0 / DV, bias=epst).then_inc(g_root, 1)
                for n in range(2):
                    for i in range(NQ):
                        evacuate(chunk_index(l, "g", n), i)
                for k in range(0, 8, 2):
                    act.wait_ge(g_t, 16 * l + 8 + k + 1)
                    nc.scalar.activation(glaT[:, k, 0:TQ], ps[:, 4 + k % 4, 0:TQ], ACT.Copy).then_inc(g_tc_act, 1)
                meet(act, met_at(l, "gate"))
                for j in range(2):
                    for name in ("ga", "gb"):
                        for i in range(4):
                            evacuate(chunk_index(l, name, j), i)
                meet(act, met_at(l, "merge"))
                norm(2 * l + 1, TQ, (l, 3))
                meet(act, met_at(l, "norm2"))

                act.wait_ge(r_lg, l + 1)
                nc.scalar.activation(rt[:, 64:64 + NQ * NE], ps[:, 0, 0:NQ * NE], ACT.Sigmoid).then_inc(r_aff, 1)
                for i in range(NQ):
                    act.wait_ge(r_nat, QT0[l] + i + 1)
                    b = 1 + 2 * (i % 3)
                    nc.scalar.activation(h2n[:, i, :], ps[:, b:b + 2, :].rearrange("p b n -> p (b n)"), ACT.Copy).then_inc(r_natc, 1)
                meet(act, met_at(l, "route"))

                with act.Fori(0, NE) as e:
                    b1 = act.value_load(blocks[0:1, 0, bass.ds(e, 1)], min_val=1, max_val=MAXB)
                    b0 = act.value_load(blocks[0:1, 1, bass.ds(e, 1)], min_val=0, max_val=MAXB)
                    with act.Fori(b0, b1) as b:
                        act.wait_ge(m["g_ps"], b + 1)
                        act.wait_ge(m["h_sb"], b + 1)
                        nc.scalar.activation(silu_g, ps[:, 1, :], ACT.Silu).then_inc(m["silu"], 1)
                        act.wait_ge(m["hT_ps"], b + 2)
                        act.wait_ge(m["y_ps"], b + 1)
                        nc.scalar.activation(U[:, 1, 2048:2560], ps[:, 3, :], ACT.Copy).then_inc(m["hT_sb"], 1)
                        act.wait_ge(m["y_sb"], b + 2)
                        for a in range(2):
                            act.dma_start(ybuf[bass.ds(b * BLK, BLK), 512 * a:512 * a + 512], yblk[64 * a:64 * a + 64, :]).then_inc(m["y_out"], 16)
                meet(act, met_at(l, "experts"))
                meet(act, met_at(l, "combine"))
            norm(2 * DEPTH, SEQ, None)
            for i in range(2):
                act.wait_ge(f_t, i + 1)
                nc.scalar.activation(fin[:, i, :], ps[:, 2 * i:2 * i + 2, :].rearrange("p b n -> p (b n)"), ACT.Copy).then_inc(f_c, 1)

        @block.vector
        def _(dve):
            own = [0]

            def link(ins):
                own[0] += 1
                ins.then_inc(chain["dve"], 1)
                dve.wait_ge(chain["dve"], own[0])

            def evacuate(cix, i):
                l, name, n = CHUNKS[cix]
                TQ = q_tiles(l) * P
                dve.wait_ge(acc_ready, NUMBER[cix, i])
                src = ps[:, i, :]
                if name == "nk":
                    ins = nc.vector.tensor_copy(nkT[:, i, :], src)
                elif name in ("q", "k"):
                    dst = qk[:, 0 if name == "q" else 1, i, :]
                    if i >= 2:
                        ins = nc.vector.tensor_copy(dst, src)
                    else:
                        t = rtmp.rearrange("p f (h a u e) -> p f h a u e", h=GH, a=2, u=2)
                        sv = src.rearrange("p (h a u e) -> p h a u e", h=GH, a=2, u=2)
                        dv = dst.rearrange("p (h a u e) -> p h a u e", h=GH, a=2, u=2)
                        for f in range(2):
                            for u in range(2):
                                for a in range(2):
                                    ins = nc.vector.tensor_tensor(t[:, f, :, a, u, :], sv[:, :, a, u, :],
                                                                  rope[:, f, i, a:a + 1, :].to_broadcast([P, GH, 32]), ALU.mult)
                        link(ins)
                        for a in range(2):
                            nc.vector.tensor_tensor(dv[:, :, a, 0, :], t[:, 0, :, a, 0, :], t[:, 1, :, a, 1, :], ALU.subtract)
                            ins = nc.vector.tensor_tensor(dv[:, :, a, 1, :], t[:, 1, :, a, 0, :], t[:, 0, :, a, 1, :], ALU.add)
                elif name == "bo":
                    dve.wait_ge(acc_free["act"], EVAC[chunk_index(l, "ga", n), i][1])
                    ins = nc.vector.tensor_tensor(mT[:, 4 * n + i, 0:TQ], SG[:, 0, i, 0:TQ], src[:, 0:TQ], ALU.mult)
                elif name == "bn":
                    dve.wait_ge(acc_free["act"], EVAC[chunk_index(l, "gb", n), i][1])
                    link(nc.vector.tensor_tensor(SG[:, 1, i, 0:TQ], SG[:, 1, i, 0:TQ], src[:, 0:TQ], ALU.mult))
                    ins = nc.vector.tensor_tensor(mT[:, 4 * n + i, 0:TQ], mT[:, 4 * n + i, 0:TQ], SG[:, 1, i, 0:TQ], ALU.add)
                else:
                    k = 4 * n + i
                    for s, a, b in streams(l):
                        ins = nc.vector.scalar_tensor_tensor(out=xT[:, k, a:b], in0=src[:, a:b],
                                                             scalar=mod[:, l, s, 16 + k:17 + k], in1=xT[:, k, a:b],
                                                             op0=ALU.mult, op1=ALU.add)
                ins.then_inc(acc_free["dve"], 1)

            def na_step(l, t):
                u0, units = NA0[l], na_units(l)
                if t < len(units):
                    h, s, i = units[t]
                    dve.wait_ge(na_sc, u0 + t + 1)
                    bank = ps[:, 4 + t % 2, :]
                    if s == 0:
                        link(nc.vector.tensor_tensor(bank[:, 0:SEQ], bank[:, 0:SEQ], bias[:, i, h, :], ALU.add))
                    nc.vector.tensor_reduce(st[:, t % 4, 0:1], bank[:, s * SEQ:TOK], AX, ALU.max, negate=True).then_inc(na_mx, 1)
                if 0 <= t - 1 < len(units):
                    h, s, i = units[t - 1]
                    dve.wait_ge(na_e, u0 + t)
                    link(nc.vector.reciprocal(st[:, (t - 1) % 4, 2:3], st[:, (t - 1) % 4, 1:2]))
                    p = Pb[:, (t - 1) % 2, s * SEQ:TOK]
                    nc.vector.tensor_scalar(p, p, st[:, (t - 1) % 4, 2:3], None, ALU.mult).then_inc(na_p, 1)

            def norm(n, T, scale):
                dve.wait_ge(n_root, n + 1)
                link(nc.vector.reciprocal(tmp10[:, 512:512 + T], tmp10[:, 0:T]))
                for k in range(KT):
                    for s, a, b in ((0, 0, SEQ), (1, SEQ, TOK)):
                        if a < T:
                            nc.vector.scalar_tensor_tensor(out=hT[:, k, a:b], in0=xT[:, k, a:b], scalar=scale(s, k),
                                                           in1=tmp10[:, 512 + a:512 + b], op0=ALU.mult,
                                                           op1=ALU.mult).then_inc(n_h, 1)

            link(nc.vector.memset(csil[:], 0.0))
            nc.vector.memset(up[0:32, :], 0.0).then_inc(s_zero, 1)
            dve.wait_ge(t_x, 4)
            nc.vector.tensor_copy(xT[:, 0:4, :], ps[:, 0:4, :]).then_inc(v_c, 1)
            dve.wait_ge(v_t, 1)
            nc.vector.tensor_copy(vcol[:], ps[:, 0, 0:152]).then_inc(v_c, 1)
            dve.wait_ge(v_c, 2)
            meet(dve, 3)
            for l in range(DEPTH):
                m, TQ, NQ = moe[l], q_tiles(l) * P, q_tiles(l)
                dve.wait_ge(a_col, l + 1)
                col = ps[:, 3:6, :].rearrange("p b (m s) -> p (b m) s", s=32)
                for s in range(2):
                    ins = nc.vector.tensor_tensor(mod[:, l, s, :], col[:, :, s], vcol[:, 64 * l:64 * l + 48], ALU.add)
                link(ins)
                for w in range(2):
                    for s in range(2):
                        row = (1, 4)[w] * 8
                        ins = nc.vector.scalar_tensor_tensor(out=s1[:, l, w, s, :], in0=mod[:, l, s, row:row + 8], scalar=1.0,
                                                             in1=vcol[:, 64 * l + 48 + 8 * w:64 * l + 56 + 8 * w],
                                                             op0=ALU.add, op1=ALU.mult)
                meet(dve, met_at(l, "ada"))
                norm(2 * l, TOK, lambda s, k: s1[:, l, 0, s, k:k + 1])
                meet(dve, met_at(l, "norm1"))

                nc.vector.memset(lrT[32:33, :], 1.0).then_inc(lr_one, 1)
                dve.wait_ge(s_bias, 256 * (l + 1))
                for i in range(2):
                    v = bias[:, i].rearrange("p h (r k) -> p (h r) k", r=GROWS)
                    ins = nc.vector.tensor_tensor(v, v, cmask.rearrange("p (a k) -> p a k", a=1).to_broadcast([P, NH * GROWS, GRID_W]), ALU.add)
                link(ins)
                for i in range(4):
                    evacuate(chunk_index(l, "nk"), i)
                for u in range(8):
                    d, i = u % 2, u // 2
                    dve.wait_ge(gl, 8 * l + u + 1)
                    nc.vector.scalar_tensor_tensor(out=gates[:, d, i, :], in0=ps[:, 4 + u % 2, :], scalar=0.0,
                                                   in1=gates[:, d, i, :], op0=ALU.min, op1=ALU.subtract).then_inc(gd, 1)
                for ev, a, b in mix_events(l):
                    if ev == "na":
                        na_step(l, a)
                    elif KIND[CHUNKS[a][1]][1] == "dve":
                        evacuate(a, b)
                for h in range(GH):
                    dve.wait_ge(g_t, 16 * l + GH + h + 1)
                    nc.vector.tensor_copy(qkT[:, 1, h, :], ps[:, 4 + h, :])
                meet(dve, met_at(l, "mix"))

                link(nc.vector.memset(attS, 0.0))
                for h in range(GH):
                    n = GH * l + h
                    for d in range(2):
                        dve.wait_ge(g_exp, 2 * n + d + 1)
                        e = gt[:, d, 0, :].rearrange("p (c t) -> p c t", t=CH)
                        link(nc.vector.tensor_copy(dec[:, d, :], e[:, :, CH - 1 if d == 0 else 0]))
                        nc.vector.tensor_tensor(gt[:, d, 0, 0:TQ], gt[:, d, 0, 0:TQ], qkT[:, 0, h, 0:TQ], ALU.mult)
                        nc.vector.tensor_tensor(gt[:, d, 1, 0:TQ], gt[:, d, 1, 0:TQ], qkT[:, 0, h, 0:TQ], ALU.mult)
                        nc.vector.tensor_tensor(gt[:, d, 2, :], gt[:, d, 2, :], qkT[:, 1, h, :], ALU.mult).then_inc(g_fac, 1)
                    dve.wait_ge(g_att, n + 1)
                    for d in range(2):
                        ins = nc.vector.tensor_tensor(attP[:, d, 0:NQ, :], ps[:, 6, d * 256:d * 256 + NQ * CH].rearrange("p (i t) -> p i t", t=CH),
                                                      amask[:, d:d + 1, :].to_broadcast([P, NQ, CH]), ALU.mult)
                    link(ins)
                    if h:
                        dve.wait_ge(g_o, GT0[l] + h * NQ)
                    for a in (0, CH):
                        ins = nc.vector.tensor_tensor(attS[a:a + CH, 0:NQ, a:a + CH],
                                                      attP[a:a + CH, 0, 0:NQ, :], attP[a:a + CH, 1, 0:NQ, :], ALU.add)
                    ins.then_inc(g_attm, 1)
                    for i in range(7):
                        for d in range(2):
                            dve.wait_ge(g_ds, 14 * n + 2 * i + d + 1)
                            b = ps[:, 2 * d + i % 2, 0:DV]
                            cc = scan_order(d)[i]
                            if i == 0:
                                ins = nc.vector.tensor_copy(S[:, d, 1, :], b)
                            else:
                                dve.wait_ge(g_st, 14 * n + 2 * (i - 1) + d + 1)
                                ins = nc.vector.scalar_tensor_tensor(out=S[:, d, i + 1, :], in0=S[:, d, i, :],
                                                                     scalar=dec[:, d, cc:cc + 1], in1=b, op0=ALU.mult, op1=ALU.add)
                            ins.then_inc(g_st, 1)
                meet(dve, met_at(l, "gla"))

                dve.wait_ge(g_root, l + 1)
                link(nc.vector.reciprocal(ssq[:, 0:NQ, :], ssq[:, 0:NQ, :]))
                for n in range(2):
                    for i in range(NQ):
                        t = 2 * QT0[l] + n * NQ + i
                        dve.wait_ge(acc_free["act"], EVAC[chunk_index(l, "g", n), i][1])
                        b = sg[:, t % 2, :].rearrange("p (a e) -> p a e", a=2)
                        link(nc.vector.tensor_tensor(b, b, gnw[:].rearrange("p (a e) -> p a e", a=1).to_broadcast([P, 2, DV]), ALU.mult))
                        for a in range(2):
                            h = 2 * n + a
                            o = O[:, i, h * DV:(h + 1) * DV]
                            ins = nc.vector.scalar_tensor_tensor(out=o, in0=o, scalar=ssq[:, i, h:h + 1], in1=b[:, a, :],
                                                                 op0=ALU.mult, op1=ALU.mult)
                        ins.then_inc(g_gated, 1)
                for k in range(1, 8, 2):
                    dve.wait_ge(g_t, 16 * l + 8 + k + 1)
                    nc.vector.tensor_copy(glaT[:, k, 0:TQ], ps[:, 4 + k % 4, 0:TQ]).then_inc(g_tc_dve, 1)
                meet(dve, met_at(l, "gate"))
                for j in range(2):
                    for name in ("bo", "bn"):
                        for i in range(4):
                            evacuate(chunk_index(l, name, j), i)
                for n in range(2):
                    for i in range(4):
                        evacuate(chunk_index(l, "wo", n), i)
                meet(dve, met_at(l, "merge"))
                norm(2 * l + 1, TQ, lambda s, k: s1[:, l, 1, s, k:k + 1])
                meet(dve, met_at(l, "norm2"))

                def R(a, n, split=None):
                    v = rt[:, a:a + n]
                    return v if split is None else v.rearrange("p (i e) -> p i e", e=split)

                def over(v, e):
                    return v.rearrange("p (n a) -> p n a", a=1).to_broadcast([P, v.shape[1], e])

                N = NQ * NE
                M, aff, sel = R(0, N, NE), R(64, N, NE), R(128, N, NE)
                dve.wait_ge(s_rw, 32)
                dve.wait_ge(r_aff, l + 1)
                link(nc.vector.tensor_tensor(sel, aff, br[:].rearrange("p (a e) -> p a e", a=1).to_broadcast([P, NQ, NE]), ALU.add))
                s4, pairs = R(128, N, EPG), R(192, NQ * NG * 6, 6)
                nc.vector.tensor_tensor(pairs[:, :, 0:3], s4[:, :, 0:3], s4[:, :, 1:4], ALU.add)
                nc.vector.tensor_tensor(pairs[:, :, 3:5], s4[:, :, 0:2], s4[:, :, 2:4], ALU.add)
                link(nc.vector.tensor_tensor(pairs[:, :, 5:6], s4[:, :, 0:1], s4[:, :, 3:4], ALU.add))
                gsc = R(288, NQ * NG)
                link(nc.vector.tensor_reduce(gsc, pairs, AX, ALU.max))

                def first_max(dst, v, e, top, wt):
                    link(nc.vector.tensor_reduce(top, v, AX, ALU.max))
                    link(nc.vector.tensor_tensor(wt, v, over(top, e), ALU.is_equal))
                    link(nc.vector.tensor_tensor(wt, wt, ramp[:, 16 - e:16].rearrange("p (a e) -> p a e", a=1).to_broadcast([P, NQ, e]), ALU.mult))
                    link(nc.vector.tensor_reduce(top, wt, AX, ALU.max))
                    link(nc.vector.tensor_tensor(dst, wt, over(top, e), ALU.is_equal))

                ing = R(312, NQ * NG)
                first_max(R(312, NQ * NG, NG), R(288, NQ * NG, NG), NG, R(304, NQ), R(328, NQ * NG, NG))
                link(nc.vector.tensor_scalar(ing, ing, BIG, -BIG, ALU.mult, ALU.add))
                selm = R(352, N, NE)
                link(nc.vector.tensor_tensor(R(352, N, EPG), s4, over(ing, EPG), ALU.add))
                oh1, sel2, oh2, t = R(496, N, NE), R(560, N, NE), R(640, N, NE), R(704, N, NE)
                first_max(oh1, selm, NE, R(416, NQ), R(424, N, NE))
                link(nc.vector.scalar_tensor_tensor(out=sel2, in0=oh1, scalar=-2 * BIG, in1=selm, op0=ALU.mult, op1=ALU.add))
                first_max(oh2, sel2, NE, R(624, NQ), R(424, N, NE))
                nc.vector.tensor_tensor(M, oh1, oh2, ALU.add).then_inc(r_sel, 1)
                a1, a2, den = R(768, NQ), R(772, NQ), R(776, NQ)
                for oh, a in ((oh1, a1), (oh2, a2)):
                    link(nc.vector.tensor_tensor(t, oh, aff, ALU.mult))
                    link(nc.vector.tensor_reduce(a, t, AX, ALU.add))
                link(nc.vector.tensor_tensor(den, a1, a2, ALU.add))
                link(nc.vector.reciprocal(den, den))
                nc.vector.tensor_tensor(wsel[:, 0:NQ, 0], a1, den, ALU.mult)
                nc.vector.tensor_tensor(wsel[:, 0:NQ, 1], a2, den, ALU.mult)
                dve.wait_ge(r_rank, l + 1)
                cnt, nbf, inc, base, pos = R(780, NE), R(796, NE), R(812, NE), R(828, NE), R(848, N, NE)
                ci = cnt.bitcast(I32)
                link(nc.vector.tensor_scalar(ci, ps[:, 7, 64:64 + NE], float(BLK - 1), None, ALU.add))
                link(nc.vector.tensor_scalar(ci, ci, BLK.bit_length() - 1, None, ALU.arith_shift_right))
                link(nc.vector.tensor_scalar(nbf, ci, 1.0, None, ALU.max))
                link(nc.vector.tensor_tensor_scan(inc, ones[:, 0:NE], nbf, 0.0, ALU.mult, ALU.add))
                link(nc.vector.tensor_tensor(base, inc, nbf, ALU.subtract))
                nc.vector.tensor_copy(blocks[:, 0, :], inc)
                nc.vector.tensor_copy(blocks[:, 1, :], base)
                link(nc.vector.tensor_scalar(base, base, float(BLK), None, ALU.mult))
                link(nc.vector.tensor_tensor(pos, ps[:, 7, 0:N].rearrange("p (i e) -> p i e", e=NE),
                                             base.rearrange("p (a e) -> p a e", a=1).to_broadcast([P, NQ, NE]), ALU.add))
                for c_, oh in enumerate((oh1, oh2)):
                    link(nc.vector.tensor_tensor(t, oh, pos, ALU.mult))
                    link(nc.vector.tensor_reduce(R(912 + 4 * c_, NQ), t, AX, ALU.add))
                    ins = nc.vector.tensor_copy(slot[:, 0:NQ, c_], R(912 + 4 * c_, NQ))
                ins.then_inc(r_slot, 1)
                meet(dve, met_at(l, "route"))

                dve.wait_ge(m["xT_ps"], 1)
                nc.vector.tensor_copy(xbT_flat, ps[:, 0, :]).then_inc(m["xT_sb"], 1)
                with dve.Fori(0, NE) as e:
                    b1 = dve.value_load(blocks[0:1, 0, bass.ds(e, 1)], min_val=1, max_val=MAXB)
                    b0 = dve.value_load(blocks[0:1, 1, bass.ds(e, 1)], min_val=0, max_val=MAXB)
                    with dve.Fori(b0, b1) as b:
                        dve.wait_ge(m["silu"], b + 1)
                        dve.wait_ge(m["u_ps"], b + 1)
                        dve.wait_ge(m["hT_ps"], b + 1)
                        nc.vector.tensor_tensor(hblk, silu_g, ps[:, 2, :], ALU.mult).then_inc(m["h_sb"], 1)
                        dve.wait_ge(m["xT_ps"], b + 2)
                        nc.vector.tensor_copy(xbT_flat, ps[:, 0, :]).then_inc(m["xT_sb"], 1)
                        dve.wait_ge(m["y_ps"], b + 2)
                        dve.wait_ge(m["y_out"], 32 * b + 32)
                        nc.vector.tensor_copy(yblk, ps[:, 4, :]).then_inc(m["y_sb"], 1)
                meet(dve, met_at(l, "experts"))

                dve.wait_ge(s_gather, 32 * (QT0[l] + NQ))
                for i in range(NQ):
                    link(nc.vector.tensor_scalar(z[:, i, :], yg[:, 2 * i, :], wsel[:, i, 0:1], None, ALU.mult))
                    nc.vector.scalar_tensor_tensor(out=z[:, i, :], in0=yg[:, 2 * i + 1, :], scalar=wsel[:, i, 1:2],
                                                   in1=z[:, i, :], op0=ALU.mult, op1=ALU.add).then_inc(c_z, 1)
                for k in range(KT):
                    dve.wait_ge(c_t, KT * l + k + 1)
                    for s, a, b in streams(l):
                        nc.vector.scalar_tensor_tensor(out=xT[:, k, a:b], in0=ps[:, k, a:b], scalar=mod[:, l, s, 40 + k:41 + k],
                                                       in1=xT[:, k, a:b], op0=ALU.mult, op1=ALU.add)
                meet(dve, met_at(l, "combine"))
            norm(2 * DEPTH, SEQ, lambda s, k: vcol[:, 128 + k:129 + k])

        @block.gpsimd
        def _(pool):
            nc.gpsimd.memset(zero, 0.0).then_inc(chain["pool"], 1)
            pool.wait_ge(chain["pool"], 1)
            pool.dma_start(rp.rearrange("l h r w -> (l h r) w").rearrange("(a b) w -> a (b w)", b=2), zero[0:120, 0:2 * RPAD]).then_inc(s_rpz, 16)
            pool.wait_ge(s_rpz, 16)
            for l in range(DEPTH):
                pool.dma_start(rp[l, :, :, GRID_W - WIN_C:GRID_W + WIN_C - 1].rearrange("h r w -> (h r) w"),
                               rpb[l].rearrange("h r w -> (h r) w")).then_inc(s_rp, 16)
            pool.wait_ge(s_rp, 32)
            for l in range(DEPTH):
                src = rp[l, :, WIN_R - GROWS:WIN_R + GROWS - 1, :].rearrange("h r w -> h (r w)").rearrange("(a h) n -> a h n", a=1)
                pool.dma_start(rx[l].rearrange("c h r w -> c h (r w)"), src.to_broadcast([GRID_W, NH, RW * RPAD])).then_inc(s_rx, 16)
            with pool.Fori(0, XROWS // P) as r:
                pool.dma_start(xbuf[bass.ds(r * P, P), :], zero).then_inc(s_zfill, 16)
            with pool.Fori(0, MAXB * BLK // P) as r:
                pool.dma_start(ybuf[bass.ds(r * P, P), :], zero).then_inc(s_zfill, 16)
            pool.wait_ge(s_zfill, ZFILLS)
            for l in range(DEPTH):
                m, NQ = moe[l], q_tiles(l)
                pool.wait_ge(r_slot, l + 1)
                pool.wait_ge(r_natc, QT0[l] + NQ)
                for i in range(NQ):
                    for c_ in range(2):
                        pool.indirect_dma_start(xbuf, bass.IndirectOffsetOnAxis(slot[:, i, c_:c_ + 1], 0), h2n[:, i, :], None,
                                                ).then_inc(m["scattered"], 16)
                pool.wait_ge(met, met_at(l, "route"))
                pool.wait_ge(m["scattered"], 32 * NQ)

                def load_x(b):
                    for a in range(2):
                        pool.dma_start(xblk[64 * a:64 * a + 64, :], xbuf[bass.ds(b * BLK, BLK), 512 * a:512 * a + 512]).then_inc(m["x_in"], 16)

                load_x(0)
                pool.wait_ge(m["xT_ps"], 1)
                load_x(1)
                with pool.Fori(0, NE) as e:
                    b1 = pool.value_load(blocks[0:1, 0, bass.ds(e, 1)], min_val=1, max_val=MAXB)
                    b0 = pool.value_load(blocks[0:1, 1, bass.ds(e, 1)], min_val=0, max_val=MAXB)
                    with pool.Fori(b0, b1) as b:
                        pool.wait_ge(m["xT_ps"], b + 2)
                        load_x(b + 2)
                total = pool.value_load(blocks[0:1, 0, NE - 1:NE], min_val=1, max_val=MAXB)
                pool.wait_ge(m["y_out"], 32 * total + 32)
                pool.wait_ge(m["x_in"], 32 * total + 64)
                nc.gpsimd.tensor_tensor(waited[:, l:l + 1], ones[0:1, 0:1], ones[0:1, 0:1], ALU.mult)
                pool.wait_ge(met, met_at(l, "experts"))
                for i in range(NQ):
                    for c_ in range(2):
                        pool.indirect_dma_start(yg[:, 2 * i + c_, :], None, ybuf, bass.IndirectOffsetOnAxis(slot[:, i, c_:c_ + 1], 0),
                                                ).then_inc(s_gather, 16)


def constants():
    k = np.zeros((P, 1361), np.float32)
    p, t = np.arange(P)[:, None], np.arange(P)[None, :]
    same = p // CH == t // CH
    k[:, 0:128] = p == t
    k[:, 128:256] = 1.0
    k[:, 256:384] = same & (p <= t)
    k[:, 384:512] = same & (p > t)
    k[:, 512:640] = same & (p >= t)
    k[:, 640:768] = same & (p < t)
    t64 = np.arange(CH)[None, :]
    k[:, 768:832] = p % CH <= t64
    k[:, 832:896] = p % CH >= t64
    k[:, 896:1024] = p < t
    half = DK // 2
    inv = np.float32(10000.0) ** (-np.arange(0, half, 2, dtype=np.float32) / np.float32(half))
    for i in range(2):
        tok = i * P + np.arange(P)
        for a, pos in enumerate((tok // GRID_W, tok % GRID_W)):
            ang = pos.astype(np.float32)[:, None] * inv[None, :]
            for f, fn in enumerate((np.cos, np.sin)):
                o = 1024 + ((f * 2 + i) * 2 + a) * 32
                k[:, o:o + 32] = fn(ang)
    col = np.arange(P)[:, None] % GRID_W
    c0 = np.clip(col - WIN_C // 2, 0, GRID_W - WIN_C)
    kc = np.arange(GRID_W)[None, :]
    k[:, 1280:1344] = np.where((kc >= c0) & (kc < c0 + WIN_C), 0.0, -BIG)
    k[:, 1344:1360] = np.arange(16, 0, -1)
    k[:, 1360] = EPS
    return k


_INS = ['x', 'c', 'ctx', 'c_ctx', 'w_ada', 'b_ada', 'norm1_w', 'norm2_w', 'w_in', 'w_gk_up', 'b_gk', 'gla_norm_w', 'rpb',
        'w_bo_gla', 'w_bo_na', 'w_out', 'w_router', 'b_router', 'w1', 'w3', 'w2', 'final_norm_w']


def kernel(**inputs):
    import numpy as _np
    import concourse.bacc as _bacc
    from concourse import mybir as _mybir
    from concourse.bass_utils import run_bass_kernel_spmd as _run

    nc = _bacc.Bacc("TRN2", target_bir_lowering=False, num_devices=1)
    arrays, args = {}, []
    for name in _INS + ["consts"]:
        a = constants() if name == "consts" else _np.ascontiguousarray(inputs[name])
        arrays[f"in_{name}"] = a
        args.append(nc.dram_tensor(f"in_{name}", a.shape, _mybir.dt.from_np(a.dtype), kind="ExternalInput").ap())
    args.append(nc.dram_tensor("out_0", (1, SEQ, D), _mybir.dt.float32, kind="ExternalOutput").ap())
    build(nc, *args)
    return _run(nc, [arrays], core_ids=[0]).results[0]["out_0"]
```

```python
from contextlib import ExitStack

import concourse.bass as bass
import numpy as np
from concourse import mybir

P = 128
D = 1024
KT = D // P
SEQ, CTX = 256, 256
TOK = SEQ + CTX
DEPTH = 2
GRID_W = 64
GROWS = SEQ // GRID_W
EPS = 1e-6
GH, DK, DV, LR = 4, 128, 256, 16
TAU = 16.0
CH = 64
NCH = TOK // CH
NH, HD = 8, 64
WIN_R, WIN_C = 8, 16
NE, NG, EPG = 16, 4, 4
FF = 1024
BLK = 64
MAXB = TOK * 2 // BLK + NE
XROWS = (MAXB + 2) * BLK
RPAD = 128
F32 = mybir.dt.float32
I32 = mybir.dt.int32
ALU = mybir.AluOpType
ACT = mybir.ActivationFunctionType
AX = mybir.AxisListType.X
BIG = 1e30

C_Q, C_K, C_V, C_G, C_LR = 0, 512, 1024, 2048, 3072
C_NQ, C_NK, C_NV, C_GA, C_GB = 3104, 3616, 4128, 4640, 5664


def weight_chunks():
    out = []
    for l in range(DEPTH):
        if l == 0:
            out += [(l, "ada", n) for n in range(4)]
        out += [(l, n, 0) for n in ("nq", "nk", "nv", "lr", "q", "k")] + [(l, "v", 0), (l, "v", 1)]
        out += [(l, "g", 0), (l, "g", 1)]
        for j in range(2):
            out += [(l, n, j) for n in ("ga", "bo", "gb", "bn")]
        out += [(l, "wo", 0), (l, "wo", 1)]
    return out


KIND = {"nq": (True, "act"), "nk": (True, "dve"), "nv": (False, "act"), "q": (False, "dve"), "k": (False, "dve"),
        "v": (False, "act"), "g": (False, "act"), "ga": (True, "act"), "bo": (True, "dve"), "gb": (True, "act"),
        "bn": (True, "dve"), "wo": (True, "dve")}


def q_tiles(l):
    return 4 if l < DEPTH - 1 else 2


def gemm_tiles(l, name):
    if KIND[name][0]:
        return 4
    return q_tiles(l) if name in ("q", "g") else 4


def jobs(l):
    ada = [(0, n) for n in range(4, 12)] + [(1, n) for n in range(4)] if l == 0 else [(1, n) for n in range(4, 12)]
    places = [(n, i) for n in ("nq", "nk", "nv") for i in (1, 3)]
    places += [("q", i) for i in range(gemm_tiles(l, "q"))] + [("k", i) for i in range(2)]
    out = {p: [("ada",) + a] for p, a in zip(places, ada)}
    for i, (al, n) in enumerate(ada[::4]):
        out.setdefault(("k", 1 + i), []).append(("col", al, n // 4))
    return out


def job_number(job):
    l, n = job[1:]
    return (n - 4 if l == 0 else 8 + n), (n - 4 if l == 0 else 8 + n if n < 4 else n - 4)


def bank_users(chunks):
    out = []
    for c, (l, name, n) in enumerate(chunks):
        if name in KIND:
            for i in range(gemm_tiles(l, name)):
                out.append(((c, i), i, KIND[name][1]))
                if n == 0:
                    out += [(job, (i + 2) % 4, "act" if job[0] == "ada" else "dve") for job in jobs(l).get((name, i), [])]
    return out


def bank_tables(chunks):
    count, evac, last, before, number, banks = {"act": 0, "dve": 0}, {}, {}, {}, {}, {}
    for n, (key, bank, e) in enumerate(bank_users(chunks)):
        count[e] += 1
        evac[key], before[key], number[key] = (e, count[e]), last.get(bank), n + 1
        last[bank], banks[key] = key, bank
    return evac, before, number, banks


def build(nc, x, c, ctx, c_ctx, w_ada, b_ada, norm1_w, norm2_w, w_in, w_gk_up, b_gk, gla_norm_w, rpb,
          w_bo_gla, w_bo_na, w_out, w_router, b_router, w1, w3, w2, final_norm_w, consts, out):
    CHUNKS = weight_chunks()
    EVAC, BEFORE, NUMBER, BANK = bank_tables(CHUNKS)
    RING = 2

    with ExitStack() as cm:
        def sb(name, shape, dt=F32):
            return cm.enter_context(nc.sbuf_tensor(name, shape, dt))

        def sem(name):
            return cm.enter_context(nc.semaphore(name))

        U = sb("units", [P, 12, 4096])
        xT = U[:, 0, :].rearrange("p (k t) -> p k t", k=KT)
        hT = U[:, 1, :].rearrange("p (k t) -> p k t", k=KT)
        ring = [U[:, 2 + r, :].rearrange("p (k n) -> p k n", k=8) for r in range(RING)]
        nqT = U[:, 4, 0:2048].rearrange("p (j t) -> p j t", j=4)
        nkT = U[:, 4, 2048:4096].rearrange("p (j t) -> p j t", j=4)
        O = U[:, 4, :].rearrange("p (i n) -> p i n", i=4)
        qk = U[:, 5, :].rearrange("p (a i n) -> p a i n", a=2, i=4)
        qkT = U[:, 6, :].rearrange("p (a h t) -> p a h t", a=2, h=GH)
        V = U[:, 7, :].rearrange("p (i n) -> p i n", i=4)
        gates = U[:, 8, :].rearrange("p (d i n) -> p d i n", d=2, i=4)
        glaT = U[:, 8, :].rearrange("p (k t) -> p k t", k=8)
        Pb = U[:, 9, 0:1024].rearrange("p (b n) -> p b n", b=2)
        PT = U[:, 9, 1024:3072].rearrange("p (b j q) -> p b j q", b=2, j=4)
        rtmp = U[:, 9, 3072:4096].rearrange("p (f n) -> p f n", f=2)
        S = U[:, 9, :].rearrange("p (d s e) -> p d s e", d=2, s=8)
        mT = U[:, 9, :].rearrange("p (k t) -> p k t", k=8)
        nv = U[:, 10, 0:2048].rearrange("p (i n) -> p i n", i=4)
        naT = U[:, 10, 2048:4096].rearrange("p (j t) -> p j t", j=4)
        tmp10 = U[:, 10, 0:2048]
        rt = U[:, 10, 0:1024]
        affT = U[:, 10, 2048:2176]
        attP = tmp10[:, 0:512].rearrange("p (d i t) -> p d i t", d=2, i=4)
        attS = tmp10[:, 512:1024].rearrange("p (i t) -> p i t", i=4)
        junk = tmp10[:, 1024:1280]
        sg = tmp10[:, 0:1024].rearrange("p (b n) -> p b n", b=2)
        SG = U[:, 11, :].rearrange("p (a i t) -> p a i t", a=2, i=4)
        zero = U[:, 7, 1536:2560]
        bias = U[:, 11, :].rearrange("p (i h k) -> p i h k", i=2, h=NH)
        gt = U[:, 11, :].rearrange("p (d a t) -> p d a t", d=2, a=4)
        h2n = U[:, 11, :].rearrange("p (i n) -> p i n", i=4)
        xload = U[:, 5, :].rearrange("p (i n) -> p i n", i=4)
        adarow = U[:, 7, 0:1536]
        wada = U[:, 6, :].rearrange("p (k n) -> p k n", k=8)
        W1 = [U[:, 4:6, :].rearrange("p a (k n) -> p (a k) n", k=4), U[:, 8:10, :].rearrange("p a (k n) -> p (a k) n", k=4)]
        W3 = [U[:, 6:8, :].rearrange("p a (k n) -> p (a k) n", k=4), U[:, 10:12, :].rearrange("p a (k n) -> p (a k) n", k=4)]
        W2 = U[:, 2:4, :].rearrange("p a (k n) -> p (a k) n", k=4)
        xblk = U[:, 1, 0:512]
        xbT = U[:, 1, 512:1024].rearrange("p (c a s) -> p c a s", c=4, a=2)
        xbT_flat = U[:, 1, 512:1024]
        silu_g = U[:, 1, 1024:1536]
        hblk = U[:, 1, 1536:2048]
        hbT = U[:, 1, 2048:2560].rearrange("p (c a s) -> p c a s", c=4, a=2)
        yblk = U[:, 1, 2560:3072]
        yg = U[:, 4:6, :].rearrange("p a (b n) -> p (a b) n", b=4)
        z = U[:, 6, :].rearrange("p (i n) -> p i n", i=4)
        fin = U[:, 7, :].rearrange("p (i n) -> p i n", i=4)

        K = sb("constants", [P, 1361])
        ident = K[:, 0:128]
        ones = K[:, 128:256]
        cum = K[:, 256:768].rearrange("p (d a t) -> p d a t", d=2, a=2)
        amask = K[:, 768:896].rearrange("p (d t) -> p d t", d=2)
        strict = K[:, 896:1024]
        rope = K[:, 1024:1280].rearrange("p (f i a e) -> p f i a e", f=2, i=2, a=2)
        cmask = K[:, 1280:1344]
        ramp = K[:, 1344:1360]
        epst = K[:, 1360:1361]
        vrow = U[:, 11, 0:256].rearrange("p (a n) -> p a n", a=2)
        vcol = sb("vector_columns", [P, 128 + 24])
        csil = sb("silu_c", [P, KT, 32])
        mod = sb("modulations", [P, DEPTH, 2, 48])
        s1 = sb("norm_scales", [P, DEPTH, 2, 2, KT])
        lrn = U[:, 9, 3072:3200].rearrange("p (i e) -> p i e", i=4)
        lrT = U[0:33, 9, 2048:2560]
        up = sb("gate_up", [33, 2 * 512])
        gnw = sb("gla_norm_w", [P, DV])
        wr = sb("router_w", [P, KT, NE])
        br = sb("router_b", [P, NE])
        dec = sb("chunk_decays", [P, 2, NCH])
        ssq = sb("head_squares", [P, 4, GH])
        st = sb("softmax_stats", [P, 4, 4])
        wsel = sb("choice_weights", [P, 4, 2])
        waited = sb("waited", [1, DEPTH])
        slot = sb("choice_slots", [P, 4, 2], I32)
        blocks = sb("expert_blocks", [P, 2, NE], I32)

        ps = cm.enter_context(nc.psum_tensor("ps", [P, 8, 512], F32))

        rp = nc.dram_tensor("bias_padded", [DEPTH, NH, 15, RPAD], F32, kind="Internal").ap()
        RW = 2 * GROWS - 1
        rx = nc.dram_tensor("bias_copies", [DEPTH, GRID_W, NH, RW, RPAD], F32, kind="Internal").ap()
        xbuf = nc.dram_tensor("dispatched", [XROWS, D], F32, kind="Internal").ap()
        ybuf = nc.dram_tensor("expert_out", [MAXB * BLK, D], F32, kind="Internal").ap()


        met = sem("compute_engines_met")
        s_const = sem("constants_in")
        s_vec = sem("vectors_in")
        s_x = sem("tokens_in")
        s_rw = sem("router_weights_in")
        s_zero = sem("zeros_made")
        s_zfill = sem("scratch_zeroed")
        s_rp = sem("bias_table_in")
        s_bias = sem("bias_in")
        s_par = sem("layer_vectors_in")
        s_w = [sem(f"weights_in_{r}") for r in range(RING)]
        s_wused = sem("chunk_used")
        s_ada = sem("ada_chunk_in")
        acc_ready = sem("acc_ready")
        acc_free = {"act": sem("acc_emptied_act"), "dve": sem("acc_emptied_dve")}
        chain = {e: sem("own_steps_" + e) for e in ("act", "dve", "pool")}
        lr_one = sem("lr_ones_row")
        t_x, v_t, v_c = sem("tokens_turned"), sem("vectors_turned"), sem("vectors_copied")
        s_rpz, s_rx = sem("bias_table_zeroed"), sem("bias_copies_made")
        a_row, a_sb, a_col = sem("ada_rows"), sem("ada_rows_copied"), sem("ada_columns")
        n_sq, n_sum, n_root, n_h, n_sh = (sem("norm_" + n) for n in ("squares", "sums", "root", "scaled", "shifted"))
        lr_ps, lr_sb, lr_tp, lr_T, gz, gl, gd = (sem(n) for n in (
            "lr_products", "lr_copied", "lr_turned", "lrT_copied", "gate_products", "gate_logs", "gates_made"))
        b_m = sem("bias_masked")
        na_sc, na_mx, na_e, na_p, na_tp, na_tc, na_o, na_oc = (sem(n) for n in (
            "na_scores", "na_max", "na_exp", "na_probs", "na_turned", "na_turned_copied", "na_out", "na_out_copied"))
        g_cum, g_exp, g_fac, g_kt, g_ktc, g_att, g_attm, g_ds, g_st, g_o, g_oc = (sem("gla_" + n) for n in (
            "sums", "exps", "factors", "kdecT", "kdec_copied", "att", "att_masked", "delta", "state", "out", "out_copied"))
        g_root, g_gated, g_t, g_tc_act, g_tc_dve = (sem("gla_" + n) for n in (
            "root", "gated", "out_turned", "turned_copied_act", "turned_copied_dve"))
        r_lg, r_aff, r_aT, r_nat, r_natc, r_sel, r_rank, r_slot = (sem("route_" + n) for n in (
            "logits", "affinities", "affinities_turned", "turned", "copied", "selection", "ranks", "slots"))
        moe = [{n: sem(f"{n}_{l}") for n in (
            "x_in", "xT_ps", "xT_sb", "g_ps", "u_ps", "silu", "h_sb", "hT_ps", "hT_sb", "y_ps", "y_sb", "y_out",
            "w1_in0", "w1_in1", "w3_in0", "w3_in1", "w2_in", "scattered")} for l in range(DEPTH)]
        AHEAD = {"h_sb": 1, "hT_ps": 1, "y_ps": 1, "y_sb": 1, "y_out": 32}
        s_gather = [sem(f"gathered_{i}") for i in range(4)]
        c_z, c_t = sem("combined"), sem("combined_turned")
        f_t, f_c, s_out = sem("final_turned"), sem("final_copied"), sem("stored")

        STAGES = ("mix", "gla", "gate", "merge", "route", "experts", "combine")
        TOKENS_MET, MODS_MET = 3, 6

        def met_at(l, stage):
            return MODS_MET + 3 * (1 + len(STAGES) * l + STAGES.index(stage))

        def meet(eng, value):
            eng.drain().then_inc(met, 1)
            eng.wait_ge(met, value)

        def chunk_source(l, name, n):
            k8 = "(k p) n -> p k n"
            cols = slice(n * 512, (n + 1) * 512)
            if name == "ada":
                return w_ada[l][:, cols].rearrange(k8, p=P)
            if name == "bo":
                return w_bo_gla[l][:, cols].rearrange(k8, p=P)
            if name == "bn":
                return w_bo_na[l][:, cols].rearrange(k8, p=P)
            if name == "wo":
                return w_out[l][:, cols].rearrange(k8, p=P)
            c0 = {"nq": C_NQ, "nk": C_NK, "nv": C_NV, "q": C_Q, "k": C_K, "lr": C_LR, "v": C_V, "g": C_G,
                  "ga": C_GA, "gb": C_GB}[name] + n * 512
            return w_in[l][:, c0:c0 + (32 if name == "lr" else 512)].rearrange(k8, p=P)

        def chunk_view(cix):
            name, r = CHUNKS[cix][1], ring[cix % RING]
            return r[:, 0:4, :] if name == "bn" else r[:, :, 0:32] if name == "lr" else r

        def chunk_index(l, name, n=0):
            return CHUNKS.index((l, name, n))

        def used(cix):
            l, name, _ = CHUNKS[cix]
            if name in KIND:
                return acc_ready, NUMBER[cix, gemm_tiles(l, name) - 1]
            return s_wused, sum(CHUNKS[k][1] not in KIND for k in range(cix + 1))

        def scan_order(d):
            return [4, 5, 6, 7, 0, 1, 2, 3] if d == 0 else [7, 6, 5, 4, 3, 2, 1, 0]

        def streams(l):
            return [(0, 0, SEQ), (1, SEQ, TOK)][:q_tiles(l) // 2]

        def na_units(l):
            return [(h, s, i) for h in range(NH) for s in range(q_tiles(l) // 2) for i in range(2)]

        NA0 = [0, len(na_units(0))]
        GT0 = [0, GH * q_tiles(0)]
        NH0 = [0, 16, 32, 48, 56]
        QT0 = [0, q_tiles(0)]

        def mix_events(l):
            tiles = [(chunk_index(l, n, j), i) for n, j in (("q", 0), ("k", 0), ("v", 0), ("v", 1))
                     for i in range(gemm_tiles(l, n))]
            steps, ev, t = len(na_units(l)) + 3, [], 0
            for n, tile in enumerate(tiles):
                ev.append(("tile",) + tile)
                if CHUNKS[tile[0]][2] == 0:
                    ev += jobs(l).get((CHUNKS[tile[0]][1], tile[1]), [])
                while t < steps * (n + 1) // len(tiles):
                    ev.append(("na", t, 0))
                    t += 1
            return ev

        ZFILLS = 16 * ((XROWS + MAXB * BLK) // P)

        block = cm.enter_context(nc.Block())

        @block.sync
        def _(sp):
            sp.dma_start(K[:], consts).then_inc(s_const, 16)
            for l in range(DEPTH):
                for src, r0, r1 in ((b_ada, 0, 48), (norm1_w, 48, 56), (norm2_w, 56, 64)):
                    sp.dma_start(vrow[64 * l + r0:64 * l + r1, 0, :], src[l].rearrange("(m p) -> m p", p=P)).then_inc(s_vec, 16)
            for src, r0 in ((final_norm_w, 0), (c[0], 8), (c_ctx, 16)):
                sp.dma_start(vrow[r0:r0 + 8, 1, :], src.rearrange("(m p) -> m p", p=P)).then_inc(s_vec, 16)
            sp.dma_start(xload[:, 0:2, :], x[0].rearrange("(i p) n -> p i n", p=P)).then_inc(s_x, 16)
            sp.dma_start(xload[:, 2:4, :], ctx[0].rearrange("(i p) n -> p i n", p=P)).then_inc(s_x, 16)
            def load_chunk(cix):
                if cix >= RING:
                    sp.wait_ge(*used(cix - RING))
                sp.dma_start(chunk_view(cix), chunk_source(*CHUNKS[cix])).then_inc(s_w[cix % RING], 16)

            def load_expert(l, e, which, buf, name):
                w = {"w1": w1, "w3": w3, "w2": w2}[which][l]
                src = w[bass.ds(e, 1)].rearrange("a (k p) n -> p (a k) n", p=P)
                sp.dma_start(buf, src).then_inc(moe[l][name], 16)

            for l in range(DEPTH):
                if l:
                    sp.wait_ge(met, met_at(l - 1, "experts"))
                    for i in range(q_tiles(l - 1)):
                        sp.wait_ge(s_gather[i], 32 * l)
                first = 0 if l == 0 else chunk_index(l, "nq")
                for cix in range(first, chunk_index(l, "wo", 1) + 1):
                    load_chunk(cix)
                    if (l, CHUNKS[cix][1]) == (0, "nq"):
                        sp.dma_start(wr[:], w_router.rearrange("(k p) e -> p k e", p=P)).then_inc(s_rw, 16)
                        sp.dma_start(br[:], b_router.rearrange("(a e) -> a e", a=1).to_broadcast([P, NE])).then_inc(s_rw, 16)
                    if CHUNKS[cix][1] == "gb":
                        sp.wait_ge(met, met_at(l, "gate"))
                        if CHUNKS[cix][2] == 0:
                            load_expert(l, 0, "w1", W1[0], "w1_in0")
                        else:
                            load_expert(l, 0, "w3", W3[0], "w3_in0")
                    if CHUNKS[cix][1] == "nk":
                        if l == 0:
                            sp.wait_ge(met, TOKENS_MET)
                            sp.wait_ge(s_rx, 32)
                        for r in range(GROWS):
                            for kr in range(GROWS):
                                src = bass.AP(tensor=rx.tensor,
                                              offset=(l * GRID_W * NH * RW + GROWS - 1 - r + kr) * RPAD + GRID_W - 1,
                                              ap=[[NH * RW * RPAD - 1, GRID_W], [RW * RPAD, NH], [1, GRID_W]])
                                sp.dma_start(bias[r % 2 * 64:r % 2 * 64 + 64, r // 2, :, kr * GRID_W:(kr + 1) * GRID_W],
                                             src).then_inc(s_bias, 16)
                        if l:
                            sp.wait_ge(met, met_at(0, "gate"))
                        sp.wait_ge(s_zero, 1)
                        for d in range(2):
                            sp.dma_start(up[16 * d:16 * d + 16, 512 * d:512 * d + 512], w_gk_up[l, d]).then_inc(s_par, 16)
                        sp.dma_start(up[32:33, :], b_gk[l].rearrange("(a d) n -> a (d n)", a=1)).then_inc(s_par, 16)
                        sp.dma_start(gnw[:], gla_norm_w[l].rearrange("(a e) -> a e", a=1).to_broadcast([P, DV])).then_inc(s_par, 16)
                m = moe[l]
                sp.wait_ge(met, met_at(l, "merge"))
                load_expert(l, 0, "w2", W2, "w2_in")
                load_expert(l, 1, "w1", W1[1], "w1_in1")
                sp.wait_ge(met, met_at(l, "route"))
                sp.wait_ge(m["scattered"], 16 * 2 * q_tiles(l))
                sp.wait_ge(m["xT_ps"], 1)
                load_expert(l, 1, "w3", W3[1], "w3_in1")
                with sp.Fori(0, NE // 2 - 1) as p:
                    b1 = sp.value_load(blocks[0:1, 1, bass.ds(2 * p + 1, 1)], min_val=1, max_val=MAXB)
                    sp.wait_ge(m["g_ps"], b1)
                    load_expert(l, 2 * p + 2, "w1", W1[0], "w1_in0")
                    sp.wait_ge(m["y_ps"], b1 + 1)
                    load_expert(l, 2 * p + 1, "w2", W2, "w2_in")
                    load_expert(l, 2 * p + 2, "w3", W3[0], "w3_in0")
                    b2 = sp.value_load(blocks[0:1, 1, bass.ds(2 * p + 2, 1)], min_val=1, max_val=MAXB)
                    sp.wait_ge(m["g_ps"], b2)
                    load_expert(l, 2 * p + 3, "w1", W1[1], "w1_in1")
                    sp.wait_ge(m["y_ps"], b2 + 1)
                    load_expert(l, 2 * p + 2, "w2", W2, "w2_in")
                    load_expert(l, 2 * p + 3, "w3", W3[1], "w3_in1")
                b1 = sp.value_load(blocks[0:1, 1, NE - 1:NE], min_val=1, max_val=MAXB)
                sp.wait_ge(m["y_ps"], b1 + 1)
                load_expert(l, NE - 1, "w2", W2, "w2_in")
            sp.wait_ge(f_c, 2)
            sp.dma_start(out[0].rearrange("(i p) n -> p i n", p=P), fin[:, 0:2, :]).then_inc(s_out, 16)
            sp.wait_ge(s_out, 16)

        @block.tensor
        def _(pe):
            def turn(dst, src, n=P):
                return nc.tensor.transpose(dst, src, ident[0:n, 0:n])

            def gemm_tile(cix, i):
                l, name, n = CHUNKS[cix]
                w, TQ = chunk_view(cix), q_tiles(l) * P
                if i == 0:
                    pe.wait_ge(s_w[cix % RING], 16 * (cix // RING + 1))
                if BEFORE[cix, i] is not None:
                    e, cnt = EVAC[BEFORE[cix, i]]
                    pe.wait_ge(acc_free[e], cnt)
                if KIND[name][0]:
                    src = {"bo": glaT, "bn": naT, "wo": mT}.get(name, hT)
                    N = TOK if name == "nk" else TQ
                    kk = 4 if name == "bn" else 8
                    for k in range(kk):
                        if name == "nq" and i == 0:
                            pe.wait_ge(n_sh, NH0[2 * l] + 2 * k + 2)
                        mm = nc.tensor.matmul(ps[:, i, 0:N], w[:, k, i * P:(i + 1) * P], src[:, k, 0:N],
                                              start=(k == 0), stop=(k == kk - 1))
                else:
                    for k in range(8):
                        mm = nc.tensor.matmul(ps[:, i, :], hT[:, k, i * P:(i + 1) * P], w[:, k, :],
                                              start=(k == 0), stop=(k == 7))
                mm.then_inc(acc_ready, 1)

            def modulate(dst, w):
                for k in range(KT):
                    for j in range(4):
                        mm = nc.tensor.matmul(dst[32 * j:32 * j + 32, :], csil[:, k, :], w[:, k, j * P:(j + 1) * P],
                                              start=(k == 0), stop=(k == KT - 1), skip_group_check=True)
                return mm

            def turn_modulations(dst, a0):
                for n in range(4):
                    mm = turn(dst[:, n * P:(n + 1) * P], adarow[:, (a0 + n) * P:(a0 + n + 1) * P])
                return mm

            def mod_job(job):
                bank = BANK[job]
                if BEFORE[job] is not None:
                    e, cnt = EVAC[BEFORE[job]]
                    pe.wait_ge(acc_free[e], cnt)
                if job[0] == "ada":
                    pe.wait_ge(s_ada, 16 * job_number(job)[0] + 16)
                    modulate(ps[:, bank, 0:P], wada).then_inc(acc_ready, 1)
                else:
                    last = ("ada", job[1], 4 * job[2] + 3)
                    pe.wait_ge(acc_free["act"], EVAC[last][1])
                    turn_modulations(ps[:, bank, :], job_number(("ada", job[1], 4 * job[2]))[1]).then_inc(acc_ready, 1)

            def na_step(l, t):
                u0, units = NA0[l], na_units(l)
                if t < len(units):
                    h, s, i = units[t]
                    hp, k0 = (h % 2) * HD, s * SEQ
                    if u0 + t >= 2:
                        pe.wait_ge(na_e, u0 + t - 1)
                    nc.tensor.matmul(ps[:, 4 + t % 2, k0:TOK], nqT[hp:hp + HD, h // 2, (2 * s + i) * P:(2 * s + i + 1) * P],
                                     nkT[hp:hp + HD, h // 2, k0:TOK], start=True, stop=True).then_inc(na_sc, 1)
                if 0 <= t - 2 < len(units):
                    h, s, i = units[t - 2]
                    pe.wait_ge(na_p, u0 + t - 1)
                    if u0 + t - 2:
                        pe.wait_ge(na_tc, u0 + t - 2)
                    for j in range(2 * s, 4):
                        mm = turn(ps[:, 6, j * P:(j + 1) * P], Pb[:, (t - 2) % 2, j * P:(j + 1) * P])
                    mm.then_inc(na_tp, 1)
                if t - 3 >= 0 and (t - 3) % 2:
                    h, s, i = units[t - 3]
                    hs, hp = (t - 3) // 2, (h % 2) * HD
                    pe.wait_ge(na_tc, u0 + t - 2)
                    if u0 // 2 + hs >= 2:
                        pe.wait_ge(na_oc, u0 // 2 + hs - 1)
                    for j in range(2 * s, 4):
                        mm = nc.tensor.matmul(ps[hp:hp + HD, 7, (hs % 2) * 256:(hs % 2) * 256 + 256],
                                              nv[:, j, h * HD:(h + 1) * HD], PT[:, hs % 2, j, :],
                                              start=(j == 2 * s), stop=(j == 3), skip_group_check=True)
                    mm.then_inc(na_o, 1)

            def gla_head(l, h):
                n, NQC = GH * l + h, 2 * q_tiles(l)
                for d in range(2):
                    if n:
                        pe.wait_ge(g_st, 14 * n)
                    for i in range(4):
                        mm = nc.tensor.matmul(ps[:, 2 * d + i // 2, (i % 2) * 256:(i % 2) * 256 + 256],
                                              gates[:, d, i, h * DK:(h + 1) * DK], cum[:, d].rearrange("p a t -> p (a t)"),
                                              start=True, stop=True)
                    mm.then_inc(g_cum, 1)
                for d in range(2):
                    pe.wait_ge(g_fac, 2 * n + d + 1)
                    if d == 0 and n:
                        pe.wait_ge(g_attm, n)
                        pe.wait_ge(g_oc, GT0[l] + h * q_tiles(l))
                    for i in range(4):
                        mm = turn(ps[:, 4 + d, i * P:(i + 1) * P], gt[:, d, 2, i * P:(i + 1) * P])
                    mm.then_inc(g_kt, 1)
                    for cc in range(NQC):
                        t0 = (cc % 2) * CH
                        mm = nc.tensor.matmul(ps[t0:t0 + CH, 6, d * 256 + (cc // 2) * CH:d * 256 + (cc // 2 + 1) * CH],
                                              gt[:, d, 2, cc * CH:(cc + 1) * CH], gt[:, d, 1, cc * CH:(cc + 1) * CH],
                                              start=True, stop=True, skip_group_check=True)
                mm.then_inc(g_att, 1)
                pe.wait_ge(g_ktc, 2 * n + 2)
                pe.wait_ge(g_exp, 2 * n + 2)
                for i in range(7):
                    for d in range(2):
                        cc = scan_order(d)[i]
                        t0 = (cc % 2) * CH
                        if i >= 2:
                            pe.wait_ge(g_st, 14 * n + 2 * (i - 2) + d + 1)
                        b = ps[:, 2 * d + i % 2, 0:DV]
                        nc.tensor.matmul(b, gt[t0:t0 + CH, d, 3, (cc // 2) * P:(cc // 2 + 1) * P],
                                         V[t0:t0 + CH, cc // 2, h * DV:(h + 1) * DV],
                                         start=True, stop=True, skip_group_check=True).then_inc(g_ds, 1)
                pe.wait_ge(g_attm, n + 1)
                pe.wait_ge(g_st, 14 * n + 14)
                for i in range(q_tiles(l)):
                    o = GT0[l] + h * q_tiles(l) + i
                    if o >= 2:
                        pe.wait_ge(g_oc, o - 1)
                    dst = ps[:, (7, 5)[i % 2], 0:DV]
                    nc.tensor.matmul(dst, attS[:, i, :], V[:, i, h * DV:(h + 1) * DV], start=True, stop=False,
                                     skip_group_check=True)
                    for cc in (2 * i, 2 * i + 1):
                        t0 = (cc % 2) * CH
                        ds_ = [d for d in range(2) if scan_order(d).index(cc)]
                        for d in ds_:
                            mm = nc.tensor.matmul(dst[t0:t0 + CH, :], gt[:, d, 0, cc * CH:(cc + 1) * CH],
                                                  S[:, d, scan_order(d).index(cc), :], start=False, stop=(d == ds_[-1]),
                                                  skip_group_check=True)
                    mm.then_inc(g_o, 1)

            def norm_sum(n, T):
                for k in range(KT):
                    pe.wait_ge(n_sq, KT * n + k + 1)
                    mm = nc.tensor.matmul(ps[:, 7, 0:T], ones, hT[:, k, 0:T], start=(k == 0), stop=(k == KT - 1))
                mm.then_inc(n_sum, 1)

            pe.wait_ge(s_const, 16)
            pe.wait_ge(s_vec, 16 * 9)
            turn(ps[:, 0, 0:128], vrow[:, 0, :])
            turn(ps[:, 0, 128:152], vrow[0:24, 1, :], 24).then_inc(v_t, 1)
            pe.wait_ge(s_x, 32)
            for k in range(KT):
                if k == 0:
                    pe.wait_ge(v_c, 1)
                for i in range(4):
                    mm = turn(ps[:, k, i * P:(i + 1) * P], xload[:, i, k * P:(k + 1) * P])
                mm.then_inc(t_x, 1)
            meet(pe, TOKENS_MET)
            norm_sum(0, TOK)

            for l in range(DEPTH):
                m, TQ, NQ = moe[l], q_tiles(l) * P, q_tiles(l)
                if l == 0:
                    for n in range(4):
                        pe.wait_ge(s_w[n % RING], 16 * (n // RING + 1))
                        modulate(ps[:, 0, n * P:(n + 1) * P], ring[n % RING]).then_inc(s_wused, 1)
                    pe.wait_ge(a_sb, 1)
                    turn_modulations(ps[:, 3, :], 0).then_inc(a_col, 1)
                    meet(pe, MODS_MET)
                else:
                    norm_sum(2 * l, TOK)

                for name in ("nq", "nk", "nv"):
                    cix = chunk_index(l, name)
                    for i in range(gemm_tiles(l, name)):
                        gemm_tile(cix, i)
                        for job in jobs(l).get((name, i), []):
                            mod_job(job)
                cix = chunk_index(l, "lr")
                pe.wait_ge(s_w[cix % RING], 16 * (cix // RING + 1))
                for i in range(4):
                    for k in range(KT):
                        mm = nc.tensor.matmul(ps[:, 7, i * 32:(i + 1) * 32], hT[:, k, i * P:(i + 1) * P], chunk_view(cix)[:, k, :],
                                              start=(k == 0), stop=(k == KT - 1), skip_group_check=True)
                mm.then_inc(s_wused, 1)
                pe.wait_ge(lr_sb, l + 1)
                for i in range(4):
                    mm = turn(ps[0:32, 6, i * P:(i + 1) * P], lrn[:, i, :])
                mm.then_inc(lr_tp, 1)
                pe.wait_ge(lr_T, l + 1)
                pe.wait_ge(lr_one, l + 1)
                pe.wait_ge(s_par, 64 * (l + 1))
                for u in range(8):
                    d, i = u % 2, u // 2
                    if 8 * l + u >= 2:
                        pe.wait_ge(gd, 8 * l + u - 1)
                    nc.tensor.matmul(ps[:, 4 + u % 2, :], lrT[:, i * P:(i + 1) * P], up[:, 512 * d:512 * d + 512],
                                     start=True, stop=True).then_inc(gz, 1)
                pe.wait_ge(gd, 8 * l + 8)
                for ev, a, b in mix_events(l):
                    if ev == "tile":
                        gemm_tile(a, b)
                    elif ev != "na":
                        mod_job((ev, a, b))
                    else:
                        if a == 0:
                            pe.wait_ge(acc_free["act"], EVAC[chunk_index(l, "nv"), 3][1])
                            pe.wait_ge(acc_free["dve"], EVAC[chunk_index(l, "nk"), 3][1])
                        na_step(l, a)
                for a in range(2):
                    T = TQ if a == 0 else TOK
                    pe.wait_ge(acc_free["dve"], EVAC[chunk_index(l, "k"), 3][1])
                    for h in range(GH):
                        b = 4 * a + h
                        if a == 0:
                            if h == 0:
                                pe.wait_ge(acc_free["act"], EVAC[chunk_index(l, "v", 1), 3][1])
                                pe.wait_ge(na_oc, (NA0[l] + len(na_units(l))) // 2)
                        for i in range(T // P):
                            mm = turn(ps[:, b, i * P:(i + 1) * P], qk[:, a, i, h * DK:(h + 1) * DK])
                        mm.then_inc(g_t, 1)
                meet(pe, met_at(l, "mix"))
                for h in range(GH):
                    gla_head(l, h)
                meet(pe, met_at(l, "gla"))
                for n in range(2):
                    for i in range(NQ):
                        gemm_tile(chunk_index(l, "g", n), i)
                pe.wait_ge(g_gated, 2 * QT0[l] + 2 * NQ)
                for k in range(8):
                    if k >= 4:
                        pe.wait_ge((g_tc_act, g_tc_dve)[k % 2], 4 * l + (k - 4) // 2 + 1)
                    for i in range(NQ):
                        mm = turn(ps[:, 4 + k % 4, i * P:(i + 1) * P], O[:, i, k * P:(k + 1) * P])
                    mm.then_inc(g_t, 1)
                meet(pe, met_at(l, "gate"))
                for j in range(2):
                    for name in ("ga", "bo", "gb", "bn"):
                        for i in range(4):
                            gemm_tile(chunk_index(l, name, j), i)
                pe.wait_ge(acc_free["dve"], EVAC[chunk_index(l, "bn", 1), 3][1])
                for n in range(2):
                    for i in range(4):
                        gemm_tile(chunk_index(l, "wo", n), i)
                meet(pe, met_at(l, "merge"))
                norm_sum(2 * l + 1, TQ)

                pe.wait_ge(s_rw, 32)
                for k in range(KT):
                    pe.wait_ge(n_sh, NH0[2 * l + 1] + (k + 1) * (TQ // SEQ))
                    for i in range(NQ):
                        mm = nc.tensor.matmul(ps[32 * i:32 * i + NE, 0, 0:P], wr[:, k, :], hT[:, k, i * P:(i + 1) * P],
                                              start=(k == 0), stop=(k == KT - 1), skip_group_check=True)
                mm.then_inc(r_lg, 1)
                for i in range(NQ):
                    b = 1 + 2 * (i % 3)
                    if i >= 3:
                        pe.wait_ge(r_natc, QT0[l] + i - 2)
                    for k in range(KT):
                        mm = turn(ps[:, b + k // 4, (k % 4) * P:(k % 4 + 1) * P], hT[:, k, i * P:(i + 1) * P])
                    mm.then_inc(r_nat, 1)
                    if i == 0:
                        pe.wait_ge(r_aff, l + 1)
                        turn(ps[:, 0, P:2 * P], affT).then_inc(r_aT, 1)
                pe.wait_ge(r_sel, l + 1)
                M = rt[:, 0:NQ * NE]
                for i in range(NQ):
                    for j in range(i + 1):
                        mm = nc.tensor.matmul(ps[:, 7, i * NE:(i + 1) * NE], ones if j < i else strict, M[:, j * NE:(j + 1) * NE],
                                              start=(j == 0), stop=(j == i), skip_group_check=True)
                for j in range(NQ):
                    mm = nc.tensor.matmul(ps[:, 7, 64:64 + NE], ones, M[:, j * NE:(j + 1) * NE],
                                          start=(j == 0), stop=(j == NQ - 1), skip_group_check=True)
                mm.then_inc(r_rank, 1)
                meet(pe, met_at(l, "route"))

                def turn_block(b):
                    pe.wait_ge(m["x_in"], 32 * b + 32)
                    for cc in range(4):
                        mm = turn(ps[:, 0, cc * P:(cc + 1) * P], xblk[:, cc * P:(cc + 1) * P])
                    mm.then_inc(m["xT_ps"], 1)

                def expert_block(b, p, par):
                    pe.wait_ge(m["xT_sb"], b + 1)
                    for bank, w, arrived, done in ((1, W1[par], "w1_in", "g_ps"), (2, W3[par], "w3_in", "u_ps")):
                        pe.wait_ge(m[f"{arrived}{par}"], 16 * p + 16)
                        for k in range(KT):
                            for a in range(2):
                                mm = nc.tensor.matmul(ps[64 * a:64 * a + 64, bank, :], xbT[:, k % 4, k // 4, :],
                                                      w[:, k, a * 512:(a + 1) * 512], start=(k == 0), stop=(k == KT - 1),
                                                      skip_group_check=True)
                        mm.then_inc(m[done], 1)
                    turn_block(b + 1)
                    pe.wait_ge(m["h_sb"], b + 2)
                    for cc in range(4):
                        mm = turn(ps[:, 3, cc * P:(cc + 1) * P], hblk[:, cc * P:(cc + 1) * P])
                    mm.then_inc(m["hT_ps"], 1)
                    pe.wait_ge(m["hT_sb"], b + 1)
                    pe.wait_ge(m["y_sb"], b + 1)

                def expert_out(par):
                    for k in range(KT):
                        for a in range(2):
                            mm = nc.tensor.matmul(ps[64 * a:64 * a + 64, 4, :], hbT[:, k % 4, k // 4, :],
                                                  W2[:, k, a * 512:(a + 1) * 512], start=(k == 0), stop=(k == KT - 1),
                                                  skip_group_check=True)
                    mm.then_inc(m["y_ps"], 1)

                for name in AHEAD:
                    pe.sem_inc(m[name], AHEAD[name])
                turn_block(0)
                with pe.Fori(0, NE // 2) as p:
                    for par in range(2):
                        b1 = pe.value_load(blocks[0:1, 0, bass.ds(2 * p + par, 1)], min_val=1, max_val=MAXB)
                        b0 = pe.value_load(blocks[0:1, 1, bass.ds(2 * p + par, 1)], min_val=0, max_val=MAXB)
                        with pe.Fori(b0, b1) as b:
                            expert_block(b, p, par)
                            pe.wait_ge(m["w2_in"], 32 * p + 16 * par + 16)
                            expert_out(par)
                meet(pe, met_at(l, "experts"))
                for k in range(KT):
                    if k == 0:
                        pe.wait_ge(c_z, QT0[l] + NQ)
                    for i in range(NQ):
                        mm = turn(ps[:, k, i * P:(i + 1) * P], z[:, i, k * P:(k + 1) * P])
                    mm.then_inc(c_t, 1)
                meet(pe, met_at(l, "combine"))

            norm_sum(2 * DEPTH, SEQ)
            pe.wait_ge(n_h, NH0[2 * DEPTH] + KT)
            for i in range(2):
                for k in range(KT):
                    mm = turn(ps[:, 2 * i + k // 4, (k % 4) * P:(k % 4 + 1) * P], hT[:, k, i * P:(i + 1) * P])
                mm.then_inc(f_t, 1)

        @block.scalar
        def _(act):
            own = [0]

            def link(ins):
                own[0] += 1
                ins.then_inc(chain["act"], 1)
                act.wait_ge(chain["act"], own[0])

            def evacuate(cix, i):
                l, name, n = CHUNKS[cix]
                TQ = q_tiles(l) * P
                act.wait_ge(acc_ready, NUMBER[cix, i])
                if name == "nq":
                    ins = nc.scalar.activation(nqT[:, i, 0:TQ], ps[:, i, 0:TQ], ACT.Copy, scale=HD ** -0.5)
                elif name == "nv":
                    ins = nc.scalar.activation(nv[:, i, :], ps[:, i, :], ACT.Copy)
                elif name == "v":
                    if (l, n, i) == (0, 0, 0):
                        act.wait_ge(s_zfill, ZFILLS)
                    ins = nc.scalar.activation(V[:, i, n * 512:(n + 1) * 512], ps[:, i, :], ACT.Copy)
                elif name == "g":
                    t = 2 * QT0[l] + n * q_tiles(l) + i
                    if n * q_tiles(l) + i >= 2:
                        act.wait_ge(g_gated, t - 1)
                    ins = nc.scalar.activation(sg[:, t % 2, :], ps[:, i, :], ACT.Silu)
                else:
                    a = 0 if name == "ga" else 1
                    if n:
                        act.wait_ge(acc_free["dve"], EVAC[chunk_index(l, ("bo", "bn")[a], 0), i][1])
                    ins = nc.scalar.activation(SG[:, a, i, 0:TQ], ps[:, i, 0:TQ], ACT.Sigmoid)
                ins.then_inc(acc_free["act"], 1)

            def load_ada(l, n):
                act.dma_start(wada, w_ada[l][:, n * 512:(n + 1) * 512].rearrange("(k p) n -> p k n", p=P)).then_inc(s_ada, 16)

            def mod_job(l, job):
                act.wait_ge(acc_ready, NUMBER[job])
                place = job_number(job)[1]
                nc.scalar.activation(adarow[:, place * P:(place + 1) * P], ps[:, BANK[job], 0:P], ACT.Copy).then_inc(acc_free["act"], 1)
                todo = [j[0] for j in jobs(l).values() if j[0][0] == "ada"]
                if todo.index(job) + 1 < len(todo):
                    load_ada(*todo[todo.index(job) + 1][1:])

            def na_step(l, t):
                u0, units = NA0[l], na_units(l)
                if t < len(units):
                    h, s, i = units[t]
                    act.wait_ge(na_mx, u0 + t + 1)
                    if u0 + t >= 2:
                        act.wait_ge(na_tp, u0 + t - 1)
                    nc.scalar.activation(Pb[:, t % 2, s * SEQ:TOK], ps[:, 4 + t % 2, s * SEQ:TOK], ACT.Exp,
                                         bias=st[:, t % 4, 0:1], accum_out=st[:, t % 4, 1:2]).then_inc(na_e, 1)
                if 0 <= t - 2 < len(units):
                    h, s, i = units[t - 2]
                    hs = (t - 2) // 2
                    act.wait_ge(na_tp, u0 + t - 1)
                    if u0 // 2 + hs >= 2:
                        act.wait_ge(na_o, u0 // 2 + hs - 1)
                    nc.scalar.activation(PT[:, hs % 2, 2 * s:4, i * P:(i + 1) * P],
                                         ps[:, 6, 2 * s * P:4 * P].rearrange("p (j q) -> p j q", q=P),
                                         ACT.Copy).then_inc(na_tc, 1)
                if t - 3 >= 0 and (t - 3) % 2:
                    h, s, i = units[t - 3]
                    hs, hp = (t - 3) // 2, (h % 2) * HD
                    act.wait_ge(na_o, u0 // 2 + hs + 1)
                    nc.scalar.activation(naT[hp:hp + HD, h // 2, s * SEQ:s * SEQ + SEQ],
                                         ps[hp:hp + HD, 7, (hs % 2) * 256:(hs % 2) * 256 + 256], ACT.Copy).then_inc(na_oc, 1)

            def norm_root(n, T):
                for k in range(KT):
                    nc.scalar.activation(hT[:, k, 0:T], xT[:, k, 0:T], ACT.Square).then_inc(n_sq, 1)
                act.wait_ge(n_sum, n + 1)
                nc.scalar.activation(tmp10[:, 0:T], ps[:, 7, 0:T], ACT.Sqrt, scale=1.0 / D, bias=epst).then_inc(n_root, 1)

            def norm_shift(n, T, l, row):
                for k in range(KT):
                    for s, a, b in ((0, 0, SEQ), (1, SEQ, TOK)):
                        if a < T:
                            act.wait_ge(n_h, NH0[n] + k * (T // SEQ) + s + 1)
                            nc.scalar.activation(hT[:, k, a:b], hT[:, k, a:b], ACT.Identity,
                                                 bias=mod[:, l, s, row * 8 + k:row * 8 + k + 1]).then_inc(n_sh, 1)

            act.wait_ge(v_c, 1)
            nc.scalar.activation(csil[:, :, 0:2].rearrange("p k s -> p s k"),
                                 vcol[:, 136:152].rearrange("p (s k) -> p s k", s=2), ACT.Silu)
            act.wait_ge(t_x, 8)
            nc.scalar.activation(xT[:, 4:8, :], ps[:, 4:8, :], ACT.Copy)
            meet(act, TOKENS_MET)
            norm_root(0, TOK)
            for l in range(DEPTH):
                m, TQ, NQ = moe[l], q_tiles(l) * P, q_tiles(l)
                if l == 0:
                    act.wait_ge(s_wused, 4)
                    nc.scalar.activation(adarow[:, 0:512], ps[:, 0, :], ACT.Copy).then_inc(a_sb, 1)
                    meet(act, MODS_MET)
                else:
                    norm_root(2 * l, TOK)
                norm_shift(2 * l, TOK, l, 0)

                load_ada(*[j[0] for j in jobs(l).values()][0][1:])
                for name in ("nq", "nk", "nv"):
                    for i in range(gemm_tiles(l, name)):
                        if name != "nk":
                            evacuate(chunk_index(l, name), i)
                        for job in jobs(l).get((name, i), []):
                            mod_job(l, job)
                act.wait_ge(*used(chunk_index(l, "lr")))
                nc.scalar.activation(lrn, ps[:, 7, 0:128].rearrange("p (i e) -> p i e", i=4), ACT.Copy).then_inc(lr_sb, 1)
                act.wait_ge(lr_tp, l + 1)
                nc.scalar.activation(lrT[0:32, :], ps[0:32, 6, :], ACT.Copy).then_inc(lr_T, 1)
                for u in range(8):
                    d, i = u % 2, u // 2
                    act.wait_ge(gz, 8 * l + u + 1)
                    g = gates[:, d, i, :]
                    link(nc.scalar.activation(g, ps[:, 4 + u % 2, :], ACT.Abs))
                    link(nc.scalar.activation(g, g, ACT.Exp, scale=-1.0))
                    nc.scalar.activation(g, g, ACT.Ln, bias=1.0).then_inc(gl, 1)
                for ev, a, b in mix_events(l):
                    if ev == "na":
                        na_step(l, a)
                    elif ev == "ada":
                        mod_job(l, (ev, a, b))
                    elif ev == "tile" and KIND[CHUNKS[a][1]][1] == "act":
                        evacuate(a, b)
                for h in range(GH):
                    act.wait_ge(g_t, 16 * l + h + 1)
                    nc.scalar.activation(qkT[:, 0, h, 0:TQ], ps[:, h, 0:TQ], ACT.Copy, scale=DK ** -0.5)
                meet(act, met_at(l, "mix"))

                for h in range(GH):
                    n = GH * l + h
                    for d in range(2):
                        act.wait_ge(g_cum, 2 * n + d + 1)
                        if h:
                            act.wait_ge(g_o, GT0[l] + h * NQ)
                        v = ps[:, 2 * d:2 * d + 2, :].rearrange("p b (i a t) -> p (b i) a t", i=2, a=2)
                        for slot_, a, scale in ((0, 0, 1 / TAU), (1, 1, -1 / TAU), (2, 1, 1 / TAU)):
                            ins = nc.scalar.activation(gt[:, d, slot_, :].rearrange("p (i t) -> p i t", i=4), v[:, :, a, :],
                                                       ACT.Exp, scale=scale)
                        ins.then_inc(g_exp, 1)
                    for d in range(2):
                        act.wait_ge(g_kt, 2 * n + d + 1)
                        nc.scalar.activation(gt[:, d, 3, :], ps[:, 4 + d, :], ACT.Copy).then_inc(g_ktc, 1)
                    for i in range(NQ):
                        o = GT0[l] + h * NQ + i
                        act.wait_ge(g_o, o + 1)
                        src = ps[:, (7, 5)[i % 2], 0:DV]
                        nc.scalar.activation(O[:, i, h * DV:(h + 1) * DV], src, ACT.Copy)
                        if h or i:
                            act.wait_ge(g_oc, o)
                        nc.scalar.activation(junk, src, ACT.Square, accum_out=ssq[:, i, h:h + 1]).then_inc(g_oc, 1)
                meet(act, met_at(l, "gla"))
                nc.scalar.activation(ssq[:, 0:NQ, :], ssq[:, 0:NQ, :], ACT.Sqrt, scale=1.0 / DV, bias=epst).then_inc(g_root, 1)
                for n in range(2):
                    for i in range(NQ):
                        evacuate(chunk_index(l, "g", n), i)
                for k in range(0, 8, 2):
                    act.wait_ge(g_t, 16 * l + 8 + k + 1)
                    nc.scalar.activation(glaT[:, k, 0:TQ], ps[:, 4 + k % 4, 0:TQ], ACT.Copy).then_inc(g_tc_act, 1)
                meet(act, met_at(l, "gate"))
                for j in range(2):
                    for name in ("ga", "gb"):
                        for i in range(4):
                            evacuate(chunk_index(l, name, j), i)
                meet(act, met_at(l, "merge"))
                norm_root(2 * l + 1, TQ)
                norm_shift(2 * l + 1, TQ, l, 3)

                act.wait_ge(r_lg, l + 1)
                for i in range(NQ):
                    g = slice(32 * i, 32 * i + NE)
                    ins = nc.scalar.activation(affT[g, :], ps[g, 0, 0:P], ACT.Sigmoid)
                ins.then_inc(r_aff, 1)
                for i in range(NQ):
                    act.wait_ge(r_nat, QT0[l] + i + 1)
                    b = 1 + 2 * (i % 3)
                    nc.scalar.activation(h2n[:, i, :], ps[:, b:b + 2, :].rearrange("p b n -> p (b n)"), ACT.Copy).then_inc(r_natc, 1)
                meet(act, met_at(l, "route"))

                with act.Fori(0, NE) as e:
                    b1 = act.value_load(blocks[0:1, 0, bass.ds(e, 1)], min_val=1, max_val=MAXB)
                    b0 = act.value_load(blocks[0:1, 1, bass.ds(e, 1)], min_val=0, max_val=MAXB)
                    with act.Fori(b0, b1) as b:
                        act.wait_ge(m["g_ps"], b + 1)
                        act.wait_ge(m["h_sb"], b + 1)
                        nc.scalar.activation(silu_g, ps[:, 1, :], ACT.Silu).then_inc(m["silu"], 1)
                        act.wait_ge(m["hT_ps"], b + 2)
                        act.wait_ge(m["y_ps"], b + 1)
                        nc.scalar.activation(U[:, 1, 2048:2560], ps[:, 3, :], ACT.Copy).then_inc(m["hT_sb"], 1)
                        act.wait_ge(m["y_sb"], b + 2)
                        for a in range(2):
                            act.dma_start(ybuf[bass.ds(b * BLK, BLK), 512 * a:512 * a + 512], yblk[64 * a:64 * a + 64, :]).then_inc(m["y_out"], 16)
                meet(act, met_at(l, "experts"))
                meet(act, met_at(l, "combine"))
            norm_root(2 * DEPTH, SEQ)
            for i in range(2):
                act.wait_ge(f_t, i + 1)
                nc.scalar.activation(fin[:, i, :], ps[:, 2 * i:2 * i + 2, :].rearrange("p b n -> p (b n)"), ACT.Copy).then_inc(f_c, 1)

        @block.vector
        def _(dve):
            own = [0]

            def link(ins):
                own[0] += 1
                ins.then_inc(chain["dve"], 1)
                dve.wait_ge(chain["dve"], own[0])

            def evacuate(cix, i):
                l, name, n = CHUNKS[cix]
                TQ = q_tiles(l) * P
                dve.wait_ge(acc_ready, NUMBER[cix, i])
                src = ps[:, i, :]
                if name == "nk":
                    ins = nc.vector.tensor_copy(nkT[:, i, :], src)
                elif name in ("q", "k"):
                    dst = qk[:, 0 if name == "q" else 1, i, :]
                    if i >= 2:
                        ins = nc.vector.tensor_copy(dst, src)
                    else:
                        t = rtmp.rearrange("p f (h a u e) -> p f h a u e", h=GH, a=2, u=2)
                        sv = src.rearrange("p (h a u e) -> p h a u e", h=GH, a=2, u=2)
                        dv = dst.rearrange("p (h a u e) -> p h a u e", h=GH, a=2, u=2)
                        for f in range(2):
                            for u in range(2):
                                for a in range(2):
                                    ins = nc.vector.tensor_tensor(t[:, f, :, a, u, :], sv[:, :, a, u, :],
                                                                  rope[:, f, i, a:a + 1, :].to_broadcast([P, GH, 32]), ALU.mult)
                        link(ins)
                        for a in range(2):
                            nc.vector.tensor_tensor(dv[:, :, a, 0, :], t[:, 0, :, a, 0, :], t[:, 1, :, a, 1, :], ALU.subtract)
                            ins = nc.vector.tensor_tensor(dv[:, :, a, 1, :], t[:, 1, :, a, 0, :], t[:, 0, :, a, 1, :], ALU.add)
                elif name == "bo":
                    dve.wait_ge(acc_free["act"], EVAC[chunk_index(l, "ga", n), i][1])
                    ins = nc.vector.tensor_tensor(mT[:, 4 * n + i, 0:TQ], SG[:, 0, i, 0:TQ], src[:, 0:TQ], ALU.mult)
                elif name == "bn":
                    dve.wait_ge(acc_free["act"], EVAC[chunk_index(l, "gb", n), i][1])
                    link(nc.vector.tensor_tensor(SG[:, 1, i, 0:TQ], SG[:, 1, i, 0:TQ], src[:, 0:TQ], ALU.mult))
                    ins = nc.vector.tensor_tensor(mT[:, 4 * n + i, 0:TQ], mT[:, 4 * n + i, 0:TQ], SG[:, 1, i, 0:TQ], ALU.add)
                else:
                    k = 4 * n + i
                    for s, a, b in streams(l):
                        ins = nc.vector.scalar_tensor_tensor(out=xT[:, k, a:b], in0=src[:, a:b],
                                                             scalar=mod[:, l, s, 16 + k:17 + k], in1=xT[:, k, a:b],
                                                             op0=ALU.mult, op1=ALU.add)
                ins.then_inc(acc_free["dve"], 1)

            def na_step(l, t):
                u0, units = NA0[l], na_units(l)
                if t < len(units):
                    h, s, i = units[t]
                    dve.wait_ge(na_sc, u0 + t + 1)
                    bank = ps[:, 4 + t % 2, :]
                    if s == 0:
                        link(nc.vector.tensor_tensor(bank[:, 0:SEQ], bank[:, 0:SEQ], bias[:, i, h, :], ALU.add))
                    nc.vector.tensor_reduce(st[:, t % 4, 0:1], bank[:, s * SEQ:TOK], AX, ALU.max, negate=True).then_inc(na_mx, 1)
                if 0 <= t - 1 < len(units):
                    h, s, i = units[t - 1]
                    dve.wait_ge(na_e, u0 + t)
                    link(nc.vector.reciprocal(st[:, (t - 1) % 4, 2:3], st[:, (t - 1) % 4, 1:2]))
                    p = Pb[:, (t - 1) % 2, s * SEQ:TOK]
                    nc.vector.tensor_scalar(p, p, st[:, (t - 1) % 4, 2:3], None, ALU.mult).then_inc(na_p, 1)

            def norm_inverse(n, T):
                dve.wait_ge(n_root, n + 1)
                link(nc.vector.reciprocal(tmp10[:, 512:512 + T], tmp10[:, 0:T]))

            def norm_scale(n, T, scale):
                for k in range(KT):
                    for s, a, b in ((0, 0, SEQ), (1, SEQ, TOK)):
                        if a < T:
                            nc.vector.scalar_tensor_tensor(out=hT[:, k, a:b], in0=xT[:, k, a:b], scalar=scale(s, k),
                                                           in1=tmp10[:, 512 + a:512 + b], op0=ALU.mult,
                                                           op1=ALU.mult).then_inc(n_h, 1)

            def modulations(l, q, bank):
                col = bank.rearrange("p (m s) -> p m s", s=32)
                for s in range(2):
                    ins = nc.vector.tensor_tensor(mod[:, l, s, 16 * q:16 * q + 16], col[:, :, s],
                                                  vcol[:, 64 * l + 16 * q:64 * l + 16 * q + 16], ALU.add)
                return ins

            def scales(l, q):
                if q == 1:
                    return
                w = q // 2
                row = (1, 4)[w] * 8
                for s in range(2):
                    nc.vector.scalar_tensor_tensor(out=s1[:, l, w, s, :], in0=mod[:, l, s, row:row + 8], scalar=1.0,
                                                   in1=vcol[:, 64 * l + 48 + 8 * w:64 * l + 56 + 8 * w],
                                                   op0=ALU.add, op1=ALU.mult)

            link(nc.vector.memset(csil[:], 0.0))
            nc.vector.memset(up[0:32, :], 0.0).then_inc(s_zero, 1)
            dve.wait_ge(v_t, 1)
            nc.vector.tensor_copy(vcol[:], ps[:, 0, 0:152]).then_inc(v_c, 1)
            dve.wait_ge(t_x, 4)
            nc.vector.tensor_copy(xT[:, 0:4, :], ps[:, 0:4, :])
            meet(dve, TOKENS_MET)
            norm_inverse(0, TOK)
            for l in range(DEPTH):
                m, TQ, NQ = moe[l], q_tiles(l) * P, q_tiles(l)
                if l == 0:
                    dve.wait_ge(a_col, 1)
                    link(modulations(0, 0, ps[:, 3, :]))
                    scales(0, 0)
                    meet(dve, MODS_MET)
                else:
                    norm_inverse(2 * l, TOK)
                norm_scale(2 * l, TOK, lambda s, k: s1[:, l, 0, s, k:k + 1])

                nc.vector.memset(lrT[32:33, :], 1.0).then_inc(lr_one, 1)
                dve.wait_ge(s_bias, 256 * (l + 1))
                for i in range(2):
                    v = bias[:, i].rearrange("p h (r k) -> p (h r) k", r=GROWS)
                    ins = nc.vector.tensor_tensor(v, v, cmask.rearrange("p (a k) -> p a k", a=1).to_broadcast([P, NH * GROWS, GRID_W]), ALU.add)
                link(ins)
                for i in range(4):
                    evacuate(chunk_index(l, "nk"), i)
                for u in range(8):
                    d, i = u % 2, u // 2
                    dve.wait_ge(gl, 8 * l + u + 1)
                    nc.vector.scalar_tensor_tensor(out=gates[:, d, i, :], in0=ps[:, 4 + u % 2, :], scalar=0.0,
                                                   in1=gates[:, d, i, :], op0=ALU.min, op1=ALU.subtract).then_inc(gd, 1)
                for ev, a, b in mix_events(l):
                    if ev == "na":
                        na_step(l, a)
                    elif ev == "col":
                        dve.wait_ge(acc_ready, NUMBER[ev, a, b])
                        modulations(a, b, ps[:, BANK[ev, a, b], :]).then_inc(acc_free["dve"], 1)
                        dve.wait_ge(acc_free["dve"], EVAC[ev, a, b][1])
                        scales(a, b)
                    elif ev == "tile" and KIND[CHUNKS[a][1]][1] == "dve":
                        evacuate(a, b)
                for h in range(GH):
                    dve.wait_ge(g_t, 16 * l + GH + h + 1)
                    nc.vector.tensor_copy(qkT[:, 1, h, :], ps[:, 4 + h, :])
                meet(dve, met_at(l, "mix"))

                link(nc.vector.memset(attS, 0.0))
                for h in range(GH):
                    n = GH * l + h
                    for d in range(2):
                        dve.wait_ge(g_exp, 2 * n + d + 1)
                        e = gt[:, d, 0, :].rearrange("p (c t) -> p c t", t=CH)
                        link(nc.vector.tensor_copy(dec[:, d, :], e[:, :, CH - 1 if d == 0 else 0]))
                        nc.vector.tensor_tensor(gt[:, d, 0, 0:TQ], gt[:, d, 0, 0:TQ], qkT[:, 0, h, 0:TQ], ALU.mult)
                        nc.vector.tensor_tensor(gt[:, d, 1, 0:TQ], gt[:, d, 1, 0:TQ], qkT[:, 0, h, 0:TQ], ALU.mult)
                        nc.vector.tensor_tensor(gt[:, d, 2, :], gt[:, d, 2, :], qkT[:, 1, h, :], ALU.mult).then_inc(g_fac, 1)
                    dve.wait_ge(g_att, n + 1)
                    for d in range(2):
                        ins = nc.vector.tensor_tensor(attP[:, d, 0:NQ, :], ps[:, 6, d * 256:d * 256 + NQ * CH].rearrange("p (i t) -> p i t", t=CH),
                                                      amask[:, d:d + 1, :].to_broadcast([P, NQ, CH]), ALU.mult)
                    link(ins)
                    if h:
                        dve.wait_ge(g_o, GT0[l] + h * NQ)
                    for a in (0, CH):
                        ins = nc.vector.tensor_tensor(attS[a:a + CH, 0:NQ, a:a + CH],
                                                      attP[a:a + CH, 0, 0:NQ, :], attP[a:a + CH, 1, 0:NQ, :], ALU.add)
                    ins.then_inc(g_attm, 1)
                    for i in range(7):
                        for d in range(2):
                            dve.wait_ge(g_ds, 14 * n + 2 * i + d + 1)
                            b = ps[:, 2 * d + i % 2, 0:DV]
                            cc = scan_order(d)[i]
                            if i == 0:
                                ins = nc.vector.tensor_copy(S[:, d, 1, :], b)
                            else:
                                dve.wait_ge(g_st, 14 * n + 2 * (i - 1) + d + 1)
                                ins = nc.vector.scalar_tensor_tensor(out=S[:, d, i + 1, :], in0=S[:, d, i, :],
                                                                     scalar=dec[:, d, cc:cc + 1], in1=b, op0=ALU.mult, op1=ALU.add)
                            ins.then_inc(g_st, 1)
                meet(dve, met_at(l, "gla"))

                dve.wait_ge(g_root, l + 1)
                link(nc.vector.reciprocal(ssq[:, 0:NQ, :], ssq[:, 0:NQ, :]))
                for n in range(2):
                    for i in range(NQ):
                        t = 2 * QT0[l] + n * NQ + i
                        dve.wait_ge(acc_free["act"], EVAC[chunk_index(l, "g", n), i][1])
                        b = sg[:, t % 2, :].rearrange("p (a e) -> p a e", a=2)
                        link(nc.vector.tensor_tensor(b, b, gnw[:].rearrange("p (a e) -> p a e", a=1).to_broadcast([P, 2, DV]), ALU.mult))
                        for a in range(2):
                            h = 2 * n + a
                            o = O[:, i, h * DV:(h + 1) * DV]
                            ins = nc.vector.scalar_tensor_tensor(out=o, in0=o, scalar=ssq[:, i, h:h + 1], in1=b[:, a, :],
                                                                 op0=ALU.mult, op1=ALU.mult)
                        ins.then_inc(g_gated, 1)
                for k in range(1, 8, 2):
                    dve.wait_ge(g_t, 16 * l + 8 + k + 1)
                    nc.vector.tensor_copy(glaT[:, k, 0:TQ], ps[:, 4 + k % 4, 0:TQ]).then_inc(g_tc_dve, 1)
                meet(dve, met_at(l, "gate"))
                for j in range(2):
                    for name in ("bo", "bn"):
                        for i in range(4):
                            evacuate(chunk_index(l, name, j), i)
                for n in range(2):
                    for i in range(4):
                        evacuate(chunk_index(l, "wo", n), i)
                meet(dve, met_at(l, "merge"))
                nc.vector.memset(affT, 0.0)
                norm_inverse(2 * l + 1, TQ)
                norm_scale(2 * l + 1, TQ, lambda s, k: s1[:, l, 1, s, k:k + 1])

                def R(a, n, split=None):
                    v = rt[:, a:a + n]
                    return v if split is None else v.rearrange("p (i e) -> p i e", e=split)

                def over(v, e):
                    return v.rearrange("p (n a) -> p n a", a=1).to_broadcast([P, v.shape[1], e])

                N = NQ * NE
                M, aff, sel = R(0, N, NE), R(64, N, NE), R(128, N, NE)
                dve.wait_ge(s_rw, 32)
                dve.wait_ge(r_aT, l + 1)
                link(nc.vector.tensor_copy(aff, ps[:, 0, P:P + 32 * NQ].rearrange("p (i e) -> p i e", e=32)[:, :, 0:NE]))
                link(nc.vector.tensor_tensor(sel, aff, br[:].rearrange("p (a e) -> p a e", a=1).to_broadcast([P, NQ, NE]), ALU.add))
                s4, pairs = R(128, N, EPG), R(192, NQ * NG * 6, 6)
                nc.vector.tensor_tensor(pairs[:, :, 0:3], s4[:, :, 0:3], s4[:, :, 1:4], ALU.add)
                nc.vector.tensor_tensor(pairs[:, :, 3:5], s4[:, :, 0:2], s4[:, :, 2:4], ALU.add)
                link(nc.vector.tensor_tensor(pairs[:, :, 5:6], s4[:, :, 0:1], s4[:, :, 3:4], ALU.add))
                gsc = R(288, NQ * NG)
                link(nc.vector.tensor_reduce(gsc, pairs, AX, ALU.max))

                def first_max(dst, v, e, top, wt):
                    link(nc.vector.tensor_reduce(top, v, AX, ALU.max))
                    link(nc.vector.tensor_tensor(wt, v, over(top, e), ALU.is_equal))
                    link(nc.vector.tensor_tensor(wt, wt, ramp[:, 16 - e:16].rearrange("p (a e) -> p a e", a=1).to_broadcast([P, NQ, e]), ALU.mult))
                    link(nc.vector.tensor_reduce(top, wt, AX, ALU.max))
                    link(nc.vector.tensor_tensor(dst, wt, over(top, e), ALU.is_equal))

                ing = R(312, NQ * NG)
                first_max(R(312, NQ * NG, NG), R(288, NQ * NG, NG), NG, R(304, NQ), R(328, NQ * NG, NG))
                link(nc.vector.tensor_scalar(ing, ing, BIG, -BIG, ALU.mult, ALU.add))
                selm = R(352, N, NE)
                link(nc.vector.tensor_tensor(R(352, N, EPG), s4, over(ing, EPG), ALU.add))
                oh1, sel2, oh2, t = R(496, N, NE), R(560, N, NE), R(640, N, NE), R(704, N, NE)
                first_max(oh1, selm, NE, R(416, NQ), R(424, N, NE))
                link(nc.vector.scalar_tensor_tensor(out=sel2, in0=oh1, scalar=-2 * BIG, in1=selm, op0=ALU.mult, op1=ALU.add))
                first_max(oh2, sel2, NE, R(624, NQ), R(424, N, NE))
                nc.vector.tensor_tensor(M, oh1, oh2, ALU.add).then_inc(r_sel, 1)
                a1, a2, den = R(768, NQ), R(772, NQ), R(776, NQ)
                for oh, a in ((oh1, a1), (oh2, a2)):
                    link(nc.vector.tensor_tensor(t, oh, aff, ALU.mult))
                    link(nc.vector.tensor_reduce(a, t, AX, ALU.add))
                link(nc.vector.tensor_tensor(den, a1, a2, ALU.add))
                link(nc.vector.reciprocal(den, den))
                nc.vector.tensor_tensor(wsel[:, 0:NQ, 0], a1, den, ALU.mult)
                nc.vector.tensor_tensor(wsel[:, 0:NQ, 1], a2, den, ALU.mult)
                dve.wait_ge(r_rank, l + 1)
                cnt, nbf, inc, base, pos = R(780, NE), R(796, NE), R(812, NE), R(828, NE), R(848, N, NE)
                ci = cnt.bitcast(I32)
                link(nc.vector.tensor_scalar(ci, ps[:, 7, 64:64 + NE], float(BLK - 1), None, ALU.add))
                link(nc.vector.tensor_scalar(ci, ci, BLK.bit_length() - 1, None, ALU.arith_shift_right))
                link(nc.vector.tensor_scalar(nbf, ci, 1.0, None, ALU.max))
                link(nc.vector.tensor_tensor_scan(inc, ones[:, 0:NE], nbf, 0.0, ALU.mult, ALU.add))
                link(nc.vector.tensor_tensor(base, inc, nbf, ALU.subtract))
                nc.vector.tensor_copy(blocks[:, 0, :], inc)
                nc.vector.tensor_copy(blocks[:, 1, :], base)
                link(nc.vector.tensor_scalar(base, base, float(BLK), None, ALU.mult))
                link(nc.vector.tensor_tensor(pos, ps[:, 7, 0:N].rearrange("p (i e) -> p i e", e=NE),
                                             base.rearrange("p (a e) -> p a e", a=1).to_broadcast([P, NQ, NE]), ALU.add))
                for c_, oh in enumerate((oh1, oh2)):
                    link(nc.vector.tensor_tensor(t, oh, pos, ALU.mult))
                    link(nc.vector.tensor_reduce(R(912 + 4 * c_, NQ), t, AX, ALU.add))
                    ins = nc.vector.tensor_copy(slot[:, 0:NQ, c_], R(912 + 4 * c_, NQ))
                ins.then_inc(r_slot, 1)
                meet(dve, met_at(l, "route"))

                dve.wait_ge(m["xT_ps"], 1)
                nc.vector.tensor_copy(xbT_flat, ps[:, 0, :]).then_inc(m["xT_sb"], 1)
                with dve.Fori(0, NE) as e:
                    b1 = dve.value_load(blocks[0:1, 0, bass.ds(e, 1)], min_val=1, max_val=MAXB)
                    b0 = dve.value_load(blocks[0:1, 1, bass.ds(e, 1)], min_val=0, max_val=MAXB)
                    with dve.Fori(b0, b1) as b:
                        dve.wait_ge(m["silu"], b + 1)
                        dve.wait_ge(m["u_ps"], b + 1)
                        dve.wait_ge(m["hT_ps"], b + 1)
                        nc.vector.tensor_tensor(hblk, silu_g, ps[:, 2, :], ALU.mult).then_inc(m["h_sb"], 1)
                        dve.wait_ge(m["xT_ps"], b + 2)
                        nc.vector.tensor_copy(xbT_flat, ps[:, 0, :]).then_inc(m["xT_sb"], 1)
                        dve.wait_ge(m["y_ps"], b + 2)
                        dve.wait_ge(m["y_out"], 32 * b + 32)
                        nc.vector.tensor_copy(yblk, ps[:, 4, :]).then_inc(m["y_sb"], 1)
                meet(dve, met_at(l, "experts"))

                for i in range(NQ):
                    dve.wait_ge(s_gather[i], 32 * l + 32)
                    link(nc.vector.tensor_scalar(z[:, i, :], yg[:, 2 * i, :], wsel[:, i, 0:1], None, ALU.mult))
                    nc.vector.scalar_tensor_tensor(out=z[:, i, :], in0=yg[:, 2 * i + 1, :], scalar=wsel[:, i, 1:2],
                                                   in1=z[:, i, :], op0=ALU.mult, op1=ALU.add).then_inc(c_z, 1)
                for k in range(KT):
                    dve.wait_ge(c_t, KT * l + k + 1)
                    for s, a, b in streams(l):
                        nc.vector.scalar_tensor_tensor(out=xT[:, k, a:b], in0=ps[:, k, a:b], scalar=mod[:, l, s, 40 + k:41 + k],
                                                       in1=xT[:, k, a:b], op0=ALU.mult, op1=ALU.add)
                meet(dve, met_at(l, "combine"))
            norm_inverse(2 * DEPTH, SEQ)
            norm_scale(2 * DEPTH, SEQ, lambda s, k: vcol[:, 128 + k:129 + k])

        @block.gpsimd
        def _(pool):
            nc.gpsimd.memset(zero, 0.0).then_inc(chain["pool"], 1)
            pool.wait_ge(chain["pool"], 1)
            pool.dma_start(rp.rearrange("l h r w -> (l h r) w").rearrange("(a b) w -> a (b w)", b=2), zero[0:120, 0:2 * RPAD]).then_inc(s_rpz, 16)
            pool.wait_ge(s_rpz, 16)
            for l in range(DEPTH):
                pool.dma_start(rp[l, :, :, GRID_W - WIN_C:GRID_W + WIN_C - 1].rearrange("h r w -> (h r) w"),
                               rpb[l].rearrange("h r w -> (h r) w")).then_inc(s_rp, 16)
            pool.wait_ge(s_rp, 32)
            for l in range(DEPTH):
                src = rp[l, :, WIN_R - GROWS:WIN_R + GROWS - 1, :].rearrange("h r w -> h (r w)").rearrange("(a h) n -> a h n", a=1)
                pool.dma_start(rx[l].rearrange("c h r w -> c h (r w)"), src.to_broadcast([GRID_W, NH, RW * RPAD])).then_inc(s_rx, 16)
            pool.wait_ge(met, MODS_MET)
            with pool.Fori(0, XROWS // P) as r:
                pool.dma_start(xbuf[bass.ds(r * P, P), :], zero).then_inc(s_zfill, 16)
                pool.wait_ge(s_zfill, 16 * r + 16)
            with pool.Fori(0, MAXB * BLK // P) as r:
                pool.dma_start(ybuf[bass.ds(r * P, P), :], zero).then_inc(s_zfill, 16)
                pool.wait_ge(s_zfill, 16 * r + (16 + 16 * (XROWS // P)))
            pool.wait_ge(s_zfill, ZFILLS)
            for l in range(DEPTH):
                m, NQ = moe[l], q_tiles(l)
                pool.wait_ge(r_slot, l + 1)
                pool.wait_ge(r_natc, QT0[l] + NQ)
                for i in range(NQ):
                    for c_ in range(2):
                        pool.indirect_dma_start(xbuf, bass.IndirectOffsetOnAxis(slot[:, i, c_:c_ + 1], 0), h2n[:, i, :], None,
                                                ).then_inc(m["scattered"], 16)
                pool.wait_ge(met, met_at(l, "route"))
                pool.wait_ge(m["scattered"], 32 * NQ)

                def load_x(b):
                    for a in range(2):
                        pool.dma_start(xblk[64 * a:64 * a + 64, :], xbuf[bass.ds(b * BLK, BLK), 512 * a:512 * a + 512]).then_inc(m["x_in"], 16)

                load_x(0)
                pool.wait_ge(m["xT_ps"], 1)
                load_x(1)
                with pool.Fori(0, NE) as e:
                    b1 = pool.value_load(blocks[0:1, 0, bass.ds(e, 1)], min_val=1, max_val=MAXB)
                    b0 = pool.value_load(blocks[0:1, 1, bass.ds(e, 1)], min_val=0, max_val=MAXB)
                    with pool.Fori(b0, b1) as b:
                        pool.wait_ge(m["xT_ps"], b + 2)
                        load_x(b + 2)
                total = pool.value_load(blocks[0:1, 0, NE - 1:NE], min_val=1, max_val=MAXB)
                pool.wait_ge(m["y_out"], 32 * total + 32)
                pool.wait_ge(m["x_in"], 32 * total + 64)
                nc.gpsimd.tensor_tensor(waited[:, l:l + 1], ones[0:1, 0:1], ones[0:1, 0:1], ALU.mult)
                pool.wait_ge(met, met_at(l, "experts"))
                for i in range(NQ):
                    for c_ in range(2):
                        pool.indirect_dma_start(yg[:, 2 * i + c_, :], None, ybuf, bass.IndirectOffsetOnAxis(slot[:, i, c_:c_ + 1], 0),
                                                ).then_inc(s_gather[i], 16)


def constants():
    k = np.zeros((P, 1361), np.float32)
    p, t = np.arange(P)[:, None], np.arange(P)[None, :]
    same = p // CH == t // CH
    k[:, 0:128] = p == t
    k[:, 128:256] = 1.0
    k[:, 256:384] = same & (p <= t)
    k[:, 384:512] = same & (p > t)
    k[:, 512:640] = same & (p >= t)
    k[:, 640:768] = same & (p < t)
    t64 = np.arange(CH)[None, :]
    k[:, 768:832] = p % CH <= t64
    k[:, 832:896] = p % CH >= t64
    k[:, 896:1024] = p < t
    half = DK // 2
    inv = np.float32(10000.0) ** (-np.arange(0, half, 2, dtype=np.float32) / np.float32(half))
    for i in range(2):
        tok = i * P + np.arange(P)
        for a, pos in enumerate((tok // GRID_W, tok % GRID_W)):
            ang = pos.astype(np.float32)[:, None] * inv[None, :]
            for f, fn in enumerate((np.cos, np.sin)):
                o = 1024 + ((f * 2 + i) * 2 + a) * 32
                k[:, o:o + 32] = fn(ang)
    col = np.arange(P)[:, None] % GRID_W
    c0 = np.clip(col - WIN_C // 2, 0, GRID_W - WIN_C)
    kc = np.arange(GRID_W)[None, :]
    k[:, 1280:1344] = np.where((kc >= c0) & (kc < c0 + WIN_C), 0.0, -BIG)
    k[:, 1344:1360] = np.arange(16, 0, -1)
    k[:, 1360] = EPS
    return k


_INS = ['x', 'c', 'ctx', 'c_ctx', 'w_ada', 'b_ada', 'norm1_w', 'norm2_w', 'w_in', 'w_gk_up', 'b_gk', 'gla_norm_w', 'rpb',
        'w_bo_gla', 'w_bo_na', 'w_out', 'w_router', 'b_router', 'w1', 'w3', 'w2', 'final_norm_w']


def kernel(**inputs):
    import numpy as _np
    import concourse.bacc as _bacc
    from concourse import mybir as _mybir
    from concourse.bass_utils import run_bass_kernel_spmd as _run

    nc = _bacc.Bacc("TRN2", target_bir_lowering=False, num_devices=1)
    arrays, args = {}, []
    for name in _INS + ["consts"]:
        a = constants() if name == "consts" else _np.ascontiguousarray(inputs[name])
        arrays[f"in_{name}"] = a
        args.append(nc.dram_tensor(f"in_{name}", a.shape, _mybir.dt.from_np(a.dtype), kind="ExternalInput").ap())
    args.append(nc.dram_tensor("out_0", (1, SEQ, D), _mybir.dt.float32, kind="ExternalOutput").ap())
    build(nc, *args)
    return _run(nc, [arrays], core_ids=[0]).results[0]["out_0"]
```

```python
from contextlib import ExitStack

import concourse.bass as bass
import numpy as np
from concourse import mybir

P = 128
D = 1024
KT = D // P
SEQ, CTX = 256, 256
TOK = SEQ + CTX
DEPTH = 2
GRID_W = 64
GROWS = SEQ // GRID_W
EPS = 1e-6
GH, DK, DV, LR = 4, 128, 256, 16
TAU = 16.0
CH = 64
NCH = TOK // CH
NH, HD = 8, 64
WIN_R, WIN_C = 8, 16
NE, NG, EPG = 16, 4, 4
FF = 1024
BLK = 64
MAXB = TOK * 2 // BLK + NE
XROWS = (MAXB + 2) * BLK
RPAD = 128
F32 = mybir.dt.float32
I32 = mybir.dt.int32
ALU = mybir.AluOpType
ACT = mybir.ActivationFunctionType
AX = mybir.AxisListType.X
BIG = 1e30

C_Q, C_K, C_V, C_G, C_LR = 0, 512, 1024, 2048, 3072
C_NQ, C_NK, C_NV, C_GA, C_GB = 3104, 3616, 4128, 4640, 5664


def weight_chunks():
    out = []
    for l in range(DEPTH):
        out += [(l, n, 0) for n in ("nq", "nk", "lr", "nv", "q", "k")] + [(l, "v", 0), (l, "v", 1)]
        out += [(l, "g", 0), (l, "g", 1)]
        for j in range(2):
            out += [(l, n, j) for n in ("ga", "bo", "gb", "bn")]
        out += [(l, "wo", 0), (l, "wo", 1)]
    return out


KIND = {"nq": (True, "act"), "nk": (True, "dve"), "nv": (False, "act"), "q": (False, "dve"), "k": (False, "dve"),
        "v": (False, "act"), "g": (False, "act"), "ga": (True, "act"), "bo": (True, "dve"), "gb": (True, "act"),
        "bn": (True, "dve"), "wo": (True, "dve")}


def q_tiles(l):
    return 4 if l < DEPTH - 1 else 2


def gemm_tiles(l, name):
    if KIND[name][0]:
        return 4
    return q_tiles(l) if name in ("q", "g") else 4


def jobs(l):
    ada = [(0, n) for n in range(4, 12)] + [(1, n) for n in range(4)] if l == 0 else [(1, n) for n in range(4, 12)]
    places = [("nq", 3), ("nk", 1), ("nk", 3), ("nv", 1), ("nv", 3), ("q", 1)]
    places += [("q", 3), ("k", 0), ("k", 1), ("k", 2), ("k", 3), ("v", 0)] if l == 0 else [("k", 0), ("k", 1)]
    out = {p: [("ada",) + a] for p, a in zip(places, ada)}
    for place, (al, n) in zip([("k", 1), ("k", 2), ("v", 1)] if l == 0 else [("k", 2), ("k", 3)], ada[::4]):
        out.setdefault(place, []).append(("col", al, n // 4))
    return out


def job_number(job):
    l, n = job[1:]
    return (n - 4 if l == 0 else 8 + n), (n - 4 if l == 0 else 8 + n if n < 4 else n - 4)


def bank_users(chunks):
    out = []
    for c, (l, name, n) in enumerate(chunks):
        if name in KIND:
            for i in range(gemm_tiles(l, name)):
                out.append(((c, i), 7 if name == "g" else i, KIND[name][1]))
                if n == 0:
                    out += [(job, (i + 2) % 4, "act" if job[0] == "ada" else "dve") for job in jobs(l).get((name, i), [])]
    return out


def bank_tables(chunks):
    count, evac, last, before, number, banks = {"act": 0, "dve": 0}, {}, {}, {}, {}, {}
    for n, (key, bank, e) in enumerate(bank_users(chunks)):
        count[e] += 1
        evac[key], before[key], number[key] = (e, count[e]), last.get(bank), n + 1
        last[bank], banks[key] = key, bank
    return evac, before, number, banks


def build(nc, x, c, ctx, c_ctx, w_ada, b_ada, norm1_w, norm2_w, w_in, w_gk_up, b_gk, gla_norm_w, rpb,
          w_bo_gla, w_bo_na, w_out, w_router, b_router, w1, w3, w2, final_norm_w, consts, out):
    CHUNKS = weight_chunks()
    EVAC, BEFORE, NUMBER, BANK = bank_tables(CHUNKS)
    RING = 2

    with ExitStack() as cm:
        def sb(name, shape, dt=F32):
            return cm.enter_context(nc.sbuf_tensor(name, shape, dt))

        def sem(name):
            return cm.enter_context(nc.semaphore(name))

        U = sb("units", [P, 12, 4096])
        xT = U[:, 0, :].rearrange("p (k t) -> p k t", k=KT)
        hT = U[:, 1, :].rearrange("p (k t) -> p k t", k=KT)
        ring = [U[:, 2 + r, :].rearrange("p (k n) -> p k n", k=8) for r in range(RING)]
        nqT = U[:, 4, 0:2048].rearrange("p (j t) -> p j t", j=4)
        nkT = U[:, 4, 2048:4096].rearrange("p (j t) -> p j t", j=4)
        O = U[:, 4, :].rearrange("p (i n) -> p i n", i=4)
        qk = U[:, 5, :].rearrange("p (a i n) -> p a i n", a=2, i=4)
        qkT = U[:, 6, :].rearrange("p (a h t) -> p a h t", a=2, h=GH)
        V = U[:, 7, :].rearrange("p (i n) -> p i n", i=4)
        gates = U[:, 8, :].rearrange("p (d i n) -> p d i n", d=2, i=4)
        glaT = U[:, 8, :].rearrange("p (k t) -> p k t", k=8)
        Pb = U[:, 9, 0:1024].rearrange("p (b n) -> p b n", b=2)
        PT = U[:, 9, 1024:3072].rearrange("p (b j q) -> p b j q", b=2, j=4)
        rtmp = U[:, 9, 3072:4096].rearrange("p (f n) -> p f n", f=2)
        S = U[:, 9, :].rearrange("p (d s e) -> p d s e", d=2, s=8)
        mT = U[:, 9, :].rearrange("p (k t) -> p k t", k=8)
        nv = U[:, 10, 0:2048].rearrange("p (i n) -> p i n", i=4)
        naT = U[:, 10, 2048:4096].rearrange("p (j t) -> p j t", j=4)
        tmp10 = U[:, 10, 0:2048]
        rt = U[:, 10, 0:1024]
        affT = U[:, 10, 2048:2176]
        attP = tmp10[:, 0:512].rearrange("p (d i t) -> p d i t", d=2, i=4)
        attS = tmp10[:, 512:1024].rearrange("p (i t) -> p i t", i=4)
        junk = tmp10[:, 1024:1280]
        G = U[:, 5, :].rearrange("p (i n) -> p i n", i=4)
        SG = U[:, 11, :].rearrange("p (a i t) -> p a i t", a=2, i=4)
        zero = U[:, 7, 1536:2560]
        bias = U[:, 11, :].rearrange("p (i h k) -> p i h k", i=2, h=NH)
        gt = U[:, 11, :].rearrange("p (d a t) -> p d a t", d=2, a=4)
        h2n = U[:, 11, :].rearrange("p (i n) -> p i n", i=4)
        xload = U[:, 5, :].rearrange("p (i n) -> p i n", i=4)
        adarow = U[:, 7, 2560:4096]
        wada = U[:, 6, :].rearrange("p (k n) -> p k n", k=8)
        wada_first = [U[:, u, :].rearrange("p (k n) -> p k n", k=8) for u in (4, 6, 8, 9)]
        W1 = [U[:, 4:6, :].rearrange("p a (k n) -> p (a k) n", k=4), U[:, 8:10, :].rearrange("p a (k n) -> p (a k) n", k=4)]
        W3 = [U[:, 6:8, :].rearrange("p a (k n) -> p (a k) n", k=4), U[:, 10:12, :].rearrange("p a (k n) -> p (a k) n", k=4)]
        W2 = U[:, 2:4, :].rearrange("p a (k n) -> p (a k) n", k=4)
        xblk = U[:, 1, 0:512]
        xbT = U[:, 1, 512:1024].rearrange("p (c a s) -> p c a s", c=4, a=2)
        xbT_flat = U[:, 1, 512:1024]
        silu_g = U[:, 1, 1024:1536]
        hblk = U[:, 1, 1536:2048]
        hbT = U[:, 1, 2048:2560].rearrange("p (c a s) -> p c a s", c=4, a=2)
        hbT_flat = U[:, 1, 2048:2560]
        yblk = U[:, 1, 2560:3072]
        yg = U[:, 4:6, :].rearrange("p a (b n) -> p (a b) n", b=4)
        z = U[:, 6, :].rearrange("p (i n) -> p i n", i=4)
        fin = U[:, 7, :].rearrange("p (i n) -> p i n", i=4)

        K = sb("constants", [P, 1361])
        ident = K[:, 0:128]
        ones = K[:, 128:256]
        cum = K[:, 256:768].rearrange("p (d a t) -> p d a t", d=2, a=2)
        amask = K[:, 768:896].rearrange("p (d t) -> p d t", d=2)
        strict = K[:, 896:1024]
        rope = K[:, 1024:1280].rearrange("p (f i a e) -> p f i a e", f=2, i=2, a=2)
        cmask = K[:, 1280:1344]
        ramp = K[:, 1344:1360]
        epst = K[:, 1360:1361]
        vrow = U[:, 11, 0:256].rearrange("p (a n) -> p a n", a=2)
        vcol = sb("vector_columns", [P, 128 + 24])
        csil = sb("silu_c", [P, KT, 32])
        mod = sb("modulations", [P, DEPTH, 2, 48])
        s1 = sb("norm_scales", [P, DEPTH, 2, 2, KT])
        lrT = U[0:33, 9, 2048:2560]
        up = sb("gate_up", [33, 2 * 512])
        gnw = sb("gla_norm_w", [P, DV])
        wr = sb("router_w", [P, KT, NE])
        br = sb("router_b", [P, NE])
        dec = sb("chunk_decays", [P, 2, NCH])
        ssq = sb("head_squares", [P, 4, GH])
        st = sb("softmax_stats", [P, 4, 4])
        wsel = sb("choice_weights", [P, 4, 2])
        waited = sb("waited", [1, DEPTH])
        warm = sb("table_loads", [1, 8])
        slot = sb("choice_slots", [P, 4, 2], I32)
        blocks = sb("expert_blocks", [P, 2, NE], I32)

        ps = cm.enter_context(nc.psum_tensor("ps", [P, 8, 512], F32))

        rp = nc.dram_tensor("bias_padded", [DEPTH, NH, 15, RPAD], F32, kind="Internal").ap()
        RW = 2 * GROWS - 1
        rx = nc.dram_tensor("bias_copies", [DEPTH, GRID_W, NH, RW, RPAD], F32, kind="Internal").ap()
        xbuf = nc.dram_tensor("dispatched", [XROWS, D], F32, kind="Internal").ap()
        ybuf = nc.dram_tensor("expert_out", [MAXB * BLK, D], F32, kind="Internal").ap()


        met = sem("compute_engines_met")
        s_const = sem("constants_in")
        s_vec = sem("vectors_in")
        s_x = sem("tokens_in")
        s_rw = sem("router_weights_in")
        s_zero = sem("zeros_made")
        s_zfill = sem("scratch_zeroed")
        s_rp = sem("bias_table_in")
        s_bias = sem("bias_in")
        s_par = sem("layer_vectors_in")
        s_w = [sem(f"weights_in_{r}") for r in range(RING)]
        s_wused = sem("chunk_used")
        s_ada = sem("ada_chunk_in")
        s_ada_first = [sem(f"first_ada_chunk_in_{n}") for n in range(4)]
        a_ps = sem("first_ada_products")
        acc_ready = sem("acc_ready")
        acc_free = {"act": sem("acc_emptied_act"), "dve": sem("acc_emptied_dve")}
        chain = {e: sem("own_steps_" + e) for e in ("act", "dve", "pool")}
        lr_one = sem("lr_ones_row")
        t_x, v_t, v_c = sem("tokens_turned"), sem("vectors_turned"), sem("vectors_copied")
        s_rpz, s_rx = sem("bias_table_zeroed"), sem("bias_copies_made")
        a_sb, a_col = sem("ada_rows_copied"), sem("ada_columns")
        n_sq, n_acc, n_sum, n_root, n_h, n_sh = (sem("norm_" + n) for n in ("squares", "squares_added", "sums", "root", "scaled", "shifted"))
        lr_T, gz, gl, gd = (sem(n) for n in (
            "lrT_copied", "gate_products", "gate_logs", "gates_made"))
        na_sc, na_mx, na_e, na_p, na_tp, na_tc, na_o, na_oc = (sem(n) for n in (
            "na_scores", "na_max", "na_exp", "na_probs", "na_turned", "na_turned_copied", "na_out", "na_out_copied"))
        g_cum, g_exp, g_fac, g_kt, g_ktc, g_att, g_attm, g_ds, g_st, g_o, g_oc = (sem("gla_" + n) for n in (
            "sums", "exps", "factors", "kdecT", "kdec_copied", "att", "att_masked", "delta", "state", "out", "out_copied"))
        g_root, g_silu, g_gated, g_t, g_tc_act, g_tc_dve = (sem("gla_" + n) for n in (
            "root", "silu", "gated", "out_turned", "turned_copied_act", "turned_copied_dve"))
        r_lg, r_aff, r_aT, r_nat, r_natc, r_sel, r_rank, r_slot = (sem("route_" + n) for n in (
            "logits", "affinities", "affinities_turned", "turned", "copied", "selection", "ranks", "slots"))
        moe = [{n: sem(f"{n}_{l}") for n in (
            "x_in", "xT_ps", "xT_sb", "g_ps", "u_ps", "silu", "h_sb", "hT_ps", "hT_sb", "y_ps", "y_sb", "y_out",
            "w1_in0", "w1_in1", "w3_in0", "w3_in1", "w2_in", "scattered")} for l in range(DEPTH)]
        AHEAD = {"h_sb": 1, "hT_ps": 1, "y_ps": 1, "y_sb": 1, "y_out": 32}
        s_gather = [sem(f"gathered_{i}") for i in range(4)]
        c_z, c_t, c_x = sem("combined"), sem("combined_turned"), sem("combined_added")
        f_t, f_c, s_out = sem("final_turned"), sem("final_copied"), sem("stored")

        STAGES = ("mix", "gla", "gate", "merge", "route", "experts", "combine")
        TOKENS_MET, MODS_MET = 3, 6

        def met_at(l, stage):
            return MODS_MET + 3 * (1 + len(STAGES) * l + STAGES.index(stage))

        def arrive(eng):
            eng.drain().then_inc(met, 1)

        def meet(eng, value):
            arrive(eng)
            eng.wait_ge(met, value)

        def chunk_source(l, name, n):
            k8 = "(k p) n -> p k n"
            cols = slice(n * 512, (n + 1) * 512)
            if name == "bo":
                return w_bo_gla[l][:, cols].rearrange(k8, p=P)
            if name == "bn":
                return w_bo_na[l][:, cols].rearrange(k8, p=P)
            if name == "wo":
                return w_out[l][:, cols].rearrange(k8, p=P)
            c0 = {"nq": C_NQ, "nk": C_NK, "nv": C_NV, "q": C_Q, "k": C_K, "lr": C_LR, "v": C_V, "g": C_G,
                  "ga": C_GA, "gb": C_GB}[name] + n * 512
            return w_in[l][:, c0:c0 + (32 if name == "lr" else 512)].rearrange(k8, p=P)

        def chunk_view(cix):
            name, r = CHUNKS[cix][1], ring[cix % RING]
            return r[:, 0:4, :] if name == "bn" else r[:, :, 0:32] if name == "lr" else r

        def chunk_index(l, name, n=0):
            return CHUNKS.index((l, name, n))

        def used(cix):
            l, name, _ = CHUNKS[cix]
            if name in KIND:
                return acc_ready, NUMBER[cix, gemm_tiles(l, name) - 1]
            return s_wused, sum(CHUNKS[k][1] not in KIND for k in range(cix + 1))

        def scan_order(d):
            return [4, 5, 6, 7, 0, 1, 2, 3] if d == 0 else [7, 6, 5, 4, 3, 2, 1, 0]

        def streams(l):
            return [(0, 0, SEQ), (1, SEQ, TOK)][:q_tiles(l) // 2]

        def gate_fill(l, h, place):
            per = q_tiles(l) // 2
            tile = [(chunk_index(l, "g", h // 2), per * (h % 2) + a) for a in range(per)]
            plan = ([(0, 0, 6), (0, 6, 8), (1, 0, 3), (1, 3, 6), (1, 6, 8)] if per == 2 else
                    [(0, 0, 4), (0, 4, 5), (0, 5, 6), (0, 6, 7), (0, 7, 8)])
            t, k0, k1 = plan[place]
            return tile[t] + (k0, k1)

        def na_units(l):
            return [(h, s, i) for h in range(NH) for s in range(q_tiles(l) // 2) for i in range(2)]

        NA0 = [0, len(na_units(0))]
        GT0 = [0, GH * q_tiles(0)]
        NH0 = [0, 16, 32, 48, 56]
        AFTER_COMBINE = [2, 4]
        SQ0 = [0, KT, 2 * KT, 2 * KT + q_tiles(0), 3 * KT + q_tiles(0)]
        QT0 = [0, q_tiles(0)]

        def mix_events(l):
            tiles = [(chunk_index(l, n, j), i) for n, j in (("q", 0), ("k", 0), ("v", 0), ("v", 1))
                     for i in range(gemm_tiles(l, n))]
            steps = len(na_units(l)) + 3
            slots = (len(tiles) - 4) * KT
            ev, t, k0 = [], 0, 0
            for n, tile in enumerate(tiles):
                for k in range(KT):
                    between = []
                    if n < 4:
                        if k in (0, 4):
                            between = [("gates", 2 * n + k // 4, 0)]
                    else:
                        while t < steps * ((n - 4) * KT + k + 1) // slots:
                            between.append(("na", t, 0))
                            t += 1
                    if between:
                        if k > k0:
                            ev.append(("tile",) + tile + (k0, k))
                        ev += between
                        k0 = k
                ev.append(("tile",) + tile + (k0, KT))
                k0 = 0
                if CHUNKS[tile[0]][2] == 0:
                    ev += jobs(l).get((CHUNKS[tile[0]][1], tile[1]), [])
            return ev

        ZFILLS = 16 * ((XROWS + MAXB * BLK) // P)

        block = cm.enter_context(nc.Block())

        @block.sync
        def _(sp):
            sp.dma_start(K[:], consts).then_inc(s_const, 16)
            for l in range(DEPTH):
                for src, r0, r1 in ((b_ada, 0, 48), (norm1_w, 48, 56), (norm2_w, 56, 64)):
                    sp.dma_start(vrow[64 * l + r0:64 * l + r1, 0, :], src[l].rearrange("(m p) -> m p", p=P)).then_inc(s_vec, 16)
            for src, r0 in ((final_norm_w, 0), (c[0], 8), (c_ctx, 16)):
                sp.dma_start(vrow[r0:r0 + 8, 1, :], src.rearrange("(m p) -> m p", p=P)).then_inc(s_vec, 16)
            sp.dma_start(xload[:, 0:2, :], x[0].rearrange("(i p) n -> p i n", p=P)).then_inc(s_x, 16)
            sp.dma_start(xload[:, 2:4, :], ctx[0].rearrange("(i p) n -> p i n", p=P)).then_inc(s_x, 16)
            for n in range(4):
                sp.dma_start(wada_first[n], w_ada[0][:, n * 512:(n + 1) * 512].rearrange("(k p) n -> p k n", p=P)).then_inc(s_ada_first[n], 16)

            def load_chunk(cix):
                if cix >= RING:
                    sp.wait_ge(*used(cix - RING))
                sp.dma_start(chunk_view(cix), chunk_source(*CHUNKS[cix])).then_inc(s_w[cix % RING], 16)

            def load_expert(l, e, which, buf, name):
                w = {"w1": w1, "w3": w3, "w2": w2}[which][l]
                src = w[bass.ds(e, 1)].rearrange("a (k p) n -> p (a k) n", p=P)
                sp.dma_start(buf, src).then_inc(moe[l][name], 16)

            for l in range(DEPTH):
                if l:
                    sp.wait_ge(met, met_at(l - 1, "experts"))
                    for i in range(q_tiles(l - 1)):
                        sp.wait_ge(s_gather[i], 32 * l)
                for cix in range(chunk_index(l, "nq"), chunk_index(l, "wo", 1) + 1):
                    load_chunk(cix)
                    if (l, CHUNKS[cix][1]) == (0, "nq"):
                        sp.dma_start(wr[:], w_router.rearrange("(k p) e -> p k e", p=P)).then_inc(s_rw, 16)
                        sp.dma_start(br[:], b_router.rearrange("(a e) -> a e", a=1).to_broadcast([P, NE])).then_inc(s_rw, 16)
                    if CHUNKS[cix][1] == "gb":
                        sp.wait_ge(met, met_at(l, "gate"))
                        if CHUNKS[cix][2] == 0:
                            load_expert(l, 0, "w1", W1[0], "w1_in0")
                        else:
                            load_expert(l, 0, "w3", W3[0], "w3_in0")
                    if CHUNKS[cix][1] == "nk":
                        if l == 0:
                            sp.wait_ge(met, TOKENS_MET)
                        sp.wait_ge(s_rx, 16 * (l + 1))
                        for r in range(GROWS):
                            for kr in range(GROWS):
                                src = bass.AP(tensor=rx.tensor,
                                              offset=(l * GRID_W * NH * RW + GROWS - 1 - r + kr) * RPAD + GRID_W - 1,
                                              ap=[[NH * RW * RPAD - 1, GRID_W], [RW * RPAD, NH], [1, GRID_W]])
                                sp.dma_start(bias[r % 2 * 64:r % 2 * 64 + 64, r // 2, :, kr * GRID_W:(kr + 1) * GRID_W],
                                             src).then_inc(s_bias, 16)
                        sp.wait_ge(s_zero, 1)
                        for d in range(2):
                            sp.dma_start(up[16 * d:16 * d + 16, 512 * d:512 * d + 512], w_gk_up[l, d]).then_inc(s_par, 16)
                        sp.dma_start(up[32:33, :], b_gk[l].rearrange("(a d) n -> a (d n)", a=1)).then_inc(s_par, 16)
                        sp.dma_start(gnw[:], gla_norm_w[l].rearrange("(a e) -> a e", a=1).to_broadcast([P, DV])).then_inc(s_par, 16)
                m = moe[l]
                sp.wait_ge(met, met_at(l, "merge"))
                load_expert(l, 0, "w2", W2, "w2_in")
                load_expert(l, 1, "w1", W1[1], "w1_in1")
                sp.wait_ge(met, met_at(l, "route"))
                sp.wait_ge(m["scattered"], 16 * 2 * q_tiles(l))
                sp.wait_ge(m["xT_ps"], 1)
                load_expert(l, 1, "w3", W3[1], "w3_in1")
                with sp.Fori(0, NE // 2 - 1) as p:
                    b1 = sp.value_load(blocks[0:1, 1, bass.ds(2 * p + 1, 1)], min_val=1, max_val=MAXB)
                    sp.wait_ge(m["g_ps"], b1)
                    load_expert(l, 2 * p + 2, "w1", W1[0], "w1_in0")
                    sp.wait_ge(m["y_ps"], b1 + 1)
                    load_expert(l, 2 * p + 1, "w2", W2, "w2_in")
                    load_expert(l, 2 * p + 2, "w3", W3[0], "w3_in0")
                    b2 = sp.value_load(blocks[0:1, 1, bass.ds(2 * p + 2, 1)], min_val=1, max_val=MAXB)
                    sp.wait_ge(m["g_ps"], b2)
                    load_expert(l, 2 * p + 3, "w1", W1[1], "w1_in1")
                    sp.wait_ge(m["y_ps"], b2 + 1)
                    load_expert(l, 2 * p + 2, "w2", W2, "w2_in")
                    load_expert(l, 2 * p + 3, "w3", W3[1], "w3_in1")
                b1 = sp.value_load(blocks[0:1, 1, NE - 1:NE], min_val=1, max_val=MAXB)
                sp.wait_ge(m["y_ps"], b1 + 1)
                load_expert(l, NE - 1, "w2", W2, "w2_in")
            sp.wait_ge(f_c, 2)
            sp.dma_start(out[0].rearrange("(i p) n -> p i n", p=P), fin[:, 0:2, :]).then_inc(s_out, 16)
            sp.wait_ge(s_out, 16)

        @block.tensor
        def _(pe):
            def turn(dst, src, n=P):
                return nc.tensor.transpose(dst, src, ident[0:n, 0:n])

            def gemm_tile(cix, i, k0=0, k1=KT):
                l, name, n = CHUNKS[cix]
                w, TQ = chunk_view(cix), q_tiles(l) * P
                if i == 0 and k0 == 0:
                    pe.wait_ge(s_w[cix % RING], 16 * (cix // RING + 1))
                if BEFORE[cix, i] is not None and k0 == 0:
                    e, cnt = EVAC[BEFORE[cix, i]]
                    pe.wait_ge(acc_free[e], cnt)
                kk = 4 if name == "bn" else 8
                for k in range(k0, min(k1, kk)):
                    if KIND[name][0]:
                        src = {"bo": glaT, "bn": naT, "wo": mT}.get(name, hT)
                        N = TOK if name == "nk" else TQ
                        if name == "nq" and i == 0:
                            pe.wait_ge(n_sh, NH0[2 * l] + 2 * k + 2)
                        mm = nc.tensor.matmul(ps[:, i, 0:N], w[:, k, i * P:(i + 1) * P], src[:, k, 0:N],
                                              start=(k == 0), stop=(k == kk - 1), skip_group_check=True)
                    else:
                        mm = nc.tensor.matmul(ps[:, BANK[cix, i], :], hT[:, k, i * P:(i + 1) * P], w[:, k, :],
                                              start=(k == 0), stop=(k == kk - 1), skip_group_check=True)
                if k1 == KT:
                    mm.then_inc(acc_ready, 1)

            def modulate(dst, w):
                for k in range(KT):
                    for j in range(4):
                        mm = nc.tensor.matmul(dst[32 * j:32 * j + 32, :], csil[:, k, :], w[:, k, j * P:(j + 1) * P],
                                              start=(k == 0), stop=(k == KT - 1), skip_group_check=True)
                return mm

            def turn_modulations(dst, a0):
                for n in range(4):
                    mm = turn(dst[:, n * P:(n + 1) * P], adarow[:, (a0 + n) * P:(a0 + n + 1) * P])
                return mm

            def mod_job(job):
                bank = BANK[job]
                if BEFORE[job] is not None:
                    e, cnt = EVAC[BEFORE[job]]
                    pe.wait_ge(acc_free[e], cnt)
                if job[0] == "ada":
                    pe.wait_ge(s_ada, 16 * job_number(job)[0] + 16)
                    modulate(ps[:, bank, 0:P], wada).then_inc(acc_ready, 1)
                else:
                    last = ("ada", job[1], 4 * job[2] + 3)
                    pe.wait_ge(acc_free["act"], EVAC[last][1])
                    turn_modulations(ps[:, bank, :], job_number(("ada", job[1], 4 * job[2]))[1]).then_inc(acc_ready, 1)

            def na_step(l, t):
                u0, units = NA0[l], na_units(l)
                if t < len(units):
                    h, s, i = units[t]
                    hp, k0 = (h % 2) * HD, s * SEQ
                    if u0 + t >= 2:
                        pe.wait_ge(na_e, u0 + t - 1)
                    nc.tensor.matmul(ps[:, 4 + t % 2, k0:TOK], nqT[hp:hp + HD, h // 2, (2 * s + i) * P:(2 * s + i + 1) * P],
                                     nkT[hp:hp + HD, h // 2, k0:TOK], start=True, stop=True).then_inc(na_sc, 1)
                if 0 <= t - 2 < len(units):
                    h, s, i = units[t - 2]
                    pe.wait_ge(na_p, u0 + t - 1)
                    if u0 + t - 2:
                        pe.wait_ge(na_tc, u0 + t - 2)
                    for j in range(2 * s, 4):
                        mm = turn(ps[:, 6, j * P:(j + 1) * P], Pb[:, (t - 2) % 2, j * P:(j + 1) * P])
                    mm.then_inc(na_tp, 1)
                if t - 3 >= 0 and (t - 3) % 2:
                    h, s, i = units[t - 3]
                    hs, hp = (t - 3) // 2, (h % 2) * HD
                    pe.wait_ge(na_tc, u0 + t - 2)
                    if u0 // 2 + hs >= 2:
                        pe.wait_ge(na_oc, u0 // 2 + hs - 1)
                    for j in range(2 * s, 4):
                        mm = nc.tensor.matmul(ps[hp:hp + HD, 7, (hs % 2) * 256:(hs % 2) * 256 + 256],
                                              nv[:, j, h * HD:(h + 1) * HD], PT[:, hs % 2, j, :],
                                              start=(j == 2 * s), stop=(j == 3), skip_group_check=True)
                    mm.then_inc(na_o, 1)

            def gla_head(l, h):
                n, NQC = GH * l + h, 2 * q_tiles(l)
                for d in range(2):
                    if n:
                        pe.wait_ge(g_st, 14 * n)
                    for i in range(4):
                        mm = nc.tensor.matmul(ps[:, 2 * d + i // 2, (i % 2) * 256:(i % 2) * 256 + 256],
                                              gates[:, d, i, h * DK:(h + 1) * DK], cum[:, d].rearrange("p a t -> p (a t)"),
                                              start=True, stop=True)
                    mm.then_inc(g_cum, 1)
                for d in range(2):
                    gemm_tile(*gate_fill(l, h, d))
                    pe.wait_ge(g_fac, 2 * n + d + 1)
                    if d == 0 and n:
                        pe.wait_ge(g_attm, n)
                        pe.wait_ge(g_oc, GT0[l] + h * q_tiles(l))
                    for i in range(4):
                        mm = turn(ps[:, 4 + d, i * P:(i + 1) * P], gt[:, d, 2, i * P:(i + 1) * P])
                    mm.then_inc(g_kt, 1)
                    for cc in range(NQC):
                        t0 = (cc % 2) * CH
                        mm = nc.tensor.matmul(ps[t0:t0 + CH, 6, d * 256 + (cc // 2) * CH:d * 256 + (cc // 2 + 1) * CH],
                                              gt[:, d, 2, cc * CH:(cc + 1) * CH], gt[:, d, 1, cc * CH:(cc + 1) * CH],
                                              start=True, stop=True, skip_group_check=True)
                mm.then_inc(g_att, 1)
                gemm_tile(*gate_fill(l, h, 2))
                pe.wait_ge(g_ktc, 2 * n + 2)
                pe.wait_ge(g_exp, 2 * n + 2)
                for i in range(7):
                    for d in range(2):
                        cc = scan_order(d)[i]
                        t0 = (cc % 2) * CH
                        if i >= 2:
                            pe.wait_ge(g_st, 14 * n + 2 * (i - 2) + d + 1)
                        b = ps[:, 2 * d + i % 2, 0:DV]
                        nc.tensor.matmul(b, gt[t0:t0 + CH, d, 3, (cc // 2) * P:(cc // 2 + 1) * P],
                                         V[t0:t0 + CH, cc // 2, h * DV:(h + 1) * DV],
                                         start=True, stop=True, skip_group_check=True).then_inc(g_ds, 1)
                gemm_tile(*gate_fill(l, h, 3))
                pe.wait_ge(g_attm, n + 1)
                pe.wait_ge(g_st, 14 * n + 14)
                for i in range(q_tiles(l)):
                    o = GT0[l] + h * q_tiles(l) + i
                    if o >= 2:
                        pe.wait_ge(g_oc, o - 1)
                    dst = ps[:, 4 + i % 2, 0:DV]
                    nc.tensor.matmul(dst, attS[:, i, :], V[:, i, h * DV:(h + 1) * DV], start=True, stop=False,
                                     skip_group_check=True)
                    for cc in (2 * i, 2 * i + 1):
                        t0 = (cc % 2) * CH
                        ds_ = [d for d in range(2) if scan_order(d).index(cc)]
                        for d in ds_:
                            mm = nc.tensor.matmul(dst[t0:t0 + CH, :], gt[:, d, 0, cc * CH:(cc + 1) * CH],
                                                  S[:, d, scan_order(d).index(cc), :], start=False, stop=(d == ds_[-1]),
                                                  skip_group_check=True)
                    mm.then_inc(g_o, 1)
                gemm_tile(*gate_fill(l, h, 4))

            def norm_sum(n, T):
                pe.wait_ge(n_acc, n + 1)
                nc.tensor.matmul(ps[:, 7, 0:T], ones, hT[:, 0, 0:T], start=True, stop=True).then_inc(n_sum, 1)

            pe.wait_ge(s_const, 16)
            pe.wait_ge(s_vec, 16 * 9)
            turn(ps[:, 0, 0:128], vrow[:, 0, :])
            turn(ps[:, 0, 128:152], vrow[0:24, 1, :], 24).then_inc(v_t, 1)
            pe.wait_ge(s_x, 32)
            for k in range(KT):
                if k == 0:
                    pe.wait_ge(v_c, 1)
                for i in range(4):
                    mm = turn(ps[:, k, i * P:(i + 1) * P], xload[:, i, k * P:(k + 1) * P])
                mm.then_inc(t_x, 1)
            meet(pe, TOKENS_MET)
            norm_sum(0, TOK)

            for l in range(DEPTH):
                m, TQ, NQ = moe[l], q_tiles(l) * P, q_tiles(l)
                if l == 0:
                    for n in range(4):
                        pe.wait_ge(s_ada_first[n], 16)
                        modulate(ps[:, 0, n * P:(n + 1) * P], wada_first[n]).then_inc(a_ps, 1)
                    pe.wait_ge(a_sb, 1)
                    turn_modulations(ps[:, 3, :], 0).then_inc(a_col, 1)
                    meet(pe, MODS_MET)
                else:
                    norm_sum(2 * l, TOK)

                def project(name):
                    for i in range(gemm_tiles(l, name)):
                        gemm_tile(chunk_index(l, name), i)
                        for job in jobs(l).get((name, i), []):
                            mod_job(job)

                def gate_tile(u):
                    d, i = u % 2, u // 2
                    if u == 0:
                        pe.wait_ge(lr_T, l + 1)
                        pe.wait_ge(lr_one, l + 1)
                        pe.wait_ge(s_par, 64 * (l + 1))
                    if 8 * l + u >= 2:
                        pe.wait_ge(gd, 8 * l + u - 1)
                    nc.tensor.matmul(ps[:, 4 + u % 2, :], lrT[:, i * P:(i + 1) * P], up[:, 512 * d:512 * d + 512],
                                     start=True, stop=True).then_inc(gz, 1)

                project("nq")
                project("nk")
                cix = chunk_index(l, "lr")
                pe.wait_ge(s_w[cix % RING], 16 * (cix // RING + 1))
                for k in range(KT):
                    mm = nc.tensor.matmul(ps[0:32, 7, :], chunk_view(cix)[:, k, :], hT[:, k, :],
                                          start=(k == 0), stop=(k == KT - 1))
                mm.then_inc(s_wused, 1)
                project("nv")
                for ev, a, b, *part in mix_events(l):
                    if ev == "tile":
                        gemm_tile(a, b, *part)
                    elif ev == "gates":
                        gate_tile(a)
                    elif ev != "na":
                        mod_job((ev, a, b))
                    else:
                        if a == 0:
                            pe.wait_ge(gd, 8 * l + 8)
                            pe.wait_ge(acc_free["act"], EVAC[chunk_index(l, "nv"), 3][1])
                            pe.wait_ge(acc_free["dve"], EVAC[chunk_index(l, "nk"), 3][1])
                        na_step(l, a)
                for a in range(2):
                    T = TQ if a == 0 else TOK
                    pe.wait_ge(acc_free["dve"], EVAC[chunk_index(l, "k"), 3][1])
                    for h in range(GH):
                        b = 4 * a + h
                        if a == 0:
                            if h == 0:
                                pe.wait_ge(acc_free["act"], EVAC[chunk_index(l, "v", 1), 3][1])
                                pe.wait_ge(na_oc, (NA0[l] + len(na_units(l))) // 2)
                        for i in range(T // P):
                            mm = turn(ps[:, b, i * P:(i + 1) * P], qk[:, a, i, h * DK:(h + 1) * DK])
                        mm.then_inc(g_t, 1)
                meet(pe, met_at(l, "mix"))
                for h in range(GH):
                    gla_head(l, h)
                arrive(pe)
                for i in range(4):
                    gemm_tile(chunk_index(l, "ga", 0), i)
                pe.wait_ge(met, met_at(l, "gla"))
                for k in range(8):
                    pe.wait_ge(g_gated, GH * l + k // 2 + 1)
                    if k >= 4:
                        pe.wait_ge((g_tc_act, g_tc_dve)[k % 2], 4 * l + (k - 4) // 2 + 1)
                    for i in range(NQ):
                        mm = turn(ps[:, 4 + k % 4, i * P:(i + 1) * P], O[:, i, k * P:(k + 1) * P])
                    mm.then_inc(g_t, 1)
                meet(pe, met_at(l, "gate"))
                for name, j in (("bo", 0), ("gb", 0), ("bn", 0), ("ga", 1), ("bo", 1), ("gb", 1), ("bn", 1)):
                    for i in range(4):
                        gemm_tile(chunk_index(l, name, j), i)
                pe.wait_ge(acc_free["dve"], EVAC[chunk_index(l, "bn", 1), 3][1])
                for k in range(KT):
                    gemm_tile(chunk_index(l, "wo", k // 4), k % 4)
                norm_sum(2 * l + 1, TQ)
                meet(pe, met_at(l, "merge"))

                pe.wait_ge(s_rw, 32)
                for k in range(KT):
                    pe.wait_ge(n_sh, NH0[2 * l + 1] + (k + 1) * (TQ // SEQ))
                    for i in range(NQ):
                        mm = nc.tensor.matmul(ps[32 * i:32 * i + NE, 0, 0:P], wr[:, k, :], hT[:, k, i * P:(i + 1) * P],
                                              start=(k == 0), stop=(k == KT - 1), skip_group_check=True)
                mm.then_inc(r_lg, 1)
                for i in range(NQ):
                    b = 1 + 2 * (i % 3)
                    if i >= 3:
                        pe.wait_ge(r_natc, QT0[l] + i - 2)
                    for k in range(KT):
                        mm = turn(ps[:, b + k // 4, (k % 4) * P:(k % 4 + 1) * P], hT[:, k, i * P:(i + 1) * P])
                    mm.then_inc(r_nat, 1)
                    if i == 0:
                        pe.wait_ge(r_aff, l + 1)
                        turn(ps[:, 0, P:2 * P], affT).then_inc(r_aT, 1)
                pe.wait_ge(r_sel, l + 1)
                M = rt[:, 0:NQ * NE]
                nc.tensor.matmul(ps[:, 7, 0:NQ * NE], strict, M, start=True, stop=False, skip_group_check=True)
                for j in range(NQ - 1):
                    n = NQ - 1 - j
                    nc.tensor.matmul(ps[:, 7, (j + 1) * NE:NQ * NE].rearrange("p (a e) -> p a e", a=n), ones,
                                     M[:, j * NE:(j + 1) * NE].rearrange("p (a e) -> p a e", a=1).to_broadcast([P, n, NE]),
                                     start=False, stop=(n == 1), skip_group_check=True)
                for j in range(NQ):
                    mm = nc.tensor.matmul(ps[:, 7, 64:64 + NE], ones, M[:, j * NE:(j + 1) * NE],
                                          start=(j == 0), stop=(j == NQ - 1), skip_group_check=True)
                mm.then_inc(r_rank, 1)
                meet(pe, met_at(l, "route"))

                def turn_block(b):
                    pe.wait_ge(m["x_in"], 32 * b + 32)
                    for cc in range(4):
                        mm = turn(ps[:, 0, cc * P:(cc + 1) * P], xblk[:, cc * P:(cc + 1) * P])
                    mm.then_inc(m["xT_ps"], 1)

                def expert_block(b, p, par):
                    pe.wait_ge(m["xT_sb"], b + 1)
                    pe.wait_ge(m[f"w1_in{par}"], 16 * p + 16)
                    for k in range(KT):
                        for a in range(2):
                            mm = nc.tensor.matmul(ps[64 * a:64 * a + 64, 1, :], xbT[:, k % 4, k // 4, :],
                                                  W1[par][:, k, a * 512:(a + 1) * 512], start=(k == 0), stop=(k == KT - 1),
                                                  skip_group_check=True)
                    mm.then_inc(m["g_ps"], 1)
                    pe.wait_ge(m[f"w3_in{par}"], 16 * p + 16)
                    for part in range(2):
                        for k in range(KT):
                            for a in range(2):
                                c0 = a * 512 + part * 256
                                mm = nc.tensor.matmul(ps[64 * a:64 * a + 64, (2, 5)[part], 0:256], xbT[:, k % 4, k // 4, :],
                                                      W3[par][:, k, c0:c0 + 256], start=(k == 0), stop=(k == KT - 1),
                                                      skip_group_check=True)
                        mm.then_inc(m["u_ps"], 1)
                    for part in range(2):
                        if part:
                            turn_block(b + 1)
                        pe.wait_ge(m["h_sb"], 2 * b + (part + 2))
                        for cc in range(2):
                            mm = turn(ps[:, (3, 6)[part], cc * P:(cc + 1) * P], hblk[:, (2 * part + cc) * P:(2 * part + cc + 1) * P])
                        mm.then_inc(m["hT_ps"], 1)
                    pe.wait_ge(m["y_sb"], b + 1)
                    pe.wait_ge(m["w2_in"], 32 * p + 16 * par + 16)
                    for part in range(2):
                        pe.wait_ge(m["hT_sb"], 2 * b + (part + 1))
                        for k in (2 * part, 2 * part + 1, 2 * part + 4, 2 * part + 5):
                            for a in range(2):
                                mm = nc.tensor.matmul(ps[64 * a:64 * a + 64, 4, :], hbT[:, k % 4, k // 4, :],
                                                      W2[:, k, a * 512:(a + 1) * 512], start=(k == 0), stop=(k == KT - 1),
                                                      skip_group_check=True)
                    mm.then_inc(m["y_ps"], 1)

                for name in AHEAD:
                    pe.sem_inc(m[name], AHEAD[name])
                turn_block(0)
                with pe.Fori(0, NE // 2) as p:
                    for par in range(2):
                        b1 = pe.value_load(blocks[0:1, 0, bass.ds(2 * p + par, 1)], min_val=1, max_val=MAXB)
                        b0 = pe.value_load(blocks[0:1, 1, bass.ds(2 * p + par, 1)], min_val=0, max_val=MAXB)
                        with pe.Fori(b0, b1) as b:
                            expert_block(b, p, par)
                meet(pe, met_at(l, "experts"))
                for i in range(NQ):
                    pe.wait_ge(c_z, QT0[l] + i + 1)
                    for k in range(KT):
                        mm = turn(ps[:, 2 * i + k // 4, (k % 4) * P:(k % 4 + 1) * P], z[:, i, k * P:(k + 1) * P])
                    mm.then_inc(c_t, 1)
                meet(pe, met_at(l, "combine"))

            norm_sum(2 * DEPTH, SEQ)
            pe.wait_ge(n_h, NH0[2 * DEPTH] + KT)
            for i in range(2):
                for k in range(KT):
                    mm = turn(ps[:, 2 * i + k // 4, (k % 4) * P:(k % 4 + 1) * P], hT[:, k, i * P:(i + 1) * P])
                mm.then_inc(f_t, 1)

        @block.scalar
        def _(act):
            own = [0]

            def link(ins):
                own[0] += 1
                ins.then_inc(chain["act"], 1)
                act.wait_ge(chain["act"], own[0])

            def evacuate(cix, i):
                l, name, n = CHUNKS[cix]
                TQ = q_tiles(l) * P
                act.wait_ge(acc_ready, NUMBER[cix, i])
                if name == "nq":
                    ins = nc.scalar.activation(nqT[:, i, 0:TQ], ps[:, i, 0:TQ], ACT.Copy, scale=HD ** -0.5)
                elif name == "nv":
                    ins = nc.scalar.activation(nv[:, i, :], ps[:, i, :], ACT.Copy)
                elif name == "v":
                    if (l, n, i) == (0, 0, 0):
                        act.wait_ge(s_zfill, ZFILLS)
                    ins = nc.scalar.activation(V[:, i, n * 512:(n + 1) * 512], ps[:, i, :], ACT.Copy)
                elif name == "g":
                    ins = nc.scalar.activation(G[:, i, n * 512:(n + 1) * 512], ps[:, BANK[cix, i], :], ACT.Copy)
                else:
                    a = 0 if name == "ga" else 1
                    if n:
                        act.wait_ge(acc_free["dve"], EVAC[chunk_index(l, ("bo", "bn")[a], 0), i][1])
                    ins = nc.scalar.activation(SG[:, a, i, 0:TQ], ps[:, i, 0:TQ], ACT.Sigmoid)
                ins.then_inc(acc_free["act"], 1)

            def load_ada(l, n):
                act.dma_start(wada, w_ada[l][:, n * 512:(n + 1) * 512].rearrange("(k p) n -> p k n", p=P)).then_inc(s_ada, 16)

            def mod_job(l, job):
                act.wait_ge(acc_ready, NUMBER[job])
                place = job_number(job)[1]
                nc.scalar.activation(adarow[:, place * P:(place + 1) * P], ps[:, BANK[job], 0:P], ACT.Copy).then_inc(acc_free["act"], 1)
                todo = [j[0] for j in jobs(l).values() if j[0][0] == "ada"]
                if todo.index(job) + 1 < len(todo):
                    load_ada(*todo[todo.index(job) + 1][1:])

            def na_step(l, t):
                u0, units = NA0[l], na_units(l)
                if t < len(units):
                    h, s, i = units[t]
                    act.wait_ge(na_mx, u0 + t + 1)
                    if u0 + t >= 2:
                        act.wait_ge(na_tp, u0 + t - 1)
                    nc.scalar.activation(Pb[:, t % 2, s * SEQ:TOK], ps[:, 4 + t % 2, s * SEQ:TOK], ACT.Exp,
                                         bias=st[:, t % 4, 0:1], accum_out=st[:, t % 4, 1:2]).then_inc(na_e, 1)
                if 0 <= t - 2 < len(units):
                    h, s, i = units[t - 2]
                    hs = (t - 2) // 2
                    act.wait_ge(na_tp, u0 + t - 1)
                    if u0 // 2 + hs >= 2:
                        act.wait_ge(na_o, u0 // 2 + hs - 1)
                    nc.scalar.activation(PT[:, hs % 2, 2 * s:4, i * P:(i + 1) * P],
                                         ps[:, 6, 2 * s * P:4 * P].rearrange("p (j q) -> p j q", q=P),
                                         ACT.Copy).then_inc(na_tc, 1)
                if t - 3 >= 0 and (t - 3) % 2:
                    h, s, i = units[t - 3]
                    hs, hp = (t - 3) // 2, (h % 2) * HD
                    act.wait_ge(na_o, u0 // 2 + hs + 1)
                    nc.scalar.activation(naT[hp:hp + HD, h // 2, s * SEQ:s * SEQ + SEQ],
                                         ps[hp:hp + HD, 7, (hs % 2) * 256:(hs % 2) * 256 + 256], ACT.Copy).then_inc(na_oc, 1)

            def load_table(j, function):
                nc.scalar.activation(warm[:, j:j + 1], epst[0:1, :], function)

            def norm_root(n, T):
                for k in range(0 if n in AFTER_COMBINE else KT):
                    if n % 2:
                        act.wait_ge(acc_free["dve"], EVAC[chunk_index(n // 2, "wo", k // 4), k % 4][1])
                    nc.scalar.activation(hT[:, k, 0:T], xT[:, k, 0:T], ACT.Square).then_inc(n_sq, 1)
                load_table(n, ACT.Sqrt)
                act.wait_ge(n_sum, n + 1)
                nc.scalar.activation(tmp10[:, 0:T], ps[:, 7, 0:T], ACT.Sqrt, scale=1.0 / D, bias=epst).then_inc(n_root, 1)

            def norm_shift(n, T, l, row):
                for k in range(KT):
                    for s, a, b in ((0, 0, SEQ), (1, SEQ, TOK)):
                        if a < T:
                            act.wait_ge(n_h, NH0[n] + k * (T // SEQ) + s + 1)
                            nc.scalar.activation(hT[:, k, a:b], hT[:, k, a:b], ACT.Identity,
                                                 bias=mod[:, l, s, row * 8 + k:row * 8 + k + 1]).then_inc(n_sh, 1)

            act.wait_ge(v_c, 1)
            nc.scalar.activation(csil[:, :, 0:2].rearrange("p k s -> p s k"),
                                 vcol[:, 136:152].rearrange("p (s k) -> p s k", s=2), ACT.Silu)
            act.wait_ge(t_x, 8)
            nc.scalar.activation(xT[:, 4:8, :], ps[:, 4:8, :], ACT.Copy)
            meet(act, TOKENS_MET)
            norm_root(0, TOK)
            for l in range(DEPTH):
                m, TQ, NQ = moe[l], q_tiles(l) * P, q_tiles(l)
                if l == 0:
                    act.wait_ge(a_ps, 4)
                    nc.scalar.activation(adarow[:, 0:512], ps[:, 0, :], ACT.Copy).then_inc(a_sb, 1)
                    meet(act, MODS_MET)
                else:
                    norm_root(2 * l, TOK)
                norm_shift(2 * l, TOK, l, 0)

                load_ada(*[j[0] for j in jobs(l).values()][0][1:])
                for name in ("nq", "nk", "nv"):
                    if name == "nv":
                        act.wait_ge(*used(chunk_index(l, "lr")))
                        nc.scalar.activation(lrT[0:32, :], ps[0:32, 7, :], ACT.Copy).then_inc(lr_T, 1)
                    for i in range(gemm_tiles(l, name)):
                        if name != "nk":
                            evacuate(chunk_index(l, name), i)
                        for job in jobs(l).get((name, i), []):
                            mod_job(l, job)

                def gate_tile(u):
                    act.wait_ge(gz, 8 * l + u + 1)
                    g = gates[:, u % 2, u // 2, :]
                    link(nc.scalar.activation(g, ps[:, 4 + u % 2, :], ACT.Abs))
                    link(nc.scalar.activation(g, g, ACT.Exp, scale=-1.0))
                    nc.scalar.activation(g, g, ACT.Ln, bias=1.0).then_inc(gl, 1)

                for ev, a, b, *part in mix_events(l):
                    if ev == "na":
                        na_step(l, a)
                    elif ev == "gates":
                        gate_tile(a)
                    elif ev == "ada":
                        mod_job(l, (ev, a, b))
                    elif ev == "tile" and part[1] == KT and KIND[CHUNKS[a][1]][1] == "act":
                        evacuate(a, b)
                for h in range(GH):
                    act.wait_ge(g_t, 16 * l + h + 1)
                    nc.scalar.activation(qkT[:, 0, h, 0:TQ], ps[:, h, 0:TQ], ACT.Copy, scale=DK ** -0.5)
                meet(act, met_at(l, "mix"))

                for h in range(GH):
                    n = GH * l + h
                    for d in range(2):
                        act.wait_ge(g_cum, 2 * n + d + 1)
                        if h:
                            act.wait_ge(g_o, GT0[l] + h * NQ)
                        v = ps[:, 2 * d:2 * d + 2, :].rearrange("p b (i a t) -> p (b i) a t", i=2, a=2)
                        for slot_, a, scale in ((0, 0, 1 / TAU), (1, 1, -1 / TAU), (2, 1, 1 / TAU)):
                            ins = nc.scalar.activation(gt[:, d, slot_, :].rearrange("p (i t) -> p i t", i=4), v[:, :, a, :],
                                                       ACT.Exp, scale=scale)
                        ins.then_inc(g_exp, 1)
                    for d in range(2):
                        act.wait_ge(g_kt, 2 * n + d + 1)
                        nc.scalar.activation(gt[:, d, 3, :], ps[:, 4 + d, :], ACT.Copy).then_inc(g_ktc, 1)
                        if d == 0 and NQ == 4:
                            evacuate(*gate_fill(l, h, 1)[:2])
                    for i in range(NQ):
                        o = GT0[l] + h * NQ + i
                        act.wait_ge(g_o, o + 1)
                        src = ps[:, 4 + i % 2, 0:DV]
                        nc.scalar.activation(O[:, i, h * DV:(h + 1) * DV], src, ACT.Copy)
                        if h or i:
                            act.wait_ge(g_oc, o)
                        nc.scalar.activation(junk, src, ACT.Square, accum_out=ssq[:, i, h:h + 1]).then_inc(g_oc, 1)
                    last = gate_fill(l, h, 4)[:2]
                    evacuate(*last)
                    act.wait_ge(acc_free["act"], EVAC[last][1])
                    i0, i1, c0 = gate_fill(l, h, 0)[1], last[1] + 1, h // 2 * 512
                    nc.scalar.activation(G[:, i0:i1, c0:c0 + 512], G[:, i0:i1, c0:c0 + 512], ACT.Silu).then_inc(g_silu, 1)
                meet(act, met_at(l, "gla"))
                nc.scalar.activation(ssq[:, 0:NQ, :], ssq[:, 0:NQ, :], ACT.Sqrt, scale=1.0 / DV, bias=epst).then_inc(g_root, 1)
                for i in range(4):
                    evacuate(chunk_index(l, "ga", 0), i)
                for k in range(0, 8, 2):
                    act.wait_ge(g_t, 16 * l + 8 + k + 1)
                    nc.scalar.activation(glaT[:, k, 0:TQ], ps[:, 4 + k % 4, 0:TQ], ACT.Copy).then_inc(g_tc_act, 1)
                meet(act, met_at(l, "gate"))
                for name, j in (("gb", 0), ("ga", 1), ("gb", 1)):
                    for i in range(4):
                        evacuate(chunk_index(l, name, j), i)
                norm_root(2 * l + 1, TQ)
                meet(act, met_at(l, "merge"))
                norm_shift(2 * l + 1, TQ, l, 3)

                load_table(5 + l, ACT.Sigmoid)
                act.wait_ge(r_lg, l + 1)
                for i in range(NQ):
                    g = slice(32 * i, 32 * i + NE)
                    ins = nc.scalar.activation(affT[g, :], ps[g, 0, 0:P], ACT.Sigmoid)
                ins.then_inc(r_aff, 1)
                for i in range(NQ):
                    act.wait_ge(r_nat, QT0[l] + i + 1)
                    b = 1 + 2 * (i % 3)
                    nc.scalar.activation(h2n[:, i, :], ps[:, b:b + 2, :].rearrange("p b n -> p (b n)"), ACT.Copy).then_inc(r_natc, 1)
                meet(act, met_at(l, "route"))

                with act.Fori(0, NE) as e:
                    b1 = act.value_load(blocks[0:1, 0, bass.ds(e, 1)], min_val=1, max_val=MAXB)
                    b0 = act.value_load(blocks[0:1, 1, bass.ds(e, 1)], min_val=0, max_val=MAXB)
                    with act.Fori(b0, b1) as b:
                        act.wait_ge(m["g_ps"], b + 1)
                        act.wait_ge(m["h_sb"], 2 * b + 1)
                        nc.scalar.activation(silu_g, ps[:, 1, :], ACT.Silu).then_inc(m["silu"], 1)
                        act.wait_ge(m["y_ps"], b + 1)
                        for part in range(2):
                            act.wait_ge(m["hT_ps"], 2 * b + (part + 2))
                            nc.scalar.activation(hbT_flat[:, part * 256:part * 256 + 256], ps[:, (3, 6)[part], 0:256],
                                                 ACT.Copy).then_inc(m["hT_sb"], 1)
                        act.wait_ge(m["y_sb"], b + 2)
                        for a in range(2):
                            act.dma_start(ybuf[bass.ds(b * BLK, BLK), 512 * a:512 * a + 512], yblk[64 * a:64 * a + 64, :]).then_inc(m["y_out"], 16)
                meet(act, met_at(l, "experts"))
                for i in range(NQ):
                    act.wait_ge(c_x, QT0[l] + i + 1)
                    nc.scalar.activation(hT[:, :, i * P:(i + 1) * P], xT[:, :, i * P:(i + 1) * P], ACT.Square).then_inc(n_sq, 1)
                meet(act, met_at(l, "combine"))
            norm_root(2 * DEPTH, SEQ)
            for i in range(2):
                act.wait_ge(f_t, i + 1)
                nc.scalar.activation(fin[:, i, :], ps[:, 2 * i:2 * i + 2, :].rearrange("p b n -> p (b n)"), ACT.Copy).then_inc(f_c, 1)

        @block.vector
        def _(dve):
            own = [0]

            def link(ins):
                own[0] += 1
                ins.then_inc(chain["dve"], 1)
                dve.wait_ge(chain["dve"], own[0])

            def evacuate(cix, i):
                l, name, n = CHUNKS[cix]
                TQ = q_tiles(l) * P
                dve.wait_ge(acc_ready, NUMBER[cix, i])
                src = ps[:, i, :]
                if name == "nk":
                    ins = nc.vector.tensor_copy(nkT[:, i, :], src)
                elif name in ("q", "k"):
                    dst = qk[:, 0 if name == "q" else 1, i, :]
                    if i >= 2:
                        ins = nc.vector.tensor_copy(dst, src)
                    else:
                        dve.wait_ge(acc_free["dve"], EVAC[cix, i][1] - 1)
                        t = rtmp.rearrange("p f (h a u e) -> p f h a u e", h=GH, a=2, u=2)
                        sv = src.rearrange("p (h a u e) -> p h a u e", h=GH, a=2, u=2)
                        dv = dst.rearrange("p (h a u e) -> p h a u e", h=GH, a=2, u=2)
                        for f in range(2):
                            for u in range(2):
                                for a in range(2):
                                    ins = nc.vector.tensor_tensor(t[:, f, :, a, u, :], sv[:, :, a, u, :],
                                                                  rope[:, f, i, a:a + 1, :].to_broadcast([P, GH, 32]), ALU.mult)
                        link(ins)
                        for a in range(2):
                            nc.vector.tensor_tensor(dv[:, :, a, 0, :], t[:, 0, :, a, 0, :], t[:, 1, :, a, 1, :], ALU.subtract)
                            ins = nc.vector.tensor_tensor(dv[:, :, a, 1, :], t[:, 1, :, a, 0, :], t[:, 0, :, a, 1, :], ALU.add)
                elif name == "bo":
                    dve.wait_ge(acc_free["act"], EVAC[chunk_index(l, "ga", n), i][1])
                    ins = nc.vector.tensor_tensor(mT[:, 4 * n + i, 0:TQ], SG[:, 0, i, 0:TQ], src[:, 0:TQ], ALU.mult)
                elif name == "bn":
                    dve.wait_ge(acc_free["act"], EVAC[chunk_index(l, "gb", n), i][1])
                    link(nc.vector.tensor_tensor(SG[:, 1, i, 0:TQ], SG[:, 1, i, 0:TQ], src[:, 0:TQ], ALU.mult))
                    ins = nc.vector.tensor_tensor(mT[:, 4 * n + i, 0:TQ], mT[:, 4 * n + i, 0:TQ], SG[:, 1, i, 0:TQ], ALU.add)
                else:
                    k = 4 * n + i
                    for s, a, b in streams(l):
                        ins = nc.vector.scalar_tensor_tensor(out=xT[:, k, a:b], in0=src[:, a:b],
                                                             scalar=mod[:, l, s, 16 + k:17 + k], in1=xT[:, k, a:b],
                                                             op0=ALU.mult, op1=ALU.add)
                ins.then_inc(acc_free["dve"], 1)

            def na_step(l, t):
                u0, units = NA0[l], na_units(l)
                if t < len(units):
                    h, s, i = units[t]
                    dve.wait_ge(na_sc, u0 + t + 1)
                    bank = ps[:, 4 + t % 2, :]
                    if s == 0:
                        link(nc.vector.tensor_tensor(bank[:, 0:SEQ], bank[:, 0:SEQ], bias[:, i, h, :], ALU.add))
                    nc.vector.tensor_reduce(st[:, t % 4, 0:1], bank[:, s * SEQ:TOK], AX, ALU.max, negate=True).then_inc(na_mx, 1)
                if 0 <= t - 1 < len(units):
                    h, s, i = units[t - 1]
                    dve.wait_ge(na_e, u0 + t)
                    link(nc.vector.reciprocal(st[:, (t - 1) % 4, 2:3], st[:, (t - 1) % 4, 1:2]))
                    p = Pb[:, (t - 1) % 2, s * SEQ:TOK]
                    nc.vector.tensor_scalar(p, p, st[:, (t - 1) % 4, 2:3], None, ALU.mult).then_inc(na_p, 1)

            def norm_add(n, T, k):
                dve.wait_ge(n_sq, SQ0[n] + k + 1)
                ins = nc.vector.tensor_tensor(hT[:, 0, 0:T], hT[:, 0, 0:T], hT[:, k, 0:T], ALU.add)
                if k < KT - 1:
                    link(ins)
                else:
                    ins.then_inc(n_acc, 1)

            def norm_inverse(n, T):
                if n == 0:
                    for k in range(1, KT):
                        norm_add(n, T, k)
                dve.wait_ge(n_root, n + 1)
                link(nc.vector.reciprocal(tmp10[:, 512:512 + T], tmp10[:, 0:T]))

            def norm_scale(n, T, scale):
                for k in range(KT):
                    for s, a, b in ((0, 0, SEQ), (1, SEQ, TOK)):
                        if a < T:
                            nc.vector.scalar_tensor_tensor(out=hT[:, k, a:b], in0=xT[:, k, a:b], scalar=scale(s, k),
                                                           in1=tmp10[:, 512 + a:512 + b], op0=ALU.mult,
                                                           op1=ALU.mult).then_inc(n_h, 1)

            def modulations(l, q, bank):
                col = bank.rearrange("p (m s) -> p m s", s=32)
                for s in range(2):
                    ins = nc.vector.tensor_tensor(mod[:, l, s, 16 * q:16 * q + 16], col[:, :, s],
                                                  vcol[:, 64 * l + 16 * q:64 * l + 16 * q + 16], ALU.add)
                return ins

            def scales(l, q):
                if q == 1:
                    return
                w = q // 2
                row = (1, 4)[w] * 8
                for s in range(2):
                    nc.vector.scalar_tensor_tensor(out=s1[:, l, w, s, :], in0=mod[:, l, s, row:row + 8], scalar=1.0,
                                                   in1=vcol[:, 64 * l + 48 + 8 * w:64 * l + 56 + 8 * w],
                                                   op0=ALU.add, op1=ALU.mult)

            link(nc.vector.memset(csil[:], 0.0))
            nc.vector.memset(up[0:32, :], 0.0).then_inc(s_zero, 1)
            dve.wait_ge(v_t, 1)
            nc.vector.tensor_copy(vcol[:], ps[:, 0, 0:152]).then_inc(v_c, 1)
            dve.wait_ge(t_x, 4)
            nc.vector.tensor_copy(xT[:, 0:4, :], ps[:, 0:4, :])
            meet(dve, TOKENS_MET)
            norm_inverse(0, TOK)
            for l in range(DEPTH):
                m, TQ, NQ = moe[l], q_tiles(l) * P, q_tiles(l)
                if l == 0:
                    dve.wait_ge(a_col, 1)
                    link(modulations(0, 0, ps[:, 3, :]))
                    scales(0, 0)
                    meet(dve, MODS_MET)
                else:
                    norm_inverse(2 * l, TOK)
                norm_scale(2 * l, TOK, lambda s, k: s1[:, l, 0, s, k:k + 1])

                nc.vector.memset(lrT[32:33, :], 1.0).then_inc(lr_one, 1)
                for i in range(4):
                    evacuate(chunk_index(l, "nk"), i)
                dve.wait_ge(s_bias, 256 * (l + 1))
                for i in range(2):
                    v = bias[:, i].rearrange("p h (r k) -> p (h r) k", r=GROWS)
                    ins = nc.vector.tensor_tensor(v, v, cmask.rearrange("p (a k) -> p a k", a=1).to_broadcast([P, NH * GROWS, GRID_W]), ALU.add)
                link(ins)
                for ev, a, b, *part in mix_events(l):
                    if ev == "na":
                        na_step(l, a)
                    elif ev == "gates":
                        g = gates[:, a % 2, a // 2, :]
                        dve.wait_ge(gl, 8 * l + a + 1)
                        nc.vector.scalar_tensor_tensor(out=g, in0=ps[:, 4 + a % 2, :], scalar=0.0, in1=g,
                                                       op0=ALU.min, op1=ALU.subtract).then_inc(gd, 1)
                    elif ev == "col":
                        dve.wait_ge(acc_ready, NUMBER[ev, a, b])
                        modulations(a, b, ps[:, BANK[ev, a, b], :]).then_inc(acc_free["dve"], 1)
                        dve.wait_ge(acc_free["dve"], EVAC[ev, a, b][1])
                        scales(a, b)
                    elif ev == "tile" and part[1] == KT and KIND[CHUNKS[a][1]][1] == "dve":
                        evacuate(a, b)
                for h in range(GH):
                    dve.wait_ge(g_t, 16 * l + GH + h + 1)
                    nc.vector.tensor_copy(qkT[:, 1, h, :], ps[:, 4 + h, :])
                meet(dve, met_at(l, "mix"))

                link(nc.vector.memset(attS, 0.0))
                for h in range(GH):
                    n = GH * l + h
                    for d in range(2):
                        dve.wait_ge(g_exp, 2 * n + d + 1)
                        e = gt[:, d, 0, :].rearrange("p (c t) -> p c t", t=CH)
                        link(nc.vector.tensor_copy(dec[:, d, :], e[:, :, CH - 1 if d == 0 else 0]))
                        nc.vector.tensor_tensor(gt[:, d, 0, 0:TQ], gt[:, d, 0, 0:TQ], qkT[:, 0, h, 0:TQ], ALU.mult)
                        nc.vector.tensor_tensor(gt[:, d, 1, 0:TQ], gt[:, d, 1, 0:TQ], qkT[:, 0, h, 0:TQ], ALU.mult)
                        nc.vector.tensor_tensor(gt[:, d, 2, :], gt[:, d, 2, :], qkT[:, 1, h, :], ALU.mult).then_inc(g_fac, 1)
                    dve.wait_ge(g_att, n + 1)
                    for d in range(2):
                        ins = nc.vector.tensor_tensor(attP[:, d, 0:NQ, :], ps[:, 6, d * 256:d * 256 + NQ * CH].rearrange("p (i t) -> p i t", t=CH),
                                                      amask[:, d:d + 1, :].to_broadcast([P, NQ, CH]), ALU.mult)
                    link(ins)
                    if h:
                        dve.wait_ge(g_o, GT0[l] + h * NQ)
                    for a in (0, CH):
                        ins = nc.vector.tensor_tensor(attS[a:a + CH, 0:NQ, a:a + CH],
                                                      attP[a:a + CH, 0, 0:NQ, :], attP[a:a + CH, 1, 0:NQ, :], ALU.add)
                    ins.then_inc(g_attm, 1)
                    for i in range(7):
                        for d in range(2):
                            dve.wait_ge(g_ds, 14 * n + 2 * i + d + 1)
                            b = ps[:, 2 * d + i % 2, 0:DV]
                            cc = scan_order(d)[i]
                            if i == 0:
                                ins = nc.vector.tensor_copy(S[:, d, 1, :], b)
                            else:
                                dve.wait_ge(g_st, 14 * n + 2 * (i - 1) + d + 1)
                                ins = nc.vector.scalar_tensor_tensor(out=S[:, d, i + 1, :], in0=S[:, d, i, :],
                                                                     scalar=dec[:, d, cc:cc + 1], in1=b, op0=ALU.mult, op1=ALU.add)
                            ins.then_inc(g_st, 1)
                    dve.wait_ge(g_silu, n + 1)
                    for i in range(gate_fill(l, h, 0)[1], gate_fill(l, h, 4)[1] + 1):
                        b = G[:, i, h // 2 * 512:h // 2 * 512 + 512].rearrange("p (a e) -> p a e", a=2)
                        nc.vector.tensor_tensor(b, b, gnw[:].rearrange("p (a e) -> p a e", a=1).to_broadcast([P, 2, DV]), ALU.mult)
                meet(dve, met_at(l, "gla"))

                dve.wait_ge(g_root, l + 1)
                link(nc.vector.reciprocal(ssq[:, 0:NQ, :], ssq[:, 0:NQ, :]))
                for h in range(GH):
                    for i in range(NQ):
                        o = O[:, i, h * DV:(h + 1) * DV]
                        ins = nc.vector.scalar_tensor_tensor(out=o, in0=o, scalar=ssq[:, i, h:h + 1],
                                                             in1=G[:, i, h * DV:(h + 1) * DV], op0=ALU.mult, op1=ALU.mult)
                    ins.then_inc(g_gated, 1)
                for k in range(1, 8, 2):
                    dve.wait_ge(g_t, 16 * l + 8 + k + 1)
                    nc.vector.tensor_copy(glaT[:, k, 0:TQ], ps[:, 4 + k % 4, 0:TQ]).then_inc(g_tc_dve, 1)
                meet(dve, met_at(l, "gate"))
                for j in range(2):
                    for name in ("bo", "bn"):
                        for i in range(4):
                            evacuate(chunk_index(l, name, j), i)
                for k in range(KT):
                    evacuate(chunk_index(l, "wo", k // 4), k % 4)
                    if k > 1:
                        norm_add(2 * l + 1, TQ, k - 1)
                norm_add(2 * l + 1, TQ, KT - 1)
                meet(dve, met_at(l, "merge"))
                nc.vector.memset(affT, 0.0)
                norm_inverse(2 * l + 1, TQ)
                norm_scale(2 * l + 1, TQ, lambda s, k: s1[:, l, 1, s, k:k + 1])

                def R(a, n, split=None):
                    v = rt[:, a:a + n]
                    return v if split is None else v.rearrange("p (i e) -> p i e", e=split)

                def over(v, e):
                    return v.rearrange("p (n a) -> p n a", a=1).to_broadcast([P, v.shape[1], e])

                N = NQ * NE
                M, aff, sel = R(0, N, NE), R(64, N, NE), R(128, N, NE)
                dve.wait_ge(s_rw, 32)
                dve.wait_ge(r_aT, l + 1)
                link(nc.vector.tensor_copy(aff, ps[:, 0, P:P + 32 * NQ].rearrange("p (i e) -> p i e", e=32)[:, :, 0:NE]))
                link(nc.vector.tensor_tensor(sel, aff, br[:].rearrange("p (a e) -> p a e", a=1).to_broadcast([P, NQ, NE]), ALU.add))
                s4, pairs = R(128, N, EPG), R(192, NQ * NG * 6, 6)
                nc.vector.tensor_tensor(pairs[:, :, 0:3], s4[:, :, 0:3], s4[:, :, 1:4], ALU.add)
                nc.vector.tensor_tensor(pairs[:, :, 3:5], s4[:, :, 0:2], s4[:, :, 2:4], ALU.add)
                link(nc.vector.tensor_tensor(pairs[:, :, 5:6], s4[:, :, 0:1], s4[:, :, 3:4], ALU.add))
                gsc = R(288, NQ * NG)
                link(nc.vector.tensor_reduce(gsc, pairs, AX, ALU.max))

                def first_max(dst, v, e, top, wt):
                    link(nc.vector.tensor_reduce(top, v, AX, ALU.max))
                    link(nc.vector.tensor_tensor(wt, v, over(top, e), ALU.is_equal))
                    link(nc.vector.tensor_tensor(wt, wt, ramp[:, 16 - e:16].rearrange("p (a e) -> p a e", a=1).to_broadcast([P, NQ, e]), ALU.mult))
                    link(nc.vector.tensor_reduce(top, wt, AX, ALU.max))
                    link(nc.vector.tensor_tensor(dst, wt, over(top, e), ALU.is_equal))

                ing = R(312, NQ * NG)
                first_max(R(312, NQ * NG, NG), R(288, NQ * NG, NG), NG, R(304, NQ), R(328, NQ * NG, NG))
                link(nc.vector.tensor_scalar(ing, ing, BIG, -BIG, ALU.mult, ALU.add))
                selm = R(352, N, NE)
                link(nc.vector.tensor_tensor(R(352, N, EPG), s4, over(ing, EPG), ALU.add))
                oh1, sel2, oh2, t = R(496, N, NE), R(560, N, NE), R(640, N, NE), R(704, N, NE)
                first_max(oh1, selm, NE, R(416, NQ), R(424, N, NE))
                link(nc.vector.scalar_tensor_tensor(out=sel2, in0=oh1, scalar=-2 * BIG, in1=selm, op0=ALU.mult, op1=ALU.add))
                first_max(oh2, sel2, NE, R(624, NQ), R(424, N, NE))
                nc.vector.tensor_tensor(M, oh1, oh2, ALU.add).then_inc(r_sel, 1)
                a1, a2, den = R(768, NQ), R(772, NQ), R(776, NQ)
                for oh, a in ((oh1, a1), (oh2, a2)):
                    link(nc.vector.tensor_tensor(t, oh, aff, ALU.mult))
                    link(nc.vector.tensor_reduce(a, t, AX, ALU.add))
                link(nc.vector.tensor_tensor(den, a1, a2, ALU.add))
                link(nc.vector.reciprocal(den, den))
                nc.vector.tensor_tensor(wsel[:, 0:NQ, 0], a1, den, ALU.mult)
                nc.vector.tensor_tensor(wsel[:, 0:NQ, 1], a2, den, ALU.mult)
                dve.wait_ge(r_rank, l + 1)
                cnt, nbf, inc, base, pos = R(780, NE), R(796, NE), R(812, NE), R(828, NE), R(848, N, NE)
                ci = cnt.bitcast(I32)
                link(nc.vector.tensor_scalar(ci, ps[:, 7, 64:64 + NE], float(BLK - 1), None, ALU.add))
                link(nc.vector.tensor_scalar(ci, ci, BLK.bit_length() - 1, None, ALU.arith_shift_right))
                link(nc.vector.tensor_scalar(nbf, ci, 1.0, None, ALU.max))
                link(nc.vector.tensor_tensor_scan(inc, ones[:, 0:NE], nbf, 0.0, ALU.mult, ALU.add))
                link(nc.vector.tensor_tensor(base, inc, nbf, ALU.subtract))
                nc.vector.tensor_copy(blocks[:, 0, :], inc)
                nc.vector.tensor_copy(blocks[:, 1, :], base)
                link(nc.vector.tensor_scalar(base, base, float(BLK), None, ALU.mult))
                link(nc.vector.tensor_tensor(pos, ps[:, 7, 0:N].rearrange("p (i e) -> p i e", e=NE),
                                             base.rearrange("p (a e) -> p a e", a=1).to_broadcast([P, NQ, NE]), ALU.add))
                for c_, oh in enumerate((oh1, oh2)):
                    link(nc.vector.tensor_tensor(t, oh, pos, ALU.mult))
                    link(nc.vector.tensor_reduce(R(912 + 4 * c_, NQ), t, AX, ALU.add))
                    ins = nc.vector.tensor_copy(slot[:, 0:NQ, c_], R(912 + 4 * c_, NQ))
                ins.then_inc(r_slot, 1)
                meet(dve, met_at(l, "route"))

                dve.wait_ge(m["xT_ps"], 1)
                nc.vector.tensor_copy(xbT_flat, ps[:, 0, :]).then_inc(m["xT_sb"], 1)
                with dve.Fori(0, NE) as e:
                    b1 = dve.value_load(blocks[0:1, 0, bass.ds(e, 1)], min_val=1, max_val=MAXB)
                    b0 = dve.value_load(blocks[0:1, 1, bass.ds(e, 1)], min_val=0, max_val=MAXB)
                    with dve.Fori(b0, b1) as b:
                        dve.wait_ge(m["silu"], b + 1)
                        dve.wait_ge(m["hT_ps"], 2 * b + 1)
                        for part in range(2):
                            dve.wait_ge(m["u_ps"], 2 * b + (part + 1))
                            cols = slice(part * 256, part * 256 + 256)
                            nc.vector.tensor_tensor(hblk[:, cols], silu_g[:, cols], ps[:, (2, 5)[part], 0:256],
                                                    ALU.mult).then_inc(m["h_sb"], 1)
                        dve.wait_ge(m["xT_ps"], b + 2)
                        nc.vector.tensor_copy(xbT_flat, ps[:, 0, :]).then_inc(m["xT_sb"], 1)
                        dve.wait_ge(m["y_ps"], b + 2)
                        dve.wait_ge(m["y_out"], 32 * b + 32)
                        nc.vector.tensor_copy(yblk, ps[:, 4, :]).then_inc(m["y_sb"], 1)
                meet(dve, met_at(l, "experts"))

                for i in range(NQ + 2):
                    if i < NQ:
                        dve.wait_ge(s_gather[i], 32 * l + 32)
                        link(nc.vector.tensor_scalar(z[:, i, :], yg[:, 2 * i, :], wsel[:, i, 0:1], None, ALU.mult))
                        nc.vector.scalar_tensor_tensor(out=z[:, i, :], in0=yg[:, 2 * i + 1, :], scalar=wsel[:, i, 1:2],
                                                       in1=z[:, i, :], op0=ALU.mult, op1=ALU.add).then_inc(c_z, 1)
                    if 0 < i <= NQ:
                        dve.wait_ge(c_t, QT0[l] + i)
                        for k in range(KT):
                            x_ = xT[:, k, (i - 1) * P:i * P]
                            ins = nc.vector.scalar_tensor_tensor(out=x_, in0=ps[:, 2 * (i - 1) + k // 4, (k % 4) * P:(k % 4 + 1) * P],
                                                                 scalar=mod[:, l, (i - 1) // 2, 40 + k:41 + k], in1=x_,
                                                           op0=ALU.mult, op1=ALU.add)
                        ins.then_inc(c_x, 1)
                    if i > 1:
                        dve.wait_ge(n_sq, SQ0[2 * l + 2] + i - 1)
                        v = hT[:, :, (i - 2) * P:(i - 1) * P]
                        link(nc.vector.tensor_tensor(v[:, 0:4], v[:, 0:4], v[:, 4:8], ALU.add))
                        link(nc.vector.tensor_tensor(v[:, 0:2], v[:, 0:2], v[:, 2:4], ALU.add))
                        ins = nc.vector.tensor_tensor(v[:, 0], v[:, 0], v[:, 1], ALU.add)
                ins.then_inc(n_acc, 1)
                meet(dve, met_at(l, "combine"))
            norm_inverse(2 * DEPTH, SEQ)
            norm_scale(2 * DEPTH, SEQ, lambda s, k: vcol[:, 128 + k:129 + k])

        @block.gpsimd
        def _(pool):
            nc.gpsimd.memset(zero, 0.0).then_inc(chain["pool"], 1)
            pool.wait_ge(chain["pool"], 1)
            pool.dma_start(rp.rearrange("l h r w -> (l h r) w").rearrange("(a b) w -> a (b w)", b=2), zero[0:120, 0:2 * RPAD]).then_inc(s_rpz, 16)
            pool.wait_ge(s_rpz, 16)
            for l in range(DEPTH):
                pool.dma_start(rp[l, :, :, GRID_W - WIN_C:GRID_W + WIN_C - 1].rearrange("h r w -> (h r) w"),
                               rpb[l].rearrange("h r w -> (h r) w")).then_inc(s_rp, 16)
            pool.wait_ge(met, MODS_MET)
            pool.wait_ge(s_rp, 32)

            def copy_bias(l):
                src = rp[l, :, WIN_R - GROWS:WIN_R + GROWS - 1, :].rearrange("h r w -> h (r w)").rearrange("(a h) n -> a h n", a=1)
                pool.dma_start(rx[l].rearrange("c h r w -> c h (r w)"), src.to_broadcast([GRID_W, NH, RW * RPAD])).then_inc(s_rx, 16)

            copy_bias(0)
            def zero_fill(buf, rows, done):
                with pool.Fori(0, rows // (2 * P)) as r:
                    for a in range(2):
                        pool.dma_start(buf[bass.ds(r * (2 * P) + a * P, P), :], zero).then_inc(s_zfill, 16)
                    pool.wait_ge(s_zfill, 32 * r + (16 * done + 32))
                if rows % (2 * P):
                    pool.dma_start(buf[rows - P:rows, :], zero).then_inc(s_zfill, 16)
                    pool.wait_ge(s_zfill, 16 * (done + rows // P))

            zero_fill(xbuf, XROWS, 0)
            zero_fill(ybuf, MAXB * BLK, XROWS // P)
            pool.wait_ge(s_zfill, ZFILLS)
            pool.wait_ge(s_rx, 16)
            copy_bias(1)
            for l in range(DEPTH):
                m, NQ = moe[l], q_tiles(l)
                pool.wait_ge(r_slot, l + 1)
                pool.wait_ge(r_natc, QT0[l] + NQ)
                for i in range(NQ):
                    for c_ in range(2):
                        pool.indirect_dma_start(xbuf, bass.IndirectOffsetOnAxis(slot[:, i, c_:c_ + 1], 0), h2n[:, i, :], None,
                                                ).then_inc(m["scattered"], 16)
                pool.wait_ge(met, met_at(l, "route"))
                pool.wait_ge(m["scattered"], 32 * NQ)

                def load_x(b):
                    for a in range(2):
                        pool.dma_start(xblk[64 * a:64 * a + 64, :], xbuf[bass.ds(b * BLK, BLK), 512 * a:512 * a + 512]).then_inc(m["x_in"], 16)

                load_x(0)
                pool.wait_ge(m["xT_ps"], 1)
                load_x(1)
                with pool.Fori(0, NE) as e:
                    b1 = pool.value_load(blocks[0:1, 0, bass.ds(e, 1)], min_val=1, max_val=MAXB)
                    b0 = pool.value_load(blocks[0:1, 1, bass.ds(e, 1)], min_val=0, max_val=MAXB)
                    with pool.Fori(b0, b1) as b:
                        pool.wait_ge(m["xT_ps"], b + 2)
                        load_x(b + 2)
                total = pool.value_load(blocks[0:1, 0, NE - 1:NE], min_val=1, max_val=MAXB)
                pool.wait_ge(m["y_out"], 32 * total + 32)
                pool.wait_ge(m["x_in"], 32 * total + 64)
                nc.gpsimd.tensor_tensor(waited[:, l:l + 1], ones[0:1, 0:1], ones[0:1, 0:1], ALU.mult)
                pool.wait_ge(met, met_at(l, "experts"))
                for i in range(NQ):
                    for c_ in range(2):
                        pool.indirect_dma_start(yg[:, 2 * i + c_, :], None, ybuf, bass.IndirectOffsetOnAxis(slot[:, i, c_:c_ + 1], 0),
                                                ).then_inc(s_gather[i], 16)


def constants():
    k = np.zeros((P, 1361), np.float32)
    p, t = np.arange(P)[:, None], np.arange(P)[None, :]
    same = p // CH == t // CH
    k[:, 0:128] = p == t
    k[:, 128:256] = 1.0
    k[:, 256:384] = same & (p <= t)
    k[:, 384:512] = same & (p > t)
    k[:, 512:640] = same & (p >= t)
    k[:, 640:768] = same & (p < t)
    t64 = np.arange(CH)[None, :]
    k[:, 768:832] = p % CH <= t64
    k[:, 832:896] = p % CH >= t64
    k[:, 896:1024] = p < t
    half = DK // 2
    inv = np.float32(10000.0) ** (-np.arange(0, half, 2, dtype=np.float32) / np.float32(half))
    for i in range(2):
        tok = i * P + np.arange(P)
        for a, pos in enumerate((tok // GRID_W, tok % GRID_W)):
            ang = pos.astype(np.float32)[:, None] * inv[None, :]
            for f, fn in enumerate((np.cos, np.sin)):
                o = 1024 + ((f * 2 + i) * 2 + a) * 32
                k[:, o:o + 32] = fn(ang)
    col = np.arange(P)[:, None] % GRID_W
    c0 = np.clip(col - WIN_C // 2, 0, GRID_W - WIN_C)
    kc = np.arange(GRID_W)[None, :]
    k[:, 1280:1344] = np.where((kc >= c0) & (kc < c0 + WIN_C), 0.0, -BIG)
    k[:, 1344:1360] = np.arange(16, 0, -1)
    k[:, 1360] = EPS
    return k


_INS = ['x', 'c', 'ctx', 'c_ctx', 'w_ada', 'b_ada', 'norm1_w', 'norm2_w', 'w_in', 'w_gk_up', 'b_gk', 'gla_norm_w', 'rpb',
        'w_bo_gla', 'w_bo_na', 'w_out', 'w_router', 'b_router', 'w1', 'w3', 'w2', 'final_norm_w']


def kernel(**inputs):
    import numpy as _np
    import concourse.bacc as _bacc
    from concourse import mybir as _mybir
    from concourse.bass_utils import run_bass_kernel_spmd as _run

    nc = _bacc.Bacc("TRN2", target_bir_lowering=False, num_devices=1)
    arrays, args = {}, []
    for name in _INS + ["consts"]:
        a = constants() if name == "consts" else _np.ascontiguousarray(inputs[name])
        arrays[f"in_{name}"] = a
        args.append(nc.dram_tensor(f"in_{name}", a.shape, _mybir.dt.from_np(a.dtype), kind="ExternalInput").ap())
    args.append(nc.dram_tensor("out_0", (1, SEQ, D), _mybir.dt.float32, kind="ExternalOutput").ap())
    build(nc, *args)
    return _run(nc, [arrays], core_ids=[0]).results[0]["out_0"]
```
